# Optimizing a Trainium2 kernel written in Bass

```python
import math
import jax, jax.numpy as jnp
from jax import lax
import numpy as np

D_MODEL = 1024
BATCH = 1
SEQ = 1024
DEPTH = 1

GRID_W = 64
CTX_LEN = 256
MIX_WIDTH = D_MODEL
POOL_WIDTH = MIX_WIDTH // 2
S5_WIDTH = MIX_WIDTH - POOL_WIDTH
POOL_WINDOWS = (2, 4, 8, 16)
N_POOL_GROUPS = len(POOL_WINDOWS)
POOL_CH = POOL_WIDTH // N_POOL_GROUPS
S5_GROUP = 16
S5_GROUPS = S5_WIDTH // S5_GROUP
S5_STATE = 64
D_FF = 2816
N_MOD = 9
EPS = 1e-6
DT_MIN = 1e-3
DT_MAX = 1e-1

kernel_name = "hybrid_pool_s5_macaron_dit_layer"

def rmsnorm(x, g):
    xf = x.astype(jnp.float32)
    y = xf * lax.rsqrt(jnp.mean(xf * xf, axis=-1, keepdims=True) + EPS)
    return (y * g.astype(jnp.float32)).astype(x.dtype)

def modulate(h, shift, scale):
    return h * (1 + scale) + shift

def swiglu(h, w1, w3, w2):
    return (jax.nn.silu(h @ w1) * (h @ w3)) @ w2

def ffn_sublayer(x, g, shift, scale, gate, w1, w3, w2):
    h = modulate(rmsnorm(x, g), shift, scale)
    return x + 0.5 * gate * swiglu(h, w1, w3, w2)

def window_mean(v, w, axis):
    n = v.shape[axis]
    lo = w // 2
    hi = w - 1 - lo
    t = np.arange(n)
    i_hi = np.clip(t + hi + 1, 0, n)
    i_lo = np.clip(t - lo, 0, n)
    vf = jnp.moveaxis(v.astype(jnp.float32), axis, 0)
    s = jnp.concatenate([jnp.zeros_like(vf[:1]), jnp.cumsum(vf, axis=0)], axis=0)
    cnt = (i_hi - i_lo).astype(np.float32).reshape((n,) + (1,) * (vf.ndim - 1))
    m = (s[i_hi] - s[i_lo]) / cnt
    return jnp.moveaxis(m, 0, axis).astype(v.dtype)

def pool_mixer(u, w_pool, scale, rows):
    bn, length, _ = u.shape
    ug = u.reshape(bn, length, N_POOL_GROUPS, POOL_CH)
    outs = []
    for k, w in enumerate(POOL_WINDOWS):
        v = ug[:, :, k]
        if rows is None:
            p = window_mean(v, w, 1)
        else:
            v2 = v.reshape(bn, rows, GRID_W, POOL_CH)
            p = window_mean(window_mean(v2, w, 1), w, 2).reshape(bn, length, POOL_CH)
        outs.append(p - v)
    d = jnp.stack(outs, axis=2)
    y = jnp.einsum('blkc,kcd->blkd', d, w_pool).reshape(bn, length, POOL_WIDTH)
    return y * scale

def s5_discretise(a_re, a_im, log_dt, b):
    lam = lax.complex(a_re.astype(jnp.float32), a_im.astype(jnp.float32))
    dt = jnp.exp(log_dt.astype(jnp.float32))[:, None]
    abar = jnp.exp(lam * dt)
    bbar = ((abar - 1) / lam)[..., None] * b
    return abar, bbar

def _ssm_combine(e1, e2):
    a1, b1 = e1
    a2, b2 = e2
    return a2 * a1, a2 * b1 + b2

def s5_scan(abar, bbar, u, h0, reverse):
    bu = jnp.einsum('gpc,blgc->blgp', bbar, u.astype(jnp.float32).astype(jnp.complex64))
    if h0 is not None:
        edge = -1 if reverse else 0
        bu = bu.at[:, edge].add(abar * h0)
    a = jnp.broadcast_to(abar, bu.shape)
    _, h = lax.associative_scan(_ssm_combine, (a, bu), axis=1, reverse=reverse)
    return h

def s5_readout(h_f, h_b, u, c_f, c_b, d_skip, w_glu):
    bn, length = u.shape[:2]
    y = (jnp.einsum('gcp,blgp->blgc', c_f, h_f).real
         + jnp.einsum('gcp,blgp->blgc', c_b, h_b).real)
    y = y.reshape(bn, length, S5_WIDTH) + d_skip.astype(jnp.float32) * u.reshape(bn, length, S5_WIDTH).astype(jnp.float32)
    y = jax.nn.gelu(y)
    y = y * jax.nn.sigmoid(y @ w_glu.astype(jnp.float32))
    return y.astype(u.dtype)

def setup_inputs(seed: int = 0) -> dict:
    key = jax.random.key(seed)
    ks = jax.random.split(key, 24)
    f32 = jnp.float32
    D, F, G, P = D_MODEL, D_FF, S5_GROUPS, S5_STATE
    nrm = lambda k, shape, s: jax.random.normal(k, shape, f32) * s
    n_idx = jnp.arange(P, dtype=f32)
    log_dt = jax.random.uniform(ks[14], (DEPTH, 2, G), f32, math.log(DT_MIN), math.log(DT_MAX))
    return {
        "x": nrm(ks[0], (BATCH, SEQ, D), 1.0),
        "c": nrm(ks[1], (BATCH, D), 1.0),
        "ctx": nrm(ks[2], (BATCH, CTX_LEN, D), 1.0),
        "c_ctx": nrm(ks[3], (D,), 1.0),
        "norm_g": 1.0 + nrm(ks[4], (DEPTH, 3, D), 0.02),
        "w_ada": nrm(ks[5], (DEPTH, D, N_MOD * D), 0.5 * D ** -0.5),
        "b_ada": nrm(ks[6], (DEPTH, N_MOD * D), 0.01),
        "ffn_w1": nrm(ks[7], (DEPTH, 2, D, F), D ** -0.5),
        "ffn_w3": nrm(ks[8], (DEPTH, 2, D, F), D ** -0.5),
        "ffn_w2": nrm(ks[9], (DEPTH, 2, F, D), F ** -0.5),
        "w_in": nrm(ks[10], (DEPTH, D, MIX_WIDTH), D ** -0.5),
        "pool_w": nrm(ks[11], (DEPTH, N_POOL_GROUPS, POOL_CH, POOL_CH), POOL_CH ** -0.5),
        "pool_scale": 1.0 + nrm(ks[12], (DEPTH, POOL_WIDTH), 0.02),
        "s5_a_re": -0.5 + nrm(ks[13], (DEPTH, 2, G, P), 0.01),
        "s5_a_im": math.pi * n_idx + nrm(ks[15], (DEPTH, 2, G, P), 0.01),
        "s5_log_dt": log_dt,
        "s5_b_re": nrm(ks[16], (DEPTH, G, P, S5_GROUP), (2.0 * S5_GROUP) ** -0.5),
        "s5_b_im": nrm(ks[17], (DEPTH, G, P, S5_GROUP), (2.0 * S5_GROUP) ** -0.5),
        "s5_c_re": nrm(ks[18], (DEPTH, 2, G, S5_GROUP, P), (2.0 * P) ** -0.5),
        "s5_c_im": nrm(ks[19], (DEPTH, 2, G, S5_GROUP, P), (2.0 * P) ** -0.5),
        "s5_d": nrm(ks[20], (DEPTH, S5_WIDTH), 1.0),
        "s5_w_glu": nrm(ks[21], (DEPTH, S5_WIDTH, S5_WIDTH), S5_WIDTH ** -0.5),
        "w_out": nrm(ks[22], (DEPTH, MIX_WIDTH, D), MIX_WIDTH ** -0.5),
        "final_g": 1.0 + nrm(ks[23], (D,), 0.02),
    }

def reference(x, c, ctx, c_ctx, norm_g, w_ada, b_ada, ffn_w1, ffn_w3, ffn_w2, w_in,
              pool_w, pool_scale, s5_a_re, s5_a_im, s5_log_dt, s5_b_re, s5_b_im,
              s5_c_re, s5_c_im, s5_d, s5_w_glu, w_out, final_g):
    f32 = jnp.float32
    bn, length, _ = x.shape
    rows = length // GRID_W
    lc = ctx.shape[1]
    xl, xc = x, ctx
    for l in range(DEPTH):
        last = l == DEPTH - 1
        ml = jnp.split((jax.nn.silu(c) @ w_ada[l] + b_ada[l])[:, None, :], N_MOD, axis=-1)
        mc = jnp.split((jax.nn.silu(c_ctx) @ w_ada[l] + b_ada[l])[None, None, :], N_MOD, axis=-1)

        xl = ffn_sublayer(xl, norm_g[l, 0], ml[0], ml[1], ml[2], ffn_w1[l, 0], ffn_w3[l, 0], ffn_w2[l, 0])
        xc = ffn_sublayer(xc, norm_g[l, 0], mc[0], mc[1], mc[2], ffn_w1[l, 0], ffn_w3[l, 0], ffn_w2[l, 0])

        hl = modulate(rmsnorm(xl, norm_g[l, 1]), ml[3], ml[4]) @ w_in[l]
        hc = modulate(rmsnorm(xc, norm_g[l, 1]), mc[3], mc[4]) @ w_in[l]
        pool_in_l, s5_in_l = hl[..., :POOL_WIDTH], hl[..., POOL_WIDTH:]
        pool_in_c, s5_in_c = hc[..., :POOL_WIDTH], hc[..., POOL_WIDTH:]

        b_cplx = lax.complex(s5_b_re[l].astype(f32), s5_b_im[l].astype(f32))
        abar_f, bbar_f = s5_discretise(s5_a_re[l, 0], s5_a_im[l, 0], s5_log_dt[l, 0], b_cplx)
        abar_b, bbar_b = s5_discretise(s5_a_re[l, 1], s5_a_im[l, 1], s5_log_dt[l, 1], b_cplx)
        c_f = lax.complex(s5_c_re[l, 0].astype(f32), s5_c_im[l, 0].astype(f32))
        c_b = lax.complex(s5_c_re[l, 1].astype(f32), s5_c_im[l, 1].astype(f32))

        uc = s5_in_c.reshape(bn, lc, S5_GROUPS, S5_GROUP)
        ul = s5_in_l.reshape(bn, length, S5_GROUPS, S5_GROUP)
        hc_f = s5_scan(abar_f, bbar_f, uc, None, False)
        hc_b = s5_scan(abar_b, bbar_b, uc, None, True)
        hl_f = s5_scan(abar_f, bbar_f, ul, hc_f[:, -1], False)
        hl_b = s5_scan(abar_b, bbar_b, ul, hc_b[:, 0], True)

        mix_l = jnp.concatenate([
            pool_mixer(pool_in_l, pool_w[l], pool_scale[l], rows),
            s5_readout(hl_f, hl_b, ul, c_f, c_b, s5_d[l], s5_w_glu[l]),
        ], axis=-1) @ w_out[l]
        xl = xl + ml[5] * mix_l
        if not last:
            mix_c = jnp.concatenate([
                pool_mixer(pool_in_c, pool_w[l], pool_scale[l], None),
                s5_readout(hc_f, hc_b, uc, c_f, c_b, s5_d[l], s5_w_glu[l]),
            ], axis=-1) @ w_out[l]
            xc = xc + mc[5] * mix_c

        xl = ffn_sublayer(xl, norm_g[l, 2], ml[6], ml[7], ml[8], ffn_w1[l, 1], ffn_w3[l, 1], ffn_w2[l, 1])
        if not last:
            xc = ffn_sublayer(xc, norm_g[l, 2], mc[6], mc[7], mc[8], ffn_w1[l, 1], ffn_w3[l, 1], ffn_w2[l, 1])
    return rmsnorm(xl, final_g)


_drawn_inputs = setup_inputs


def setup_inputs(seed=0):
    import zlib

    import numpy as np

    out = dict(_drawn_inputs(seed))
    spreads = {}
    factors = {'ctx': 64.0,
     'c_ctx': 64.0,
     'norm_g': 8.0,
     'b_ada': 5.814,
     'pool_scale': 70.92,
     's5_a_re': 64.0,
     's5_a_im': 51.872,
     's5_log_dt': 63.64,
     's5_b_re': 64.0,
     's5_b_im': 64.0,
     's5_c_re': 64.0,
     's5_c_im': 64.0,
     'final_g': 25.312,
     's5_d': 3.399,
     's5_w_glu': 4.553}
    for name, (base, spread) in spreads.items():
        noise = np.random.default_rng([zlib.crc32(name.encode()), seed]).standard_normal(out[name].shape)
        drawn = base * np.exp(spread * noise) if base else spread * noise
        out[name] = __import__('jax').numpy.asarray(drawn.astype(out[name].dtype))
    for name, factor in factors.items():
        out[name] = (out[name] * factor).astype(out[name].dtype)
    return out
```

```python
from contextlib import ExitStack

import numpy as np
import concourse.bass as bass
from concourse import mybir

P = 128
F32 = mybir.dt.float32
F32R = mybir.dt.float32r
I32 = mybir.dt.int32
ALU = mybir.AluOpType
ACT = mybir.ActivationFunctionType
KB = 1024

D = 1024
DK = D // P
SEQ, CTX = 1024, 256
FF = 2816
NF = FF // P
NR = 2
FR = NF // NR
TB = 512
HALF = 512
GW = 64
GR = SEQ // GW
WINDOWS = (2, 4, 8, 16)
G, ST, GC = 32, 64, 16
T = 8
KL, KC = SEQ // T, CTX // T
EPS = 1e-6
S5_LOADS = 13

MAGIC = 12582912.0
LOG2E = 1.4426950408889634
LN2 = (0.693359375, -2.12194440e-4)
INV2PI = 0.15915494309189535
TWO_PI = (6.28125, 0.0019350051879882812, 3.0199159819e-7)
PI_IN = 3.1415925


def hybrid_layer(nc, x, c, ctx_tok, c_ctx, norm_g, w_ada, b_ada, ffn_w1, ffn_w3, ffn_w2, w_in,
                 pool_w, pool_scale, s5_a_re, s5_a_im, s5_log_dt, s5_b_re, s5_b_im,
                 s5_c_re, s5_c_im, s5_d, s5_w_glu, w_out, final_g, out):
    base = (nc._sbuf_addr_for_side("left") + 31) // 32 * 32

    def at(name, shape, kb, dt=F32):
        return nc.alloc_sbuf_tensor_at(name, shape, dt, offset=base + int(kb * KB))

    xl = at("xl", [P, T, D], 0)
    gate = at("gate", [P, 2, D], 32)
    ident = at("ident", [P, P], 40)
    ones = at("ones", [P, P], 40.5)
    vcol = at("vcol", [P, 44], 41)
    scol = at("scol", [P, 16], 41.1875)
    gcol = at("gcol", [P, 5, DK], 41.25)
    bcol = at("bcol", [P, 5, DK], 41.4375)
    ssq = at("ssq", [P, 4], 41.625)
    rs = at("rs", [P, 6, 4], 41.6875)
    xc = at("xc", [P, 2, D], 42)
    h_hi = at("h_hi", [P, DK, TB], 50, F32R)
    h_lo = at("h_lo", [P, DK, TB], 66, F32R)
    a_hi = at("a_hi", [P, FR, TB], 82, F32R)
    a_lo = at("a_lo", [P, FR, TB], 104, F32R)
    up_raw = at("up_raw", [P, 4, DK, P], 126)
    up_hi = at("up_hi", [P, 2, DK, P], 142, F32R)
    up_lo = at("up_lo", [P, 2, DK, P], 150, F32R)
    dn_raw = at("dn_raw", [P, 4, HALF], 158)
    dn_hi = at("dn_hi", [P, 2, HALF], 166, F32R)
    dn_lo = at("dn_lo", [P, 2, HALF], 170, F32R)
    xn = at("xn", [P, 4, D], 174)
    h32 = at("h32", [P, 2, TB], 190)
    sg = at("sg", [P, 2, TB], 194)
    a32 = at("a32", [P, 2, TB], 198)
    evt = at("evt", [P, 2, HALF], 202)
    h32f = at("fgrow", [P, D], 50)[:, :]
    ada = at("ada", [P, 2, DK, 512], 50)
    acc = at("acc", [P, 2, 2, 512], 82)
    brow = at("brow", [1, 2, 512], 90)
    growt = at("growt", [P, 2, 512], 94)
    inv_r = at("inv_r", [P, 4, GR], 206)
    inv_c = at("inv_c", [P, 4, GW], 206.25)
    bn = at("bn", [P, 2, G, GC], 102)
    cn = at("cn", [P, 2, G, GC], 106)
    bb = at("bb", [P, 2, G, GC], 110)
    craw = at("craw", [P, 2, 4, P], 114)
    bf = at("bf", [P, 2, G, GC], 102)
    bk = at("bk", [P, 2, G, GC], 114)
    t1 = at("t1", [P, G, GC], 118)
    t2 = at("t2", [P, G, GC], 120)
    vn = at("vn", [P, 2, 16, T, GC], 122)
    vts = at("vts", [P, 16, 2, P], 138)
    wn = at("wn", [P, 2, 16, T, GC], 154)
    kp = at("kp", [GC, 16, 15, GC], 170)
    dm = at("dm", [GC, G, GC], 186)
    sm = at("sm", [G, 16, P], 188)
    pw = at("pw", [P, 9, 2, G], 196)
    pwv = at("pwv", [P, T, 2, G], 199)
    pww = at("pww", [P, T, 2, G], 201)
    q4t = at("q4t", [P, 4, G], 203)
    smi = at("smi", [G, P], 203.5, I32)
    vecrow = at("vecrow", [44, P], 204)
    dt2 = at("dt2", [G, 8, 2], 204.5)
    dt2i = at("dt2i", [G, 2], 204.75, I32)
    pt = at("pt", [P, 2, 4, G], 205)
    vp = at("vp", [P, 4, SEQ], 82)
    hs = at("hs", [P, 4, CTX + SEQ], 98)
    U = at("U", [P, G, KC + KL], 42)
    vt = at("vt", [P, G, 2, P], 142)
    S = at("S", [P, KL, 2, G], 174)
    Sc = at("Sc", [P, KC, 2, G], 130)
    scn = at("scn", [P, 3, 2 * G], 138)
    abar = at("abar", [P, 2, 2, G], 207.25)
    wy = at("wy", [P, 2, G, P], 142)
    M = at("M", [P, G, P], 62)
    Hk = at("Hk", [P, 2, G, KL], 98)
    bxa = at("bxa", [P, 23 * GW], 98)
    bxb = at("bxb", [P, 23 * GW], 104)
    y = at("y", [P, T, G * GC], 174)
    yg = at("yg", [P, 4, SEQ], 98)
    pws = at("pws", [P, 4, P], 140)
    wglu = at("wglu", [P, 4, 512], 142)
    gs = at("gs", [P, 2, TB], 126)
    m32 = at("m32", [P, 2, TB], 130)

    v_dram = nc.dram_tensor("v_dram", [P, G, 2, P], F32, kind="Internal").ap()
    w_dram = nc.dram_tensor("w_dram", [P, 2, G, P], F32, kind="Internal").ap()
    k_dram = nc.dram_tensor("k_dram", [GC, G, 15 * GC], F32, kind="Internal").ap()
    u_dram = nc.dram_tensor("u_dram", [4, P, CTX + SEQ], F32, kind="Internal").ap()
    g_dram = nc.dram_tensor("g_dram", [2, P, D], F32, kind="Internal").ap()

    xl_d = x.rearrange("o (k t) c -> k (o t) c", t=T)
    xc_d = ctx_tok.rearrange("o (q i) c -> q (o i) c", i=2)
    out_d = out.rearrange("o (k t) c -> k (o t) c", t=T)
    ada_d = w_ada[0].rearrange("(k p) n -> p k n", p=P)
    w1_d = ffn_w1[0].rearrange("l (k p) f -> l p k f", p=P)
    w3_d = ffn_w3[0].rearrange("l (k p) f -> l p k f", p=P)
    win_d = w_in[0].rearrange("(k p) f -> p k f", p=P)

    up_src, dn_src = [], []
    BLOCKS = [dict(ffn=0, ctx=True, t0=0, gate=0), dict(ffn=0, ctx=False, t0=0, gate=1),
              dict(ffn=0, ctx=False, t0=4, gate=1), dict(ffn=1, ctx=False, t0=0, gate=0),
              dict(ffn=1, ctx=False, t0=4, gate=0)]

    def add_ffn(b):
        b["up0"], b["dn0"] = len(up_src), len(dn_src)
        l = b["ffn"]
        for r in range(NR):
            for f in range(FR):
                fs = slice((r * FR + f) * P, (r * FR + f + 1) * P)
                up_src.append(w1_d[l][:, :, fs])
                up_src.append(w3_d[l][:, :, fs])
            for h in range(2):
                for k in range(FR):
                    row = (r * FR + k) * P
                    dn_src.append(ffn_w2[0, l, row:row + P, h * HALF:(h + 1) * HALF])

    for b in BLOCKS[:3]:
        add_ffn(b)
    PROJ = [dict(ctx=True, t0=0, tiles=range(4, 8)), dict(ctx=False, t0=0, tiles=range(8)),
            dict(ctx=False, t0=4, tiles=range(8))]
    for pr in PROJ:
        pr["up0"] = len(up_src)
        for m in pr["tiles"]:
            up_src.append(win_d[:, :, m * P:(m + 1) * P])
    MIX = [dict(t0=0), dict(t0=4)]
    for mx in MIX:
        mx["dn0"] = len(dn_src)
        for h in range(2):
            for k in range(DK):
                dn_src.append(w_out[0, k * P:(k + 1) * P, h * HALF:(h + 1) * HALF])
    for b in BLOCKS[3:]:
        add_ffn(b)
    UP_MIX = PROJ[0]["up0"]
    UP_F2 = BLOCKS[3]["up0"]
    DN_MIX = MIX[0]["dn0"]

    for n, b in enumerate(BLOCKS):
        b["F0"] = n * NF
    ev = 0
    for b in BLOCKS[:3]:
        b["ev0"] = ev
        ev += 2 * NR * (2 if b["ctx"] else 4)
    for mx in MIX:
        mx["ev0"] = ev
        ev += 2 * 4
    for b in BLOCKS[3:]:
        b["ev0"] = ev
        ev += 2 * NR * 4
    EV_END = ev

    PREPS = [dict(ctx=True, t0=0, col=0, ev=0), dict(ctx=False, t0=0, col=2, ev=0),
             dict(ctx=False, t0=4, col=2, ev=0),
             dict(ctx=True, t0=0, col=1, ev=BLOCKS[1]["ev0"]),
             dict(ctx=False, t0=0, col=3, ev=BLOCKS[2]["ev0"]),
             dict(ctx=False, t0=4, col=3, ev=MIX[0]["ev0"]),
             dict(ctx=False, t0=0, col=4, ev=MIX[1]["ev0"]),
             dict(ctx=False, t0=4, col=4, ev=BLOCKS[3]["ev0"])]
    tiles0 = 0
    for n, p in enumerate(PREPS):
        p["n"] = n
        p["nt"] = 2 if p["ctx"] else 4
        p["q0"] = tiles0
        tiles0 += p["nt"]
    Q_FINAL = tiles0

    def xt(st, t):
        return xc[:, t, :] if st["ctx"] else xl[:, st["t0"] + t, :]

    with ExitStack() as ctx:
        def sem(name):
            return ctx.enter_context(nc.semaphore(name))

        ps = ctx.enter_context(nc.psum_tensor("ps", [P, 8, 512], F32))

        vec_ld, x_ld, s5_ld, fg_ld, gate_ld = (sem(n) for n in ("vec_ld", "x_ld", "s5_ld", "fg_ld", "gate_ld"))
        ada_ld = [sem(f"ada_ld{i}") for i in range(2)]
        up_ld = [sem(f"up_ld{i}") for i in range(4)]
        dn_ld = [sem(f"dn_ld{i}") for i in range(4)]
        const_ok, vec_t, vec_ok, sil_ok = (sem(n) for n in ("const_ok", "vec_t", "vec_ok", "sil_ok"))
        dve_step, pool_step = sem("dve_step"), sem("pool_step")
        ang_ok, sin_ok, q4_ok, q4_t, q4_ev, ct_t, ct_ev = (
            sem(n) for n in ("ang_ok", "sin_ok", "q4_ok", "q4_t", "q4_ev", "ct_t", "ct_ev"))
        acc_ok, mod_t, mod_ev, grow_ok = (sem(n) for n in ("acc_ok", "mod_t", "mod_ev", "grow_ok"))
        grow_st = [sem(f"grow_st{i}") for i in range(2)]
        v_ok, w_ok, vt_t, vt_ev, kt_t, kt_ev, kd_ok = (
            sem(n) for n in ("v_ok", "w_ok", "vt_t", "vt_ev", "kt_t", "kt_ev", "kd_ok"))
        v_st, w_st, k_st, setup_ok = sem("v_st"), sem("w_st"), sem("k_st"), sem("setup_ok")
        sq_ok, rstd_ok, xn_ok, ht_ok, hhi_ok, h32_ok, hlo_ok = (
            sem(n) for n in ("sq_ok", "rstd_ok", "xn_ok", "ht_ok", "hhi_ok", "h32_ok", "hlo_ok"))
        up_hi_ok, up_lo_ok, up_used = sem("up_hi_ok"), sem("up_lo_ok"), sem("up_used")
        dn_hi_ok, dn_lo_ok, dn_used = sem("dn_hi_ok"), sem("dn_lo_ok"), sem("dn_used")
        silu_ok, prod_ok, ahi_ok, alo_ok = sem("silu_ok"), sem("prod_ok"), sem("ahi_ok"), sem("alo_ok")
        gated, added = sem("gated"), sem("added")
        pj_ev = sem("pj_ev")
        u_st, u_ld, vt_ld, m_ld, w_ld, glu_ld, pws_ld = (
            sem(n) for n in ("u_st", "u_ld", "vt_ld", "m_ld", "w_ld", "glu_ld", "pws_ld"))
        sc_t, sc_ev, sl_t, sl_eva, sl_evd = (sem(n) for n in ("sc_t", "sc_ev", "sl_t", "sl_eva", "sl_evd"))
        scan_step, hk_a, hk_d = sem("scan_step"), sem("hk_a"), sem("hk_d")
        y_t, y_ev, yt_t, yg_ok = (sem(n) for n in ("y_t", "y_ev", "yt_t", "yg_ok"))
        pool_ok, pm_t, z_t, gs_ok, m32_ok, mhi_ok, mlo_ok = (
            sem(n) for n in ("pool_ok", "pm_t", "z_t", "gs_ok", "m32_ok", "mhi_ok", "mlo_ok"))
        fin_ok, out_st = sem("fin_ok"), sem("out_st")

        block = ctx.enter_context(nc.Block())

        @block.sync
        def _(sp):
            ld = sp.dma_start
            ld(vecrow[0:8, :], c.rearrange("o (k p) -> (o k) p", p=P)).then_inc(vec_ld, 16)
            ld(vecrow[8:16, :], c_ctx.rearrange("(k p) -> k p", p=P)).then_inc(vec_ld, 16)
            ld(vecrow[16:40, :], norm_g[0].rearrange("l (k p) -> (l k) p", p=P)).then_inc(vec_ld, 16)
            ld(vecrow[40:44, :], pool_scale[0].rearrange("(k p) -> k p", p=P)).then_inc(vec_ld, 16)
            ld(sm[:, 0, :].rearrange("g (d p) -> g d p", d=2), s5_a_re[0].rearrange("d g p -> g d p")).then_inc(s5_ld, 16)
            ld(sm[:, 1, :].rearrange("g (d p) -> g d p", d=2), s5_a_im[0].rearrange("d g p -> g d p")).then_inc(s5_ld, 16)
            for d in range(2):
                ld(dt2[:, 0, d:d + 1], s5_log_dt[0, d].rearrange("(g o) -> g o", o=1)).then_inc(s5_ld, 16)
                for i, src in enumerate((s5_b_re, s5_b_im)):
                    ld(bn[d * ST:(d + 1) * ST, i, :, :], src[0].rearrange("g p c -> p g c")).then_inc(s5_ld, 16)
                for i, src in enumerate((s5_c_re, s5_c_im)):
                    ld(craw[:, i, :, d * ST:(d + 1) * ST],
                       src[0, d].rearrange("(i g) c p -> (g c) i p", g=8)).then_inc(s5_ld, 16)
            ld(dm[:, :, :].rearrange("p g c -> p (g c)"), s5_d[0:1, :].broadcast_to([GC, G * GC])).then_inc(s5_ld, 16)
            for q in range(18):
                if q >= 2:
                    sp.wait_ge(mod_t, q - 1)
                ld(ada[:, q % 2, :, :], ada_d[:, :, q * 512:(q + 1) * 512]).then_inc(ada_ld[q % 2], 16)
                ld(brow[0:1, q % 2, :], b_ada[0:1, q * 512:(q + 1) * 512]).then_inc(ada_ld[q % 2], 16)
                if q == 0:
                    ld(xc[:, :, :], xc_d).then_inc(x_ld, 16)
                    ld(xl[:, :, :], xl_d).then_inc(x_ld, 16)
            for n in range(4):
                sp.wait_ge(grow_ok, n + 1)
                ld(g_dram[n // 2, :, (n % 2) * 512:(n % 2 + 1) * 512], growt[:, n % 2, :]).then_inc(grow_st[n % 2], 16)
            for i in range(2):
                sp.wait_ge(grow_st[i], 32)

            def load_up(n):
                if n >= 4:
                    sp.wait_ge(up_lo_ok, n - 3)
                ld(up_raw[:, n % 4, :, :], up_src[n]).then_inc(up_ld[n % 4], 16)

            def load_dn(n):
                if n >= 4:
                    sp.wait_ge(dn_lo_ok, n - 3)
                ld(dn_raw[:, n % 4, :], dn_src[n]).then_inc(dn_ld[n % 4], 16)

            def load_ffn(b):
                for r in range(NR):
                    for u in range(2 * FR):
                        load_up(b["up0"] + r * 2 * FR + u)
                    for u in range(2 * FR):
                        load_dn(b["dn0"] + r * 2 * FR + u)

            sp.wait_ge(v_st, 2 * 16)
            sp.wait_ge(w_st, 2 * 32)
            sp.wait_ge(k_st, 2 * 16)
            for b in BLOCKS[:3]:
                load_ffn(b)
            for n in range(UP_MIX, UP_F2):
                load_up(n)
            sp.wait_ge(pj_ev, 4)
            ld(u_dram[:, :, 0:CTX].rearrange("c p n -> p c n"), hs[:, :, 0:CTX]).then_inc(u_st, 16)
            for tb in range(2):
                sp.wait_ge(pj_ev, 12 + 8 * tb)
                n0 = CTX + tb * TB
                ld(u_dram[:, :, n0:n0 + TB].rearrange("c p n -> p c n"), hs[:, :, n0:n0 + TB]).then_inc(u_st, 16)
            sp.wait_ge(up_used, UP_F2)
            ld(vt[:, :, :, :], v_dram).then_inc(vt_ld, 16)
            sp.wait_ge(u_st, 48)
            uc = u_dram[:, :, 0:CTX].rearrange("c (g i) (s k) -> s i (c g) k", i=GC, s=T)
            ul = u_dram[:, :, CTX:].rearrange("c (g i) (s k) -> s i (c g) k", i=GC, s=T)
            for s in range(T):
                ld(U[s * GC:(s + 1) * GC, :, 0:KC], uc[s]).then_inc(u_ld, 16)
                ld(U[s * GC:(s + 1) * GC, :, KC:], ul[s]).then_inc(u_ld, 16)
            for s in range(T):
                ld(M[s * GC:(s + 1) * GC, :, :], k_dram[:, :, (7 - s) * GC:(15 - s) * GC]).then_inc(m_ld, 16)
            ld(pws[:, :, :], pool_w[0].rearrange("k c d -> c k d")).then_inc(pws_ld, 16)
            sp.wait_ge(sl_t, 16)
            ld(wy[:, :, :, :], w_dram).then_inc(w_ld, 16)
            ld(gate[:, :, :], g_dram.rearrange("n p d -> p n d")).then_inc(gate_ld, 16)
            sp.wait_ge(y_t, 8)
            ld(wglu[:, :, :], s5_w_glu[0].rearrange("(k p) n -> p k n", p=P)).then_inc(glu_ld, 16)
            for mx in MIX:
                for u in range(16):
                    load_dn(mx["dn0"] + u)
            sp.wait_ge(z_t, 8)
            for b in BLOCKS[3:]:
                load_ffn(b)
            sp.wait_ge(added, BLOCKS[4]["ev0"] - 0)
            sp.wait_ge(dn_used, len(dn_src))
            ld(h32f, final_g.rearrange("(o n) -> o n", o=1).broadcast_to([P, D])).then_inc(fg_ld, 16)
            for t in range(T):
                sp.wait_ge(fin_ok, t + 1)
                ld(out_d[:, t, :], xl[:, t, :]).then_inc(out_st, 16)
            sp.wait_ge(out_st, 16 * T)

        @block.gpsimd
        def _(pool):
            gp = nc.gpsimd
            count = [0]

            def step(ins):
                count[0] += 1
                ins.then_inc(pool_step, 1)
                pool.wait_ge(pool_step, count[0])

            step(gp.memset(ident[:, :], 0.0))
            step(gp.affine_select(out=ident[:, :], in_=ident[:, :], compare_op=ALU.not_equal, fill=1.0,
                                  base=0, pattern=[[-1, P]], channel_multiplier=1))
            gp.memset(ones[:, :], 1.0).then_inc(const_ok, 1)
            for i, w in enumerate(WINDOWS):
                lo, hi = w // 2, w - 1 - w // 2
                for tab, n in ((inv_r, GR), (inv_c, GW)):
                    if n > lo + hi:
                        gp.memset(tab[:, i, lo:n - hi], 1.0 / w)
                    for t in list(range(min(lo, n))) + list(range(max(lo, n - hi), n)):
                        gp.memset(tab[:, i, t:t + 1], 1.0 / (min(t + hi + 1, n) - max(t - lo, 0)))
            pool.wait_ge(s5_ld, 16 * S5_LOADS)
            step(gp.affine_select(out=dm[:, :, :], in_=dm[:, :, :], compare_op=ALU.is_equal, fill=0.0,
                                  base=0, pattern=[[0, G], [-1, GC]], channel_multiplier=1))
            pool.wait_ge(q4_ev, 1)

            def cmul(outr, outi, ar, ai, br, bi, ta, tb, neg=False):
                step(gp.tensor_tensor(ta, ar, br, ALU.mult))
                step(gp.tensor_tensor(tb, ai, bi, ALU.mult))
                step(gp.tensor_tensor(outr, ta, tb, ALU.add if neg else ALU.subtract))
                step(gp.tensor_tensor(ta, ar, bi, ALU.mult))
                step(gp.tensor_tensor(tb, ai, br, ALU.mult))
                step(gp.tensor_tensor(outi, ta, tb, ALU.subtract if neg else ALU.add))

            step(gp.memset(pw[:, 0, 0, :], 1.0))
            step(gp.memset(pw[:, 0, 1, :], 0.0))
            step(gp.tensor_copy(pw[:, 1, :, :], q4t[:, 0:2, :]))
            for n in (1, 2, 4):
                def b(i):
                    return pw[:, n, i, :].unsqueeze(1).broadcast_to([P, n, G])
                cmul(pw[:, n + 1:2 * n + 1, 0, :], pw[:, n + 1:2 * n + 1, 1, :],
                     pw[:, 1:n + 1, 0, :], pw[:, 1:n + 1, 1, :], b(0), b(1), pt[:, 0, 0:n, :], pt[:, 1, 0:n, :])
            step(gp.tensor_copy(pwv[0:ST, ::-1, :, :], pw[0:ST, 0:8, :, :]))
            step(gp.tensor_copy(pwv[ST:P, :, :, :], pw[ST:P, 0:8, :, :]))
            step(gp.tensor_copy(pww[0:ST, :, :, :], pw[0:ST, 1:9, :, :]))
            step(gp.tensor_copy(pww[ST:P, ::-1, :, :], pw[ST:P, 1:9, :, :]))
            for i in range(2):
                step(gp.tensor_copy(abar[:, 0, i, :], pw[:, 8, 0, :]))
            step(gp.tensor_copy(abar[:, 1, 0, :], pw[:, 8, 1, :]))
            step(gp.tensor_scalar(abar[:, 1, 1, :], pw[:, 8, 1, :], -1.0, None, ALU.mult))

            def over_c(a, n=G):
                return a.unsqueeze(2).broadcast_to([P, n, GC])
            cmul(bb[:, 0], bb[:, 1], over_c(q4t[:, 2, :]), over_c(q4t[:, 3, :]), bn[:, 0], bn[:, 1], t1[:, :, :], t2[:, :, :])
            pool.wait_ge(ct_ev, 2)
            step(gp.tensor_copy(bf[0:ST], bb[0:ST]))
            step(gp.memset(bf[ST:P], 0.0))
            step(gp.tensor_copy(bk[ST:P], bb[ST:P]))
            step(gp.memset(bk[0:ST], 0.0))
            for gh in range(2):
                gs_ = slice(gh * 16, gh * 16 + 16)
                ta, tb = t1[:, 0:16, :], t2[:, 0:16, :]
                if gh:
                    pool.wait_ge(vt_t, 8)
                for s in range(T):
                    cmul(vn[:, 0, :, s, :], vn[:, 1, :, s, :], over_c(pwv[:, s, 0, gs_], 16), over_c(pwv[:, s, 1, gs_], 16),
                         bb[:, 0, gs_], bb[:, 1, gs_], ta, tb)
                gp.tensor_copy(pt[:, 0, 0, 0:1], pw[:, 0, 0, 0:1]).then_inc(v_ok, 1)
                if gh:
                    pool.wait_ge(w_st, 32)
                    pool.wait_ge(kt_t, 16)
                for t in range(T):
                    cmul(wn[:, 0, :, t, :], wn[:, 1, :, t, :], over_c(pww[:, t, 0, gs_], 16), over_c(pww[:, t, 1, gs_], 16),
                         cn[:, 0, gs_], cn[:, 1, gs_], ta, tb, neg=True)
                gp.tensor_copy(pt[:, 0, 1, 0:1], pw[:, 0, 0, 0:1]).then_inc(w_ok, 1)
                for i in range(2):
                    pool.dma_start(w_dram[:, i, gs_, :], wn[:, i].rearrange("p g t c -> p g (t c)")).then_inc(w_st, 16)
                pool.wait_ge(vt_ev, 8 * (gh + 1))
                pool.dma_start(v_dram[:, gs_], vts[:, :, :, :]).then_inc(v_st, 16)
                pool.wait_ge(kt_ev, 16 * (gh + 1))
                step(gp.tensor_tensor(kp[:, :, 7, :], kp[:, :, 7, :], dm[:, gs_, :], ALU.add))
                pool.dma_start(k_dram[:, gs_, :], kp[:, :, :, :].rearrange("p g n c -> p g (n c)")).then_inc(k_st, 16)
            pool.wait_ge(v_st, 32)
            pool.wait_ge(w_st, 64)
            pool.wait_ge(k_st, 32)
            gp.tensor_copy(pt[:, 0, 0, 1:2], pw[:, 0, 0, 0:1]).then_inc(setup_ok, 1)

            def add_tiles(st, nt, halves):
                for hh in range(halves):
                    for t in range(nt):
                        e = st["ev0"] + hh * nt + t
                        pool.wait_ge(gated, e + 1)
                        dst = xt(st, t)[:, (hh % 2) * HALF:(hh % 2 + 1) * HALF]
                        gp.tensor_tensor(dst, dst, evt[:, e % 2, :], ALU.add).then_inc(added, 1)

            for b in BLOCKS[:3]:
                add_tiles(b, 2 if b["ctx"] else 4, 2 * NR)
            pool.wait_ge(pj_ev, 20)
            pool.wait_ge(u_st, 48)
            for i, w in enumerate(WINDOWS):
                hi = w // 2 - 1
                v = vp[:, i, :].rearrange("p (r c) -> p r c", c=GW)
                cur, nxt = bxa, bxb

                def rows(buf):
                    return buf[:, 0:(GR + hi) * GW].rearrange("p (r c) -> p r c", c=GW)

                def cols(buf):
                    return buf[:, 0:GR * (GW + hi)].rearrange("p (r c) -> p r c", c=GW + hi)
                step(gp.tensor_copy(rows(cur)[:, 0:GR, :], v))
                if hi:
                    step(gp.memset(rows(cur)[:, GR:, :], 0.0))
                m = 1
                while m < w:
                    a, o = rows(cur), rows(nxt)
                    step(gp.tensor_tensor(o[:, m:, :], a[:, m:, :], a[:, 0:GR + hi - m, :], ALU.add))
                    step(gp.tensor_copy(o[:, 0:m, :], a[:, 0:m, :]))
                    cur, nxt = nxt, cur
                    m *= 2
                step(gp.tensor_tensor(cols(nxt)[:, :, 0:GW], rows(cur)[:, hi:, :],
                                      inv_r[:, i, :].unsqueeze(2).broadcast_to([P, GR, GW]), ALU.mult))
                cur, nxt = nxt, cur
                if hi:
                    step(gp.memset(cols(cur)[:, :, GW:], 0.0))
                m = 1
                while m < w:
                    a, o = cols(cur), cols(nxt)
                    step(gp.tensor_tensor(o[:, :, m:], a[:, :, m:], a[:, :, 0:GW + hi - m], ALU.add))
                    step(gp.tensor_copy(o[:, :, 0:m], a[:, :, 0:m]))
                    cur, nxt = nxt, cur
                    m *= 2
                pooled = nxt[:, 0:SEQ].rearrange("p (r c) -> p r c", c=GW)
                step(gp.tensor_tensor(pooled, cols(cur)[:, :, hi:],
                                      inv_c[:, i, :].unsqueeze(1).broadcast_to([P, GR, GW]), ALU.mult))
                step(gp.tensor_tensor(pooled, pooled, v, ALU.subtract))
                gp.tensor_copy(vp[:, i, :].rearrange("p (s k) -> p s k", s=T),
                               nxt[:, 0:SEQ].rearrange("p (k s) -> p s k", s=T)).then_inc(pool_ok, 1)
                pool.wait_ge(pool_ok, i + 1)
            for mx in MIX:
                mx["ctx"] = False
                add_tiles(mx, 4, 2)
            for b in BLOCKS[3:]:
                add_tiles(b, 4, 2 * NR)

        def next_units(b_up0, b_dn0, r):
            return None

        @block.scalar
        def _(act):
            sa = nc.scalar.activation
            act.wait_ge(vec_t, 1)
            sa(vcol[:, :], ps[:, 0, 0:44], ACT.Copy).then_inc(vec_ok, 1)
            act.wait_ge(vec_ok, 1)
            sa(scol[:, :], vcol[:, 0:16], ACT.Silu).then_inc(sil_ok, 1)
            for i in range(2):
                act.wait_ge(ct_t, i + 1)
                sa(cn[:, i].rearrange("p g c -> p (g c)"), ps[:, 1 + i, :], ACT.Copy, scale=1.0 - 2.0 * i).then_inc(ct_ev, 1)
            act.wait_ge(ang_ok, 1)
            sa(sm[:, 4, :], sm[:, 3, :], ACT.Sin).then_inc(sin_ok, 1)
            sa(sm[:, 5, :], sm[:, 3, :], ACT.Sin, scale=0.5).then_inc(sin_ok, 1)
            act.wait_ge(q4_t, 1)
            sa(q4t[:, :, :], ps[:, 3, 0:4 * G].rearrange("p (a g) -> p a g", a=4), ACT.Copy).then_inc(q4_ev, 1)

            def modulation(q):
                m, h = q // 2, q % 2
                act.wait_ge(mod_t, q + 1)
                for cond in range(2 if m < 5 else 1):
                    src = ps[:, 4 + 2 * (q % 2) + cond, :]
                    n = m // 3
                    if m % 3 == 0:
                        sa(bcol[:, (2 + n) if cond == 0 else n, 4 * h:4 * h + 4], src[:, 0:4], ACT.Copy).then_inc(mod_ev, 1)
                    elif m == 2:
                        sa(gate[:, 1 - cond, h * 512:(h + 1) * 512], src, ACT.Copy, scale=0.5).then_inc(mod_ev, 1)
                    elif m % 3 == 2 and cond == 0:
                        e = 2 * (m // 3 - 1) + h
                        if e >= 2:
                            act.wait_ge(grow_st[e % 2], 16)
                        sa(growt[:, h, :], src, ACT.Copy, scale=0.5 if m == 8 else 1.0).then_inc(grow_ok, 1)

            def v_evict(gh):
                for i in range(8):
                    act.wait_ge(vt_t, gh * 8 + i + 1)
                    if gh and i == 0:
                        act.wait_ge(v_st, 16)
                    sa(vts[:, 2 * i:2 * i + 2, :, :].rearrange("p g a n -> p (g a n)"), ps[:, i % 2, :], ACT.Copy).then_inc(vt_ev, 1)

            def k_evict(gh):
                for i in range(16):
                    act.wait_ge(kt_t, gh * 16 + i + 1)
                    if gh and i == 0:
                        act.wait_ge(k_st, 16)
                    sa(kp[:, i, :, :].rearrange("p n c -> p (n c)"), ps[0:GC, 2 + i % 2, 0:15 * GC], ACT.Copy).then_inc(kt_ev, 1)

            for q in range(9):
                modulation(q)
            v_evict(0)
            k_evict(0)
            for q in range(9, 18):
                modulation(q)
            v_evict(1)
            k_evict(1)

            def conv_up(n):
                act.wait_ge(up_ld[n % 4], 16 * (n // 4 + 1))
                if n >= 2:
                    act.wait_ge(up_used, n - 1)
                sa(up_hi[:, n % 2], up_raw[:, n % 4], ACT.Copy).then_inc(up_hi_ok, 1)

            def conv_dn(n):
                act.wait_ge(dn_ld[n % 4], 16 * (n // 4 + 1))
                if n >= 2:
                    act.wait_ge(dn_used, n - 1)
                sa(dn_hi[:, n % 2], dn_raw[:, n % 4], ACT.Copy).then_inc(dn_hi_ok, 1)

            def squares(p):
                if p["ev"]:
                    act.wait_ge(added, p["ev"])
                for t in range(p["nt"]):
                    q = p["q0"] + t
                    if p["n"] >= 1:
                        act.wait_ge(ht_ok, 8 * p["n"])
                        act.wait_ge(rstd_ok, p["n"])
                    sa(xn[:, t, :], xt(p, t), ACT.Square, accum_out=ssq[:, t:t + 1]).then_inc(sq_ok, 1)

            def hi_of_h(p, k0, k1):
                nk = p["nt"] * P
                for k in range(k0, k1):
                    act.wait_ge(h32_ok, 8 * p["n"] + k + 1)
                    sa(h_hi[:, k, 0:nk], h32[:, k % 2, 0:nk], ACT.Copy).then_inc(hhi_ok, 1)

            def ffn(b, prep, look):
                nt = 2 if b["ctx"] else 4
                nk = nt * P
                u, dd, F = b["up0"], b["dn0"], b["F0"]
                for r in range(NR):
                    for f in range(FR):
                        nxt = [("u", u + 2 * f + 2), ("u", u + 2 * f + 3)] if f < FR - 1 else [("d", dd), ("d", dd + 1)]
                        fn = {"u": conv_up, "d": conv_dn}
                        fn[nxt[0][0]](nxt[0][1])
                        act.wait_ge(up_used, u + 2 * f + 1)
                        if F + f >= 2:
                            act.wait_ge(prod_ok, F + f - 1)
                        sa(sg[:, (F + f) % 2, 0:nk], ps[:, 2 * ((F + f) % 2), 0:nk], ACT.Silu).then_inc(silu_ok, 1)
                        fn[nxt[1][0]](nxt[1][1])
                        act.wait_ge(prod_ok, F + f + 1)
                        sa(a_hi[:, f, 0:nk], a32[:, (F + f) % 2, 0:nk], ACT.Copy).then_inc(ahi_ok, 1)
                        if r == 1 and prep is not None and f == 4:
                            squares(prep)
                    for i in range(2 * FR):
                        if i + 2 < 2 * FR:
                            conv_dn(dd + i + 2)
                        elif r == 0:
                            conv_up(u + 2 * FR + i + 2 - 2 * FR)
                        elif look is not None:
                            conv_up(look + i + 2 - 2 * FR)
                        if r == 1 and prep is not None and i in (FR, FR + 6):
                            hi_of_h(prep, *((0, 4) if i == FR else (4, 8)))
                    u += 2 * FR
                    dd += 2 * FR
                    F += FR

            act.wait_ge(setup_ok, 1)
            for i in range(2):
                act.wait_ge(grow_st[i], 32)
            squares(PREPS[0])
            hi_of_h(PREPS[0], 0, 8)
            conv_up(0)
            conv_up(1)
            ffn(BLOCKS[0], PREPS[1], BLOCKS[1]["up0"])
            ffn(BLOCKS[1], PREPS[2], BLOCKS[2]["up0"])
            ffn(BLOCKS[2], None, PROJ[0]["up0"])
            for pr, prep in zip(PROJ, PREPS[3:6]):
                squares(prep)
                hi_of_h(prep, 0, 8)
                for j in range(len(pr["tiles"])):
                    n = pr["up0"] + j + 2
                    if n < UP_F2:
                        conv_up(n)
            for i in range(4):
                act.wait_ge(sc_t, i + 1)
                cc, gq = i // 2, (i % 2) * 16
                src = ps[:, i, :].rearrange("p (g k) -> p k g", k=KC)
                sa(Sc[0:ST, :, cc, gq:gq + 16], src[0:ST], ACT.Copy)
                sa(Sc[ST:P, ::-1, cc, gq:gq + 16], src[ST:P], ACT.Copy).then_inc(sc_ev, 1)
            for i in range(16):
                act.wait_ge(sl_t, i + 1)
                cc, gq = i % 2, (i // 2) * 4
                src = ps[:, 4 + i % 4, :].rearrange("p (g k) -> p k g", k=KL)
                sa(S[0:ST, :, cc, gq:gq + 4], src[0:ST], ACT.Copy).then_inc(sl_eva, 1)
            act.wait_ge(scan_step, 3 * (KC + KL) - 3)
            act.wait_ge(pool_ok, 4)
            sa(Hk[0:ST, :, :, 0:1].rearrange("p a g k -> p (a g k)"), Sc[0:ST, KC - 1].rearrange("p a g -> p (a g)"), ACT.Copy)
            sa(Hk[0:ST, :, :, 1:].rearrange("p a g k -> p (a g) k"),
               S[0:ST, 0:KL - 1].rearrange("p k a g -> p (a g) k"), ACT.Copy).then_inc(hk_a, 1)
            for i in range(8):
                act.wait_ge(y_t, i + 1)
                if i == 0:
                    act.wait_ge(hk_d, 1)
                sa(y[:, :, 64 * i:64 * i + 64].rearrange("p t (g c) -> p g t c", c=GC),
                   ps[:, i % 4, :].rearrange("p (g t c) -> p g t c", g=4, c=GC), ACT.Copy).then_inc(y_ev, 1)
            for i in range(8):
                act.wait_ge(yt_t, i + 1)
                cc, tb = i % 4, i // 4
                sa(yg[:, cc, tb * TB:(tb + 1) * TB], ps[:, 4 + i % 4, :], ACT.Gelu_apprx_tanh).then_inc(yg_ok, 1)
            for tb in range(2):
                for j in range(8):
                    n = tb * 8 + j
                    if j >= 4:
                        act.wait_ge(z_t, tb * 4 + j - 3)
                        if n >= 6:
                            act.wait_ge(m32_ok, (n - 2) + 1)
                        sa(gs[:, n % 2, :], ps[:, 4 + j % 4, :], ACT.Sigmoid).then_inc(gs_ok, 1)
                    act.wait_ge(m32_ok, n + 1)
                    if n == 0:
                        act.wait_ge(y_t, 8)
                    if tb and j == 0:
                        act.wait_ge(dn_used, MIX[1]["dn0"])
                    sa(h_hi[:, j, :], m32[:, n % 2, :], ACT.Copy).then_inc(mhi_ok, 1)
                d0 = MIX[tb]["dn0"]
                conv_dn(d0)
                conv_dn(d0 + 1)
                for i in range(14):
                    conv_dn(d0 + i + 2)
            squares(PREPS[6])
            hi_of_h(PREPS[6], 0, 8)
            conv_up(UP_F2)
            conv_up(UP_F2 + 1)
            ffn(BLOCKS[3], PREPS[7], BLOCKS[4]["up0"])
            ffn(BLOCKS[4], None, None)
            for g4 in range(2):
                act.wait_ge(added, EV_END)
                for t in range(4):
                    if g4:
                        act.wait_ge(rstd_ok, len(PREPS) + 1)
                    sa(xn[:, t, :], xl[:, 4 * g4 + t, :], ACT.Square, accum_out=ssq[:, t:t + 1]).then_inc(sq_ok, 1)

        @block.vector
        def _(dve):
            ve = nc.vector
            tt, ts, stt = ve.tensor_tensor, ve.tensor_scalar, ve.scalar_tensor_tensor
            count = [0]

            def step(ins):
                count[0] += 1
                ins.then_inc(dve_step, 1)
                dve.wait_ge(dve_step, count[0])

            def exp(dst, src, k, f, ki):
                step(ts(f, src, -88.0, 89.0, ALU.max, ALU.min))
                step(ts(k, f, LOG2E, MAGIC, ALU.mult, ALU.add))
                step(ts(k, k, -MAGIC, None, ALU.add))
                step(stt(out=f, in0=k, scalar=-LN2[0], in1=f, op0=ALU.mult, op1=ALU.add))
                step(stt(out=f, in0=k, scalar=-LN2[1], in1=f, op0=ALU.mult, op1=ALU.add))
                step(ts(k, k, 127.0, None, ALU.add))
                step(ve.tensor_copy(ki, k))
                step(ts(ki, ki, 23, None, ALU.logical_shift_left))
                step(ts(k, f, 1.0 / 5040, None, ALU.mult))
                for n in (720, 120, 24, 6, 2, 1):
                    step(stt(out=k, in0=k, scalar=1.0 / n, in1=f, op0=ALU.add, op1=ALU.mult))
                step(ts(k, k, 1.0, None, ALU.add))
                step(tt(dst, k, ki.bitcast(F32), ALU.mult))

            dve.wait_ge(s5_ld, 16 * S5_LOADS)
            are, aim = sm[:, 0, :], sm[:, 1, :]
            exp(dt2[:, 1, :], dt2[:, 0, :], dt2[:, 2, :], dt2[:, 3, :], dt2i[:, :])
            for d in range(2):
                half = slice(d * ST, (d + 1) * ST)
                step(ts(sm[:, 2, half], sm[:, 0, half], dt2[:, 1, d:d + 1], None, ALU.mult))
                step(ts(sm[:, 3, half], sm[:, 1, half], dt2[:, 1, d:d + 1], None, ALU.mult))
            th, k_ = sm[:, 3, :], sm[:, 6, :]
            step(ts(k_, th, INV2PI, MAGIC, ALU.mult, ALU.add))
            step(ts(k_, k_, -MAGIC, None, ALU.add))
            for part in TWO_PI:
                step(stt(out=th, in0=k_, scalar=-part, in1=th, op0=ALU.mult, op1=ALU.add))
            step(ts(th, th, -PI_IN, PI_IN, ALU.max, ALU.min))
            ts(th, th, 1.0, None, ALU.mult).then_inc(ang_ok, 1)
            exp(sm[:, 7, :], sm[:, 2, :], sm[:, 6, :], sm[:, 8, :], smi[:, :])
            dve.wait_ge(sin_ok, 2)
            mag, s1, s2 = sm[:, 7, :], sm[:, 4, :], sm[:, 5, :]
            ar, ai, cr, ci = (sm[:, 9 + i, :] for i in range(4))
            step(tt(s2, s2, s2, ALU.mult))
            step(ts(s2, s2, -2.0, 1.0, ALU.mult, ALU.add))
            step(tt(ar, mag, s2, ALU.mult))
            step(tt(ai, mag, s1, ALU.mult))
            nr, den, ta, tb = sm[:, 13, :], sm[:, 14, :], sm[:, 15, :], sm[:, 6, :]
            step(ts(nr, ar, -1.0, None, ALU.add))
            step(tt(den, are, are, ALU.mult))
            step(tt(ta, aim, aim, ALU.mult))
            step(tt(den, den, ta, ALU.add))
            step(ve.reciprocal(den, den))
            step(tt(ta, nr, are, ALU.mult))
            step(tt(tb, ai, aim, ALU.mult))
            step(tt(ta, ta, tb, ALU.add))
            step(tt(cr, ta, den, ALU.mult))
            step(tt(ta, ai, are, ALU.mult))
            step(tt(tb, nr, aim, ALU.mult))
            step(tt(ta, ta, tb, ALU.subtract))
            tt(ci, ta, den, ALU.mult).then_inc(q4_ok, 1)

            dve.wait_ge(sil_ok, 1)
            for q in range(18):
                m, h = q // 2, q % 2
                conds = 2 if m < 5 else 1
                dve.wait_ge(ada_ld[q % 2], 32 * (q // 2 + 1))
                if q >= 2:
                    dve.wait_ge(mod_t, q - 1)
                for k in range(DK):
                    for cond in range(conds):
                        a = acc[:, q % 2, cond, :]
                        sc = scol[:, 8 * cond + k:8 * cond + k + 1]
                        if k == 0:
                            ins = ts(a, ada[:, q % 2, k, :], sc, None, ALU.mult)
                        else:
                            ins = stt(out=a, in0=ada[:, q % 2, k, :], scalar=sc, in1=a, op0=ALU.mult, op1=ALU.add)
                        if k == DK - 1 and cond == conds - 1:
                            ins.then_inc(acc_ok, 1)
                        else:
                            step(ins)
                if m % 3 == 1:
                    dve.wait_ge(mod_t, q + 1)
                    n = m // 3
                    for cond in range(conds):
                        step(stt(out=gcol[:, (2 + n) if cond == 0 else n, 4 * h:4 * h + 4],
                                 in0=ps[:, 4 + 2 * (q % 2) + cond, 0:4], scalar=1.0,
                                 in1=vcol[:, 16 + 8 * n + 4 * h:16 + 8 * n + 4 * h + 4], op0=ALU.add, op1=ALU.mult))

            def rstd(n, nt, last):
                v, r, a, b_ = (rs[:, i, 0:nt] for i in range(4))
                ri = rs[:, 4, 0:nt].bitcast(I32)
                dve.wait_ge(sq_ok, last)
                step(ts(v, ssq[:, 0:nt], 1.0 / D, EPS, ALU.mult, ALU.add))
                step(ts(ri, v.bitcast(I32), 1, None, ALU.logical_shift_right))
                step(ve.tensor_copy(a, ri))
                step(ts(a, a, -1.0, float(0x5f3759df), ALU.mult, ALU.add))
                step(ve.tensor_copy(ri, a))
                step(ve.tensor_copy(r, ri.bitcast(F32)))
                for it in range(4):
                    step(tt(a, r, r, ALU.mult))
                    step(tt(a, a, v, ALU.mult))
                    step(ts(a, a, -0.5, 1.5, ALU.mult, ALU.add))
                    if it < 3:
                        step(tt(r, r, a, ALU.mult))
                    else:
                        tt(rs[:, 5, 0:nt], r, a, ALU.mult).then_inc(rstd_ok, 1)
                        dve.wait_ge(rstd_ok, n + 1)

            def normalise(p):
                rstd(p["n"], p["nt"], p["q0"] + p["nt"])
                for t in range(p["nt"]):
                    ts(xn[:, t, :], xt(p, t), rs[:, 5, t:t + 1], None, ALU.mult).then_inc(xn_ok, 1)

            def split_h(p, k0, k1):
                nk = p["nt"] * P

                def low(k):
                    dve.wait_ge(hhi_ok, 8 * p["n"] + k + 1)
                    tt(h_lo[:, k, 0:nk], h32[:, k % 2, 0:nk], h_hi[:, k, 0:nk].bitcast(F32), ALU.subtract).then_inc(hlo_ok, 1)
                for k in range(k0, k1):
                    dve.wait_ge(ht_ok, 8 * p["n"] + k + 1)
                    if 8 * p["n"] + k >= 2:
                        dve.wait_ge(hlo_ok, 8 * p["n"] + k - 1)
                    ts(h32[:, k % 2, 0:nk], ps[:, k % 4, 0:nk], gcol[:, p["col"], k:k + 1], bcol[:, p["col"], k:k + 1],
                       ALU.mult, ALU.add).then_inc(h32_ok, 1)
                    if k > k0:
                        low(k - 1)
                low(k1 - 1)

            def lo_up(n):
                dve.wait_ge(up_hi_ok, n + 1)
                tt(up_lo[:, n % 2], up_raw[:, n % 4], up_hi[:, n % 2].bitcast(F32), ALU.subtract).then_inc(up_lo_ok, 1)

            def lo_dn(n):
                dve.wait_ge(dn_hi_ok, n + 1)
                tt(dn_lo[:, n % 2], dn_raw[:, n % 4], dn_hi[:, n % 2].bitcast(F32), ALU.subtract).then_inc(dn_lo_ok, 1)

            def gated_tile(e, t, g_row, hh):
                if e >= 2:
                    dve.wait_ge(added, e - 1)
                tt(evt[:, e % 2, :], ps[:, 4 + t, :], gate[:, g_row, hh * HALF:(hh + 1) * HALF], ALU.mult).then_inc(gated, 1)

            def ffn(b, prep, look):
                nt = 2 if b["ctx"] else 4
                nk = nt * P
                u, dd, F = b["up0"], b["dn0"], b["F0"]
                fn = {"u": lo_up, "d": lo_dn}
                for r in range(NR):
                    for f in range(FR):
                        nxt = [("u", u + 2 * f + 2), ("u", u + 2 * f + 3)] if f < FR - 1 else [("d", dd), ("d", dd + 1)]
                        fn[nxt[0][0]](nxt[0][1])
                        n = F + f
                        dve.wait_ge(silu_ok, n + 1)
                        dve.wait_ge(up_used, u + 2 * f + 2)
                        if n >= 2:
                            dve.wait_ge(ahi_ok, n - 1)
                            dve.wait_ge(alo_ok, n - 1)
                        tt(a32[:, n % 2, 0:nk], sg[:, n % 2, 0:nk], ps[:, 2 * (n % 2) + 1, 0:nk], ALU.mult).then_inc(prod_ok, 1)
                        fn[nxt[1][0]](nxt[1][1])
                        dve.wait_ge(ahi_ok, n + 1)
                        tt(a_lo[:, f, 0:nk], a32[:, n % 2, 0:nk], a_hi[:, f, 0:nk].bitcast(F32), ALU.subtract).then_inc(alo_ok, 1)
                        if r == 1 and prep is not None and f == 6:
                            normalise(prep)
                    for i in range(2 * FR):
                        if i in (FR - 1, 2 * FR - 1):
                            hh = i // FR
                            e0 = b["ev0"] + (2 * r + hh) * nt
                            dve.wait_ge(dn_used, dd + i + 1)
                            for t in range(nt):
                                gated_tile(e0 + t, t, b["gate"], hh)
                                if t == nt // 2 - 1:
                                    if i == FR - 1:
                                        lo_dn(dd + i + 2)
                                    elif r == 0:
                                        lo_up(u + 2 * FR + 1)
                                    elif look is not None:
                                        lo_up(look + 1)
                        elif i + 2 < 2 * FR:
                            lo_dn(dd + i + 2)
                        elif r == 0:
                            lo_up(u + 2 * FR)
                        elif look is not None:
                            lo_up(look)
                        if r == 1 and prep is not None and i in (FR, FR + 6):
                            split_h(prep, *((0, 4) if i == FR else (4, 8)))
                    u += 2 * FR
                    dd += 2 * FR
                    F += FR

            dve.wait_ge(x_ld, 32)
            normalise(PREPS[0])
            split_h(PREPS[0], 0, 8)
            lo_up(0)
            lo_up(1)
            ffn(BLOCKS[0], PREPS[1], BLOCKS[1]["up0"])
            ffn(BLOCKS[1], PREPS[2], BLOCKS[2]["up0"])
            ffn(BLOCKS[2], None, PROJ[0]["up0"])
            ev_i = 0
            for pr, prep in zip(PROJ, PREPS[3:6]):
                normalise(prep)
                split_h(prep, 0, 8)
                for j, mt in enumerate(pr["tiles"]):
                    n = pr["up0"] + j
                    if n + 2 < UP_F2:
                        lo_up(n + 2)
                    dve.wait_ge(up_used, n + 1)
                    src = ps[:, 4 + j % 4, :]
                    if pr["ctx"]:
                        ve.tensor_copy(hs[:, mt - 4, 0:CTX].rearrange("p (s i k) -> p s i k", s=4, i=2),
                                       src[:, 0:CTX].rearrange("p (i k s) -> p s i k", s=4, i=2)).then_inc(pj_ev, 1)
                    elif mt >= 4:
                        n0 = CTX + pr["t0"] * P
                        ve.tensor_copy(hs[:, mt - 4, n0:n0 + TB], src).then_inc(pj_ev, 1)
                    else:
                        ve.tensor_copy(vp[:, mt, :].rearrange("p (k s) -> p s k", s=T)[:, pr["t0"]:pr["t0"] + 4, :],
                                       src.rearrange("p (s k) -> p s k", s=4)).then_inc(pj_ev, 1)
                    ev_i += 1

            scans = [0]

            def scan_to(dst, prev):
                pr_, tm = scn[:, 0:2, :], scn[:, 2, :]
                ve.tensor_tensor(pr_, abar[:, :, :, :].rearrange("p a b g -> p a (b g)"),
                                 prev.rearrange("p a g -> p (a g)").unsqueeze(1).broadcast_to([P, 2, 2 * G]), ALU.mult).then_inc(scan_step, 1)
                scans[0] += 1
                dve.wait_ge(scan_step, scans[0])
                ve.tensor_tensor(tm.rearrange("p (a g) -> p a g", a=2), scn[:, 0, :].rearrange("p (a g) -> p a g", a=2),
                                 scn[:, 1, :].rearrange("p (a g) -> p a g", a=2)[:, ::-1, :], ALU.add).then_inc(scan_step, 1)
                scans[0] += 1
                dve.wait_ge(scan_step, scans[0])
                ve.tensor_tensor(dst.rearrange("p a g -> p (a g)"), tm, dst.rearrange("p a g -> p (a g)"), ALU.add).then_inc(scan_step, 1)
                scans[0] += 1
                dve.wait_ge(scan_step, scans[0])

            dve.wait_ge(sc_ev, 4)
            for k in range(1, KC):
                scan_to(Sc[:, k], Sc[:, k - 1])
            for i in range(16):
                dve.wait_ge(sl_t, i + 1)
                cc, gq = i % 2, (i // 2) * 4
                src = ps[:, 4 + i % 4, :].rearrange("p (g k) -> p k g", k=KL)
                ve.tensor_copy(S[ST:P, ::-1, cc, gq:gq + 4], src[ST:P]).then_inc(sl_evd, 1)
            dve.wait_ge(sl_evd, 16)
            dve.wait_ge(sl_eva, 16)
            for k in range(KL):
                scan_to(S[:, k], Sc[:, KC - 1] if k == 0 else S[:, k - 1])
            dve.wait_ge(pool_ok, 4)
            ve.tensor_copy(Hk[ST:P, :, :, KL - 1:KL].rearrange("p a g k -> p (a g k)"), Sc[ST:P, KC - 1].rearrange("p a g -> p (a g)"))
            ve.tensor_copy(Hk[ST:P, :, :, 0:KL - 1].rearrange("p a g k -> p (a g) k")[:, :, ::-1],
                           S[ST:P, 0:KL - 1].rearrange("p k a g -> p (a g) k")).then_inc(hk_d, 1)
            dve.wait_ge(y_t, 8)
            dve.wait_ge(gate_ld, 16)
            for tb in range(2):
                for j in range(8):
                    n = tb * 8 + j
                    if n >= 2:
                        dve.wait_ge(mhi_ok, n - 1)
                        dve.wait_ge(mlo_ok, n - 1)
                    if j < 4:
                        dve.wait_ge(pm_t, tb * 4 + j + 1)
                        ts(m32[:, n % 2, :], ps[:, j, :], vcol[:, 40 + j:41 + j], None, ALU.mult).then_inc(m32_ok, 1)
                    else:
                        dve.wait_ge(gs_ok, tb * 4 + j - 3)
                        tt(m32[:, n % 2, :], gs[:, n % 2, :], yg[:, j - 4, tb * TB:(tb + 1) * TB], ALU.mult).then_inc(m32_ok, 1)
                    dve.wait_ge(mhi_ok, n + 1)
                    tt(h_lo[:, j, :], m32[:, n % 2, :], h_hi[:, j, :].bitcast(F32), ALU.subtract).then_inc(mlo_ok, 1)
                mx = MIX[tb]
                lo_dn(mx["dn0"])
                lo_dn(mx["dn0"] + 1)
                for i in range(16):
                    if i in (7, 15):
                        dve.wait_ge(dn_used, mx["dn0"] + i + 1)
                        for t in range(4):
                            gated_tile(mx["ev0"] + (i // 8) * 4 + t, t, 0, i // 8)
                            if t == 1 and i == 7:
                                lo_dn(mx["dn0"] + i + 2)
                    elif i + 2 < 16:
                        lo_dn(mx["dn0"] + i + 2)
            normalise(PREPS[6])
            split_h(PREPS[6], 0, 8)
            lo_up(UP_F2)
            lo_up(UP_F2 + 1)
            for b in BLOCKS[3:]:
                b["gate"] = 1
            ffn(BLOCKS[3], PREPS[7], BLOCKS[4]["up0"])
            ffn(BLOCKS[4], None, None)
            for g4 in range(2):
                rstd(len(PREPS) + g4, 4, Q_FINAL + 4 * (g4 + 1))
                for t in range(4):
                    tl = xl[:, 4 * g4 + t, :]
                    if g4 == 0 and t == 0:
                        dve.wait_ge(fg_ld, 16)
                    stt(out=tl, in0=tl, scalar=rs[:, 5, t:t + 1], in1=h32f, op0=ALU.mult, op1=ALU.mult).then_inc(fin_ok, 1)

        @block.tensor
        def _(pe):
            mm = nc.tensor.matmul
            tr = nc.tensor.transpose
            pe.wait_ge(const_ok, 1)
            pe.wait_ge(pool_step, 2)
            pe.wait_ge(vec_ld, 64)
            tr(ps[:, 0, 0:44], vecrow[:, :], ident[0:44, 0:44]).then_inc(vec_t, 1)
            pe.wait_ge(s5_ld, 16 * S5_LOADS)
            for i in range(2):
                for j in range(4):
                    ins = tr(ps[:, 1 + i, j * P:(j + 1) * P], craw[:, i, j, :], ident[:, :])
                ins.then_inc(ct_t, 1)
            pe.wait_ge(q4_ok, 1)
            for i in range(4):
                ins = tr(ps[:, 3, i * G:(i + 1) * G], sm[:, 9 + i, :], ident[0:G, 0:G])
            ins.then_inc(q4_t, 1)

            evs = [0]
            ev_after = []
            for q in range(18):
                m = q // 2
                if m % 3 == 0:
                    evs[0] += 2 if m < 5 else 1
                elif m == 2:
                    evs[0] += 2
                ev_after.append(evs[0])

            def modulation(q):
                m = q // 2
                pe.wait_ge(acc_ok, q + 1)
                if q >= 2:
                    if ev_after[q - 2]:
                        pe.wait_ge(mod_ev, ev_after[q - 2])
                    gr = sum(1 for z in range(q - 1) if (z // 2) in (5, 8))
                    if gr:
                        pe.wait_ge(grow_ok, gr)
                for cond in range(2 if m < 5 else 1):
                    o = ps[:, 4 + 2 * (q % 2) + cond, :]
                    a = acc[:, q % 2, cond, :]
                    if m % 3 == 2:
                        mm(o, ones[:, :], a, start=True, stop=False)
                        ins = mm(o, ones[0:1, :], brow[0:1, q % 2, :], start=False, stop=True)
                    else:
                        for j in range(4):
                            mm(o[:, j:j + 1], a[:, j * P:(j + 1) * P], ones[:, 0:1], start=True, stop=False)
                            ins = mm(o[:, j:j + 1], brow[0:1, q % 2, j * P:(j + 1) * P], ones[0:1, 0:1], start=False, stop=True)
                ins.then_inc(mod_t, 1)

            def v_transposes(gh):
                pe.wait_ge(v_ok, gh + 1)
                for i in range(8):
                    n = gh * 8 + i
                    if n >= 2:
                        pe.wait_ge(vt_ev, n - 1)
                    elif n == 0:
                        pe.wait_ge(vec_ok, 1)
                        pe.wait_ge(ct_ev, 2)
                    for g2 in range(2):
                        for a in range(2):
                            ins = tr(ps[:, i % 2, (2 * g2 + a) * P:(2 * g2 + a + 1) * P],
                                     vn[:, a, 2 * i + g2].rearrange("p s c -> p (s c)"), ident[:, :])
                    ins.then_inc(vt_t, 1)

            def responses(gh):
                pe.wait_ge(w_ok, gh + 1)
                for i in range(16):
                    n, g = gh * 16 + i, gh * 16 + i
                    if n >= 2:
                        pe.wait_ge(kt_ev, n - 1)
                    elif n == 0:
                        pe.wait_ge(q4_ev, 1)
                    o = ps[0:GC, 2 + i % 2, :]
                    w = [wn[:, a, i].rearrange("p t c -> p (t c)") for a in range(2)]
                    for a in range(2):
                        mm(o[:, 0:7 * GC], bk[:, a, g, :], w[a][:, GC:], start=a == 0, stop=a == 1)
                    for a in range(2):
                        mm(o[:, 7 * GC:8 * GC], bb[:, a, g, :], cn[:, a, g, :], start=a == 0, stop=a == 1)
                    for a in range(2):
                        ins = mm(o[:, 8 * GC:15 * GC], bf[:, a, g, :], w[a][:, 0:7 * GC], start=a == 0, stop=a == 1)
                    ins.then_inc(kt_t, 1)

            for q in range(9):
                modulation(q)
            v_transposes(0)
            responses(0)
            for q in range(9, 18):
                modulation(q)
            v_transposes(1)
            responses(1)

            def transposes(p, k0):
                if k0 == 0:
                    pe.wait_ge(xn_ok, p["q0"] + p["nt"])
                for k in range(k0, k0 + 4):
                    n = 8 * p["n"] + k
                    if n >= 4:
                        pe.wait_ge(h32_ok, n - 3)
                    for t in range(p["nt"]):
                        ins = tr(ps[:, k % 4, t * P:(t + 1) * P], xn[:, t, k * P:(k + 1) * P], ident[:, :])
                    ins.then_inc(ht_ok, 1)

            def three(o, l_hi, l_lo, r_hi, r_lo, start, stop):
                mm(o, l_hi, r_hi, start=start, stop=False)
                mm(o, l_hi, r_lo, start=False, stop=False)
                return mm(o, l_lo, r_hi, start=False, stop=stop)

            def up_unit(n, o, nk):
                pe.wait_ge(up_lo_ok, n + 1)
                for k in range(DK):
                    ins = three(o, up_hi[:, n % 2, k], up_lo[:, n % 2, k], h_hi[:, k, 0:nk], h_lo[:, k, 0:nk], k == 0, k == DK - 1)
                ins.then_inc(up_used, 1)

            def ffn(b, prep):
                nt = 2 if b["ctx"] else 4
                nk = nt * P
                u, dd, F = b["up0"], b["dn0"], b["F0"]
                for r in range(NR):
                    for f in range(FR):
                        n = F + f
                        if n >= 2:
                            pe.wait_ge(silu_ok, n - 1)
                        up_unit(u + 2 * f, ps[:, 2 * (n % 2), 0:nk], nk)
                        if n >= 2:
                            pe.wait_ge(prod_ok, n - 1)
                        up_unit(u + 2 * f + 1, ps[:, 2 * (n % 2) + 1, 0:nk], nk)
                    for hh in range(2):
                        e0 = b["ev0"] + (2 * r + hh) * nt
                        for k in range(FR):
                            n = dd + hh * FR + k
                            pe.wait_ge(dn_lo_ok, n + 1)
                            pe.wait_ge(alo_ok, F + k + 1)
                            for t in range(nt):
                                if k == 0 and e0 > 0:
                                    pe.wait_ge(gated, max(e0 - nt + t + 1, 1) if e0 - b["ev0"] else e0)
                                ts_ = slice(t * P, (t + 1) * P)
                                ins = three(ps[:, 4 + t, :], a_hi[:, k, ts_], a_lo[:, k, ts_],
                                            dn_hi[:, n % 2, :], dn_lo[:, n % 2, :], k == 0, k == FR - 1)
                            ins.then_inc(dn_used, 1)
                            if r == 1 and hh == 1 and k == 5 and prep is not None:
                                transposes(prep, 4)
                        if r == 1 and hh == 0 and prep is not None:
                            pe.wait_ge(prod_ok, F + FR)
                            transposes(prep, 0)
                    u += 2 * FR
                    dd += 2 * FR
                    F += FR

            pe.wait_ge(kt_ev, 32)
            transposes(PREPS[0], 0)
            transposes(PREPS[0], 4)
            pe.wait_ge(hlo_ok, 8)
            ffn(BLOCKS[0], PREPS[1])
            pe.wait_ge(hlo_ok, 16)
            ffn(BLOCKS[1], PREPS[2])
            pe.wait_ge(hlo_ok, 24)
            ffn(BLOCKS[2], None)
            pe.wait_ge(gated, MIX[0]["ev0"])
            done = 0
            for pr, prep in zip(PROJ, PREPS[3:6]):
                nk = prep["nt"] * P
                pe.wait_ge(up_used, pr["up0"])
                transposes(prep, 0)
                transposes(prep, 4)
                pe.wait_ge(hlo_ok, 8 * prep["n"] + 8)
                for j in range(len(pr["tiles"])):
                    if done >= 4:
                        pe.wait_ge(pj_ev, done - 3)
                    up_unit(pr["up0"] + j, ps[:, 4 + j % 4, 0:nk], nk)
                    done += 1
            pe.wait_ge(pj_ev, 20)
            pe.wait_ge(vt_ld, 16)
            pe.wait_ge(u_ld, 16 * 2 * T)
            for i in range(4):
                cc, gq = i // 2, (i % 2) * 16
                for g in range(16):
                    ins = mm(ps[:, i, g * KC:(g + 1) * KC], vt[:, gq + g, cc, :], U[:, gq + g, 0:KC], start=True, stop=True)
                ins.then_inc(sc_t, 1)
            for i in range(16):
                if i >= 4:
                    pe.wait_ge(sl_eva, i - 3)
                    pe.wait_ge(sl_evd, i - 3)
                cc, gq = i % 2, (i // 2) * 4
                for g in range(4):
                    ins = mm(ps[:, 4 + i % 4, g * KL:(g + 1) * KL], vt[:, gq + g, cc, :], U[:, gq + g, KC:], start=True, stop=True)
                ins.then_inc(sl_t, 1)
            pe.wait_ge(w_ld, 16)
            pe.wait_ge(m_ld, 16 * T)
            pe.wait_ge(sc_ev, 4)
            pe.wait_ge(hk_a, 1)
            pe.wait_ge(hk_d, 1)
            for i in range(8):
                if i >= 4:
                    pe.wait_ge(y_ev, i - 3)
                for g4 in range(4):
                    g = 4 * i + g4
                    o = ps[:, i % 4, g4 * P:(g4 + 1) * P]
                    mm(o, U[:, g, KC:], M[:, g, :], start=True, stop=False)
                    mm(o, Hk[:, 0, g, :], wy[:, 0, g, :], start=False, stop=False)
                    ins = mm(o, Hk[:, 1, g, :], wy[:, 1, g, :], start=False, stop=True)
                ins.then_inc(y_t, 1)
            pe.wait_ge(y_ev, 8)
            for i in range(8):
                cc, tb = i % 4, i // 4
                if i >= 4:
                    pe.wait_ge(yg_ok, i - 3)
                for t in range(4):
                    ins = tr(ps[:, 4 + i % 4, t * P:(t + 1) * P], y[:, tb * 4 + t, cc * P:(cc + 1) * P], ident[:, :])
                ins.then_inc(yt_t, 1)
            pe.wait_ge(pws_ld, 16)
            pe.wait_ge(pool_ok, 4)
            pe.wait_ge(yg_ok, 8)
            pe.wait_ge(glu_ld, 16)
            for tb in range(2):
                for j in range(4):
                    if tb:
                        pe.wait_ge(m32_ok, j + 1)
                    mm(ps[:, j, :], pws[:, j, :], vp[:, j, tb * TB:(tb + 1) * TB], start=True, stop=True).then_inc(pm_t, 1)
                if tb:
                    pe.wait_ge(gated, MIX[1]["ev0"])
                for j in range(4):
                    for k in range(4):
                        ins = mm(ps[:, 4 + j, :], wglu[:, k, j * P:(j + 1) * P], yg[:, k, tb * TB:(tb + 1) * TB],
                                 start=k == 0, stop=k == 3)
                    ins.then_inc(z_t, 1)
                mx = MIX[tb]
                pe.wait_ge(mlo_ok, tb * 8 + 8)
                for hh in range(2):
                    for k in range(DK):
                        n = mx["dn0"] + hh * DK + k
                        pe.wait_ge(dn_lo_ok, n + 1)
                        for t in range(4):
                            if k == 0 and hh == 1:
                                pe.wait_ge(gated, mx["ev0"] + t + 1)
                            ts_ = slice(t * P, (t + 1) * P)
                            ins = three(ps[:, 4 + t, :], h_hi[:, k, ts_], h_lo[:, k, ts_],
                                        dn_hi[:, n % 2, :], dn_lo[:, n % 2, :], k == 0, k == DK - 1)
                        ins.then_inc(dn_used, 1)
            pe.wait_ge(m32_ok, 16)
            transposes(PREPS[6], 0)
            transposes(PREPS[6], 4)
            pe.wait_ge(hlo_ok, 8 * 7)
            pe.wait_ge(gated, BLOCKS[3]["ev0"])
            ffn(BLOCKS[3], PREPS[7])
            pe.wait_ge(hlo_ok, 8 * 8)
            ffn(BLOCKS[4], None)


_INS = ['x', 'c', 'ctx', 'c_ctx', 'norm_g', 'w_ada', 'b_ada', 'ffn_w1', 'ffn_w3', 'ffn_w2', 'w_in', 'pool_w',
        'pool_scale', 's5_a_re', 's5_a_im', 's5_log_dt', 's5_b_re', 's5_b_im', 's5_c_re', 's5_c_im', 's5_d',
        's5_w_glu', 'w_out', 'final_g']


def kernel(**inputs):
    import numpy as _np
    import concourse.bacc as _bacc
    from concourse import mybir as _mybir
    from concourse.bass_utils import run_bass_kernel_spmd as _run

    nc = _bacc.Bacc("TRN2", target_bir_lowering=False, num_devices=1)
    arrays, args = {}, []
    for name in _INS:
        a = _np.ascontiguousarray(inputs[name])
        arrays[f"in_{name}_dram"] = a
        args.append(nc.dram_tensor(f"in_{name}_dram", a.shape, _mybir.dt.from_np(a.dtype), kind="ExternalInput").ap())
    args.append(nc.dram_tensor("out_0_dram", (1, SEQ, D), _mybir.dt.float32, kind="ExternalOutput").ap())
    hybrid_layer(nc, *args)
    r = _run(nc, [arrays], core_ids=[0])
    return r.results[0]["out_0_dram"]
```

```python
from contextlib import ExitStack

import numpy as np
import concourse.bass as bass
from concourse import mybir

P = 128
F32 = mybir.dt.float32
F32R = mybir.dt.float32r
I32 = mybir.dt.int32
ALU = mybir.AluOpType
ACT = mybir.ActivationFunctionType
KB = 1024

D = 1024
DK = D // P
SEQ, CTX = 1024, 256
FF = 2816
NF = FF // P
NR = 2
FR = NF // NR
TB = 512
HALF = 512
GW = 64
GR = SEQ // GW
WINDOWS = (2, 4, 8, 16)
G, ST, GC = 32, 64, 16
T = 8
SCAN_STEPS = 8
V_POOL = 5
KL, KC = SEQ // T, CTX // T
EPS = 1e-6
S5_LOADS = 13

MAGIC = 12582912.0
LOG2E = 1.4426950408889634
LN2 = (0.693359375, -2.12194440e-4)
INV2PI = 0.15915494309189535
TWO_PI = (6.28125, 0.0019350051879882812, 3.0199159819e-7)
PI_IN = 3.1415925


def hybrid_layer(nc, x, c, ctx_tok, c_ctx, norm_g, w_ada, b_ada, ffn_w1, ffn_w3, ffn_w2, w_in,
                 pool_w, pool_scale, s5_a_re, s5_a_im, s5_log_dt, s5_b_re, s5_b_im,
                 s5_c_re, s5_c_im, s5_d, s5_w_glu, w_out, final_g, out):
    base = (nc._sbuf_addr_for_side("left") + 31) // 32 * 32

    def at(name, shape, kb, dt=F32):
        return nc.alloc_sbuf_tensor_at(name, shape, dt, offset=base + int(kb * KB))

    xl = at("xl", [P, T, D], 0)
    gate = at("gate", [P, 2, D], 32)
    ident = at("ident", [P, P], 40)
    ones = at("ones", [P, P], 40.5)
    vcol = at("vcol", [P, 116], 41)
    scol = at("scol", [P, 2, DK], 41.46875)
    gcol = at("gcol", [P, 5, DK], 41.53125)
    bcol = at("bcol", [P, 5, DK], 41.6875)
    ssq = at("ssq", [P, 4], 41.84375)
    rs = at("rs", [P, 6, 4], 41.875)
    gb = at("gb", [P, 3, DK], 207.75)
    xc = at("xc", [P, 2, D], 42)
    h_hi = at("h_hi", [P, DK, TB], 50, F32R)
    h_lo = at("h_lo", [P, DK, TB], 66, F32R)
    a_hi = at("a_hi", [P, FR, TB], 82, F32R)
    a_lo = at("a_lo", [P, FR, TB], 104, F32R)
    up_raw = at("up_raw", [P, 4, DK, P], 126)
    up_hi = at("up_hi", [P, 2, DK, P], 142, F32R)
    up_lo = at("up_lo", [P, 2, DK, P], 150, F32R)
    dn_raw = at("dn_raw", [P, 4, HALF], 158)
    dn_hi = at("dn_hi", [P, 2, HALF], 166, F32R)
    dn_lo = at("dn_lo", [P, 2, HALF], 170, F32R)
    xn = at("xn", [P, 4, D], 174)
    h32 = at("h32", [P, 2, TB], 190)
    sg = at("sg", [P, 2, TB], 194)
    a32 = at("a32", [P, 2, TB], 198)
    evt = at("evt", [P, 2, HALF], 202)
    h32f = at("fgrow", [P, D], 50)[:, :]
    adx = at("adx", [P, 2, DK, 256], 174)
    acc = at("acc", [P, 2, 2, 256], 190)
    ada = at("ada", [P, 2, DK, 512], 50)
    inv_r = at("inv_r", [P, 4, GR], 206)
    inv_c = at("inv_c", [P, 4, GW], 206.25)
    abar = at("abar", [P, 2, 2, 2, 16], 207.25)
    bn = at("bn", [P, 2, G, GC], 102)
    cn = at("cn", [P, 2, G, GC], 106)
    bb = at("bb", [P, 2, G, GC], 110)
    craw = at("craw", [P, 2, 4, P], 114)
    bf = at("bf", [P, 2, G, GC], 102)
    bk = at("bk", [P, 2, G, GC], 114)
    t1 = at("t1", [P, 2, G, GC], 118)
    t3 = at("t3", [P, 2, G, GC], 82)
    vn = at("vn", [P, 2, G, T, GC], 122)
    vts = at("vts", [P, 16, 2, P], 154)
    wn = at("wn", [P, 2, G, T, GC], 0)
    kp = at("kp", [GC, 16, 15, GC], 170)
    dm = at("dm", [GC, G, GC], 186)
    sm = at("sm", [G, 16, P], 188)
    pw = at("pw", [P, 9, 2, G], 196)
    pwv = at("pwv", [P, T, 2, G], 199)
    pww = at("pww", [P, T, 2, G], 201)
    q4t = at("q4t", [P, 4, G], 203)
    smi = at("smi", [G, P], 203.5, I32)
    vecrow = at("vecrow", [116, P], 204)
    dt2 = at("dt2", [G, 8, 2], 204.5)
    dt2i = at("dt2i", [G, 2], 204.75, I32)
    pt = at("pt", [P, 2, 4, G], 205)
    vp = at("vp", [P, 5, SEQ], 82)
    hs = at("hs", [P, 4, CTX + SEQ], 102)
    Uc = at("Uc", [P, G, KC], 122)
    U = at("U", [P, G, KL], 158)
    vt = at("vt", [P, 2, G, P], 174)
    S = at("S", [P, KL, 2, 2, 16], 126)
    Sc = at("Sc", [P, KC, 2, 2, 16], 42)
    scn = at("scn", [P, 2, 3, 2, 16], 118)
    pws = at("pws", [P, 4, P], 120)
    M = at("M", [P, G, P], 50)
    wy = [at("wy_re", [P, G, P], 102), at("wy_im", [P, G, P], 66)]
    Hk = at("Hk", [P, 2, G, KL], 174)
    bxa = at("bxa", [P, 23 * GW], 102)
    bxb = at("bxb", [P, 23 * GW], 108)
    y = at("y", [P, T, G * GC], 126)
    yg = at("yg", [P, 4, SEQ], 142)
    wglu = at("wglu", [P, 4, 512], 42)
    mp_hi = at("mp_hi", [P, 4, TB], 102, F32R)
    mp_lo = at("mp_lo", [P, 4, TB], 110, F32R)
    ms_hi = at("ms_hi", [P, 4, TB], 82, F32R)
    ms_lo = at("ms_lo", [P, 4, TB], 90, F32R)

    v_dram = nc.dram_tensor("v_dram", [P, 2, G, P], F32, kind="Internal").ap()
    w_dram = nc.dram_tensor("w_dram", [2, P, G, P], F32, kind="Internal").ap()
    k_dram = nc.dram_tensor("k_dram", [GC, G, 15 * GC], F32, kind="Internal").ap()
    u_dram = nc.dram_tensor("u_dram", [4, P, CTX + SEQ], F32, kind="Internal").ap()

    xl_d = x.rearrange("o (k t) c -> k (o t) c", t=T)
    xc_d = ctx_tok.rearrange("o (q i) c -> q (o i) c", i=2)
    out_d = out.rearrange("o (k t) c -> k (o t) c", t=T)
    ada_d = w_ada[0].rearrange("(k p) n -> p k n", p=P)
    w1_d = ffn_w1[0].rearrange("l (k p) f -> l p k f", p=P)
    w3_d = ffn_w3[0].rearrange("l (k p) f -> l p k f", p=P)
    win_d = w_in[0].rearrange("(k p) f -> p k f", p=P)

    up_src, dn_src = [], []
    BLOCKS = [dict(ffn=0, ctx=True, t0=0, gate=0), dict(ffn=0, ctx=False, t0=0, gate=1),
              dict(ffn=0, ctx=False, t0=4, gate=1), dict(ffn=1, ctx=False, t0=0, gate=1),
              dict(ffn=1, ctx=False, t0=4, gate=1)]

    def add_ffn(b):
        b["up0"], b["dn0"] = len(up_src), len(dn_src)
        l = b["ffn"]
        for r in range(NR):
            for f in range(FR):
                fs = slice((r * FR + f) * P, (r * FR + f + 1) * P)
                up_src.append(w1_d[l][:, :, fs])
                up_src.append(w3_d[l][:, :, fs])
            for h in range(2):
                for k in range(FR):
                    row = (r * FR + k) * P
                    dn_src.append(ffn_w2[0, l, row:row + P, h * HALF:(h + 1) * HALF])

    for b in BLOCKS[:3]:
        add_ffn(b)
    PROJ = [dict(ctx=False, t0=0, tiles=range(8)), dict(ctx=True, t0=0, tiles=range(4, 8)),
            dict(ctx=False, t0=4, tiles=range(8))]
    for pr in PROJ:
        pr["up0"] = len(up_src)
        for m in pr["tiles"]:
            up_src.append(win_d[:, :, m * P:(m + 1) * P])
    MIX = [dict(ctx=False, t0=0), dict(ctx=False, t0=4)]
    for mx in MIX:
        mx["dn0"] = len(dn_src)
        for h in range(2):
            for k in range(DK):
                dn_src.append(w_out[0, k * P:(k + 1) * P, h * HALF:(h + 1) * HALF])
    for b in BLOCKS[3:]:
        add_ffn(b)
    UP_MIX = PROJ[0]["up0"]
    UP_F2 = BLOCKS[3]["up0"]
    DN_MIX = MIX[0]["dn0"]

    for n, b in enumerate(BLOCKS):
        b["F0"] = n * NF
    ev = 0
    for b in BLOCKS[:3]:
        b["ev0"] = ev
        ev += 2 * NR * (2 if b["ctx"] else 4)
    for mx in MIX:
        mx["ev0"] = ev
        ev += 2 * 4
    for b in BLOCKS[3:]:
        b["ev0"] = ev
        ev += 2 * NR * 4
    EV_END = ev

    PREPS = [dict(ctx=True, t0=0, col=0, ev=0), dict(ctx=False, t0=0, col=2, ev=0),
             dict(ctx=False, t0=4, col=2, ev=0),
             dict(ctx=False, t0=0, col=3, ev=BLOCKS[2]["ev0"]),
             dict(ctx=True, t0=0, col=1, ev=BLOCKS[1]["ev0"]),
             dict(ctx=False, t0=4, col=3, ev=MIX[0]["ev0"]),
             dict(ctx=False, t0=0, col=4, ev=MIX[1]["ev0"]),
             dict(ctx=False, t0=4, col=4, ev=BLOCKS[3]["ev0"])]
    tiles0 = 0
    for n, p in enumerate(PREPS):
        p["n"] = n
        p["ads"] = [0, 0, 10, 20, 20, 20, 20, 24][n]
        p["nt"] = 2 if p["ctx"] else 4
        p["q0"] = tiles0
        tiles0 += p["nt"]
    Q_FINAL = tiles0

    AD = {0: [], 1: list(range(0, 10)), 2: list(range(10, 20)), 3: list(range(20, 24)), 4: []}
    AD_COLS, AD_GATE_MIX, AD_COLS2, AD_ALL = 8, 12, 20, 24
    for n, b in enumerate(BLOCKS):
        b["ad"] = AD[n]
        b["prev_nt"] = [0, 2, 4, 4, 4][n]

    def bank_set(r, hh):
        return 1 - r if hh == 0 else r

    gs, m32 = sg, a32
    SCAN_END = 6 * (KC - 1 + KL)

    def mix_tile(tb, j, lo):
        if tb == 0:
            return (h_lo if lo else h_hi)[:, j, :]
        if j < 4:
            return (mp_lo if lo else mp_hi)[:, j, :]
        return (ms_lo if lo else ms_hi)[:, j - 4, :]

    def xt(st, t):
        return xc[:, t, :] if st["ctx"] else xl[:, st["t0"] + t, :]

    with ExitStack() as ctx:
        def sem(name):
            return ctx.enter_context(nc.semaphore(name))

        ps = ctx.enter_context(nc.psum_tensor("ps", [P, 8, 512], F32))

        vec_ld, xc_ld, xl_ld, s5_ld, fg_ld = (sem(n) for n in ("vec_ld", "xc_ld", "xl_ld", "s5_ld", "fg_ld"))
        ada_ld = [sem(f"ada_ld{i}") for i in range(2)]
        ad_ld = [sem(f"ad_ld{i}") for i in range(2)]
        up_ld = [sem(f"up_ld{i}") for i in range(4)]
        dn_ld = [sem(f"dn_ld{i}") for i in range(4)]
        const_ok, vec_t, vec_ok, sil_ok = (sem(n) for n in ("const_ok", "vec_t", "vec_ok", "sil_ok"))
        dve_step, pool_step = sem("dve_step"), sem("pool_step")
        ang_ok, sin_ok, q4_ok, q4_t, q4_ev, ct_t, ct_ev = (
            sem(n) for n in ("ang_ok", "sin_ok", "q4_ok", "q4_t", "q4_ev", "ct_t", "ct_ev"))
        gb_ok, mod_t, mod_ev = sem("gb_ok"), sem("mod_t"), sem("mod_ev")
        ad_acc, ad_t, ad_ev = sem("ad_acc"), sem("ad_t"), sem("ad_ev")
        pw_ok, vp_v_ok, vd_ok, w_ok, bf_ok, vt_t, vt_ev, kt_t, kt_ev = (
            sem(n) for n in ("pw_ok", "vp_v_ok", "vd_ok", "w_ok", "bf_ok", "vt_t", "vt_ev", "kt_t", "kt_ev"))
        v_st, w_st, k_st, setup_ok = sem("v_st"), sem("w_st"), sem("k_st"), sem("setup_ok")
        sq_ok, rstd_ok, xn_ok, ht_ok, hhi_ok, h32_ok, hlo_ok = (
            sem(n) for n in ("sq_ok", "rstd_ok", "xn_ok", "ht_ok", "hhi_ok", "h32_ok", "hlo_ok"))
        up_hi_ok, up_lo_ok, up_used = sem("up_hi_ok"), sem("up_lo_ok"), sem("up_used")
        dn_hi_ok, dn_lo_ok, dn_used = sem("dn_hi_ok"), sem("dn_lo_ok"), sem("dn_used")
        silu_ok, prod_ok, ahi_ok, alo_ok = sem("silu_ok"), sem("prod_ok"), sem("ahi_ok"), sem("alo_ok")
        gated, added = sem("gated"), sem("added")
        pj_ev = sem("pj_ev")
        u_st = [sem(f"u_st{i}") for i in range(3)]
        u_ld, uc_ld, vt_ld, m_ld, w_ld, glu_ld, pws_ld = (
            sem(n) for n in ("u_ld", "uc_ld", "vt_ld", "m_ld", "w_ld", "glu_ld", "pws_ld"))
        sc_t, sc_ev, sl_t, sl_ev = (sem(n) for n in ("sc_t", "sc_ev", "sl_t", "sl_ev"))
        scan_step, hk_a, hk_d = sem("scan_step"), sem("hk_a"), sem("hk_d")
        y_t, y_ev, yt_t, yg_ok = (sem(n) for n in ("y_t", "y_ev", "yt_t", "yg_ok"))
        pool_ok, pm_t, z_t, gs_ok, m32_ok, mhi_ok, mlo_ok = (
            sem(n) for n in ("pool_ok", "pm_t", "z_t", "gs_ok", "m32_ok", "mhi_ok", "mlo_ok"))
        fin_ok, out_st = sem("fin_ok"), sem("out_st")

        block = ctx.enter_context(nc.Block())

        @block.sync
        def _(sp):
            ld = sp.dma_start
            ld(vecrow[0:8, :], c.rearrange("o (k p) -> (o k) p", p=P)).then_inc(vec_ld, 16)
            ld(vecrow[8:16, :], c_ctx.rearrange("(k p) -> k p", p=P)).then_inc(vec_ld, 16)
            ld(vecrow[16:40, :], norm_g[0].rearrange("l (k p) -> (l k) p", p=P)).then_inc(vec_ld, 16)
            ld(vecrow[40:44, :], pool_scale[0].rearrange("(k p) -> k p", p=P)).then_inc(vec_ld, 16)
            ld(vecrow[44:116, :], b_ada[0].rearrange("(k p) -> k p", p=P)).then_inc(vec_ld, 16)
            ld(sm[:, 0, :].rearrange("g (d p) -> g d p", d=2), s5_a_re[0].rearrange("d g p -> g d p")).then_inc(s5_ld, 16)
            ld(sm[:, 1, :].rearrange("g (d p) -> g d p", d=2), s5_a_im[0].rearrange("d g p -> g d p")).then_inc(s5_ld, 16)
            for d in range(2):
                ld(dt2[:, 0, d:d + 1], s5_log_dt[0, d].rearrange("(g o) -> g o", o=1)).then_inc(s5_ld, 16)
                for i, src in enumerate((s5_b_re, s5_b_im)):
                    ld(bn[d * ST:(d + 1) * ST, i, :, :], src[0].rearrange("g p c -> p g c")).then_inc(s5_ld, 16)
                for i, src in enumerate((s5_c_re, s5_c_im)):
                    ld(craw[:, i, :, d * ST:(d + 1) * ST],
                       src[0, d].rearrange("(i g) c p -> (g c) i p", g=8)).then_inc(s5_ld, 16)
            ld(dm[:, :, :].rearrange("p g c -> p (g c)"), s5_d[0:1, :].broadcast_to([GC, G * GC])).then_inc(s5_ld, 16)
            ld(xc[:, :, :], xc_d).then_inc(xc_ld, 16)
            for q in range(6):
                if q >= 2:
                    sp.wait_ge(mod_t, q - 1)
                ld(ada[:, q % 2, :, :], ada_d[:, :, q * 512:(q + 1) * 512]).then_inc(ada_ld[q % 2], 16)

            def load_up(n):
                if n >= 4:
                    sp.wait_ge(up_lo_ok, n - 3)
                ld(up_raw[:, n % 4, :, :], up_src[n]).then_inc(up_ld[n % 4], 16)

            def load_dn(n):
                if n >= 4:
                    sp.wait_ge(dn_lo_ok, n - 3)
                ld(dn_raw[:, n % 4, :], dn_src[n]).then_inc(dn_ld[n % 4], 16)

            def load_ffn(b, transposed):
                for r in range(NR):
                    for u in range(2 * FR):
                        load_up(b["up0"] + r * 2 * FR + u)
                        if r == 0 and u % 2 == 1 and u // 2 < len(b["ad"]):
                            n = b["ad"][u // 2]
                            if u == 1:
                                sp.wait_ge(ht_ok, transposed)
                                sp.wait_ge(hlo_ok, transposed)
                            if n >= 2:
                                sp.wait_ge(ad_acc, n - 1)
                            ld(adx[:, n % 2, :, :], ada_d[:, :, 3 * D + n * 256:3 * D + (n + 1) * 256]).then_inc(ad_ld[n % 2], 16)
                    for u in range(2 * FR):
                        load_dn(b["dn0"] + r * 2 * FR + u)

            sp.wait_ge(w_st, 32)
            sp.wait_ge(kt_t, 32)
            ld(xl[:, :, :], xl_d).then_inc(xl_ld, 16)
            sp.wait_ge(setup_ok, 1)
            load_ffn(BLOCKS[0], 8)
            load_ffn(BLOCKS[1], 16)
            load_ffn(BLOCKS[2], 24)
            for n in range(UP_MIX, UP_F2 - 4):
                load_up(n)
            uc = u_dram[:, :, 0:CTX].rearrange("c (g i) (s k) -> s i (c g) k", i=GC, s=T)
            ul = u_dram[:, :, CTX:].rearrange("c (g i) (s k) -> s i (c g) k", i=GC, s=T)

            def store_u(i, n0, n1):
                ld(u_dram[:, :, n0:n1].rearrange("c p n -> p c n"), hs[:, :, n0:n1]).then_inc(u_st[i], 16)
            sp.wait_ge(pj_ev, 8)
            store_u(0, CTX, CTX + TB)
            sp.wait_ge(pj_ev, 12)
            store_u(1, 0, CTX)
            sp.wait_ge(u_st[0], 16)
            sp.wait_ge(dn_used, DN_MIX)
            for s in range(4):
                ld(U[s * GC:(s + 1) * GC, :, :], ul[s]).then_inc(u_ld, 16)
            sp.wait_ge(u_st[1], 16)
            for s in range(T):
                ld(Uc[s * GC:(s + 1) * GC, :, :], uc[s]).then_inc(uc_ld, 16)
            for n in range(UP_F2 - 4, UP_F2):
                load_up(n)
            sp.wait_ge(hlo_ok, 8 * 6)
            sp.wait_ge(added, MIX[0]["ev0"])
            ld(vt[:, :, :, :], v_dram).then_inc(vt_ld, 16)
            sp.wait_ge(pj_ev, 20)
            store_u(2, CTX + TB, CTX + 2 * TB)
            sp.wait_ge(u_st[2], 16)
            for s in range(4, T):
                ld(U[s * GC:(s + 1) * GC, :, :], ul[s]).then_inc(u_ld, 16)
            ld(pws[:, :, :], pool_w[0].rearrange("k c d -> c k d")).then_inc(pws_ld, 16)
            sp.wait_ge(up_used, UP_F2)
            for s in range(T):
                ld(M[s * GC:(s + 1) * GC, :, :], k_dram[:, :, (7 - s) * GC:(15 - s) * GC]).then_inc(m_ld, 16)
            ld(wy[1][:, :, :], w_dram[1]).then_inc(w_ld, 16)
            sp.wait_ge(pool_ok, 4)
            ld(wy[0][:, :, :], w_dram[0]).then_inc(w_ld, 16)
            sp.wait_ge(hk_a, 2)
            sp.wait_ge(hk_d, 2)
            ld(wglu[:, :, :], s5_w_glu[0].rearrange("(k p) n -> p k n", p=P)).then_inc(glu_ld, 16)
            sp.wait_ge(y_t, 8)
            for mx in MIX:
                for u in range(16):
                    load_dn(mx["dn0"] + u)
            sp.wait_ge(m32_ok, 16)
            load_ffn(BLOCKS[3], 56)
            sp.wait_ge(gated, BLOCKS[3]["ev0"])
            ld(gate[:, 0, :], final_g.rearrange("(o n) -> o n", o=1).broadcast_to([P, D])).then_inc(fg_ld, 16)
            load_ffn(BLOCKS[4], 0)
            for t in range(T):
                sp.wait_ge(fin_ok, t + 1)
                ld(out_d[:, t, :], xl[:, t, :]).then_inc(out_st, 16)
            sp.wait_ge(out_st, 16 * T)

        @block.gpsimd
        def _(pool):
            gp = nc.gpsimd
            count = [0]

            def step(ins):
                count[0] += 1
                ins.then_inc(pool_step, 1)
                pool.wait_ge(pool_step, count[0])

            step(gp.memset(ident[:, :], 0.0))
            step(gp.affine_select(out=ident[:, :], in_=ident[:, :], compare_op=ALU.not_equal, fill=1.0,
                                  base=0, pattern=[[-1, P]], channel_multiplier=1))
            gp.memset(ones[:, :], 1.0).then_inc(const_ok, 1)
            for i, w in enumerate(WINDOWS):
                lo, hi = w // 2, w - 1 - w // 2
                for tab, n in ((inv_r, GR), (inv_c, GW)):
                    if n > lo + hi:
                        gp.memset(tab[:, i, lo:n - hi], 1.0 / w)
                    for t in list(range(min(lo, n))) + list(range(max(lo, n - hi), n)):
                        gp.memset(tab[:, i, t:t + 1], 1.0 / (min(t + hi + 1, n) - max(t - lo, 0)))
            pool.wait_ge(s5_ld, 16 * S5_LOADS)
            step(gp.affine_select(out=dm[:, :, :], in_=dm[:, :, :], compare_op=ALU.is_equal, fill=0.0,
                                  base=0, pattern=[[0, G], [-1, GC]], channel_multiplier=1))
            pool.wait_ge(q4_ev, 1)

            def cmul(outr, outi, ar, ai, br, bi, ta, tb, neg=False):
                step(gp.tensor_tensor(ta, ar, br, ALU.mult))
                step(gp.tensor_tensor(tb, ai, bi, ALU.mult))
                step(gp.tensor_tensor(outr, ta, tb, ALU.add if neg else ALU.subtract))
                step(gp.tensor_tensor(ta, ar, bi, ALU.mult))
                step(gp.tensor_tensor(tb, ai, br, ALU.mult))
                step(gp.tensor_tensor(outi, ta, tb, ALU.subtract if neg else ALU.add))

            step(gp.memset(pw[:, 0, 0, :], 1.0))
            step(gp.memset(pw[:, 0, 1, :], 0.0))
            step(gp.tensor_copy(pw[:, 1, :, :], q4t[:, 0:2, :]))
            for n in (1, 2, 4):
                def b(i):
                    return pw[:, n, i, :].unsqueeze(1).broadcast_to([P, n, G])
                cmul(pw[:, n + 1:2 * n + 1, 0, :], pw[:, n + 1:2 * n + 1, 1, :],
                     pw[:, 1:n + 1, 0, :], pw[:, 1:n + 1, 1, :], b(0), b(1), pt[:, 0, 0:n, :], pt[:, 1, 0:n, :])
            step(gp.tensor_copy(pww[0:ST, :, :, :], pw[0:ST, 1:9, :, :]))
            step(gp.tensor_copy(pww[ST:P, ::-1, :, :], pw[ST:P, 1:9, :, :]))
            step(gp.tensor_copy(pwv[0:ST, ::-1, :, :], pw[0:ST, 0:8, :, :]))
            step(gp.tensor_copy(pwv[ST:P, :, :, :], pw[ST:P, 0:8, :, :]))

            def over_c(a):
                return a.unsqueeze(2).broadcast_to([P, G, GC])
            ta, tb = t1[:, 0], t1[:, 1]
            cmul(bb[:, 0], bb[:, 1], over_c(q4t[:, 2, :]), over_c(q4t[:, 3, :]), bn[:, 0], bn[:, 1], ta, tb)
            gp.tensor_copy(pt[:, 0, 0, 0:1], pw[:, 0, 0, 0:1]).then_inc(pw_ok, 1)
            for s in range(V_POOL):
                cmul(vn[:, 0, :, s, :], vn[:, 1, :, s, :], over_c(pwv[:, s, 0, :]), over_c(pwv[:, s, 1, :]),
                     bb[:, 0], bb[:, 1], ta, tb)
            gp.tensor_copy(pt[:, 0, 1, 0:1], pw[:, 0, 0, 0:1]).then_inc(vp_v_ok, 1)
            pool.wait_ge(ct_ev, 2)
            step(gp.tensor_copy(bf[0:ST], bb[0:ST]))
            step(gp.memset(bf[ST:P], 0.0))
            step(gp.tensor_copy(bk[ST:P], bb[ST:P]))
            step(gp.memset(bk[0:ST], 0.0))
            a8 = pw[:, 8, :, :].rearrange("p a (h g) -> p a h g", h=2)
            for i in range(2):
                step(gp.tensor_copy(abar[:, :, 0, i, :], a8[:, 0]))
            step(gp.tensor_copy(abar[:, :, 1, 0, :], a8[:, 1]))
            gp.tensor_scalar(abar[:, :, 1, 1, :], a8[:, 1], -1.0, None, ALU.mult).then_inc(bf_ok, 1)
            pool.wait_ge(w_ok, 1)
            for i in range(2):
                pool.dma_start(w_dram[i], wn[:, i].rearrange("p g t c -> p g (t c)")).then_inc(w_st, 16)
            for gh in range(2):
                gs_ = slice(gh * 16, gh * 16 + 16)
                pool.wait_ge(vt_ev, 8 * (gh + 1))
                for i in range(2):
                    pool.dma_start(v_dram[:, i, gs_, :], vts[:, :, i, :]).then_inc(v_st, 16)
                pool.wait_ge(kt_ev, 16 * (gh + 1))
                step(gp.tensor_tensor(kp[:, :, 7, :], kp[:, :, 7, :], dm[:, gs_, :], ALU.add))
                pool.dma_start(k_dram[:, gs_, :], kp[:, :, :, :].rearrange("p g n c -> p g (n c)")).then_inc(k_st, 16)
            pool.wait_ge(v_st, 64)
            pool.wait_ge(w_st, 32)
            pool.wait_ge(k_st, 32)
            gp.tensor_copy(pt[:, 0, 0, 1:2], pw[:, 0, 0, 0:1]).then_inc(setup_ok, 1)

            def add_tiles(st, nt, halves):
                for hh in range(halves):
                    for t in range(nt):
                        e = st["ev0"] + hh * nt + t
                        pool.wait_ge(gated, e + 1)
                        dst = xt(st, t)[:, (hh % 2) * HALF:(hh % 2 + 1) * HALF]
                        gp.tensor_tensor(dst, dst, evt[:, e % 2, :], ALU.add).then_inc(added, 1)

            for b in BLOCKS[:3]:
                add_tiles(b, 2 if b["ctx"] else 4, 2 * NR)
            pool.wait_ge(pj_ev, 20)
            for i in range(3):
                pool.wait_ge(u_st[i], 16)
            for i, w in enumerate(WINDOWS):
                hi = w // 2 - 1
                v = vp[:, i + 1, :].rearrange("p (r c) -> p r c", c=GW)
                cur, nxt = bxa, bxb

                def rows(buf):
                    return buf[:, 0:(GR + hi) * GW].rearrange("p (r c) -> p r c", c=GW)

                def cols(buf):
                    return buf[:, 0:GR * (GW + hi)].rearrange("p (r c) -> p r c", c=GW + hi)
                o = rows(cur)
                step(gp.tensor_tensor(o[:, 1:GR, :], v[:, 1:, :], v[:, 0:GR - 1, :], ALU.add))
                step(gp.tensor_copy(o[:, 0:1, :], v[:, 0:1, :]))
                if hi:
                    step(gp.tensor_copy(o[:, GR:GR + 1, :], v[:, GR - 1:GR, :]))
                if hi > 1:
                    step(gp.memset(o[:, GR + 1:, :], 0.0))
                m = 2
                while m < w:
                    a, o = rows(cur), rows(nxt)
                    step(gp.tensor_tensor(o[:, m:, :], a[:, m:, :], a[:, 0:GR + hi - m, :], ALU.add))
                    step(gp.tensor_copy(o[:, 0:m, :], a[:, 0:m, :]))
                    cur, nxt = nxt, cur
                    m *= 2
                step(gp.tensor_tensor(cols(nxt)[:, :, 0:GW], rows(cur)[:, hi:, :],
                                      inv_r[:, i, :].unsqueeze(2).broadcast_to([P, GR, GW]), ALU.mult))
                cur, nxt = nxt, cur
                if hi:
                    step(gp.memset(cols(cur)[:, :, GW:], 0.0))
                m = 1
                while m < w:
                    a, o = cols(cur), cols(nxt)
                    step(gp.tensor_tensor(o[:, :, m:], a[:, :, m:], a[:, :, 0:GW + hi - m], ALU.add))
                    step(gp.tensor_copy(o[:, :, 0:m], a[:, :, 0:m]))
                    cur, nxt = nxt, cur
                    m *= 2
                pooled = nxt[:, 0:SEQ].rearrange("p (r c) -> p r c", c=GW)
                step(gp.tensor_tensor(pooled, cols(cur)[:, :, hi:],
                                      inv_c[:, i, :].unsqueeze(1).broadcast_to([P, GR, GW]), ALU.mult))
                gp.tensor_tensor(vp[:, i, :].rearrange("p (s k) -> p k s", s=T), nxt[:, 0:SEQ].rearrange("p (k s) -> p k s", s=T),
                                 vp[:, i + 1, :].rearrange("p (k s) -> p k s", s=T), ALU.subtract).then_inc(pool_ok, 1)
                pool.wait_ge(pool_ok, i + 1)
            for mx in MIX:
                add_tiles(mx, 4, 2)
            for b in BLOCKS[3:]:
                add_tiles(b, 4, 2 * NR)

        @block.scalar
        def _(act):
            sa = nc.scalar.activation
            def modulation(q):
                m, h = q // 2, q % 2
                act.wait_ge(mod_t, q + 1)
                if m == 1:
                    act.wait_ge(gb_ok, 1)
                for cond in range(2):
                    if m == 2:
                        ins = sa(gate[:, 1 - cond, h * 512:(h + 1) * 512], ps[:, 4 + 2 * (q % 2) + cond, :], ACT.Copy, scale=0.5)
                    else:
                        for j in range(4):
                            k = 4 * h + j
                            src = ps[:, 4 + 2 * (q % 2), 2 * j + cond:2 * j + cond + 1]
                            ins = mod_column(src, m, 2 * (1 - cond), k)
                ins.then_inc(mod_ev, 1)

            def mod_column(src, m, col, k):
                if m % 3 == 0:
                    return sa(bcol[:, col, k:k + 1], src, ACT.Identity, bias=vcol[:, 44 + 8 * m + k:45 + 8 * m + k])
                n = m // 3
                return sa(gcol[:, col, k:k + 1], src, ACT.Identity, scale=vcol[:, 16 + 8 * n + k:17 + 8 * n + k],
                          bias=gb[:, n, k:k + 1])

            def ad_evict(n):
                m, part = 3 + n // 4, n % 4
                act.wait_ge(ad_t, n + 1)
                if m == 5 and part == 0:
                    act.wait_ge(gated, BLOCKS[1]["ev0"])
                if m == 8 and part == 0:
                    act.wait_ge(gated, MIX[0]["ev0"])
                for cond in range(2 if m < 5 else 1):
                    src = ps[:, 4 + 2 * (n % 2) + cond, :]
                    if m % 3 == 2:
                        ins = sa(gate[:, m // 8, part * 256:(part + 1) * 256], src[:, 0:256], ACT.Copy, scale=0.5 if m == 8 else 1.0)
                    else:
                        for j in range(2):
                            ins = mod_column(src[:, j:j + 1], m, m // 3 + (2 if cond == 0 else 0), 2 * part + j)
                ins.then_inc(ad_ev, 1)

            def v_evict(gh):
                for i in range(8):
                    act.wait_ge(vt_t, gh * 8 + i + 1)
                    if gh and i == 0:
                        act.wait_ge(v_st, 32)
                    sa(vts[:, 2 * i:2 * i + 2, :, :].rearrange("p g a n -> p (g a n)"), ps[:, i % 2, :], ACT.Copy).then_inc(vt_ev, 1)

            def k_evict(gh):
                for i in range(16):
                    act.wait_ge(kt_t, gh * 16 + i + 1)
                    if gh and i == 0:
                        act.wait_ge(k_st, 16)
                    sa(kp[:, i, :, :].rearrange("p n c -> p (n c)"), ps[0:GC, 2 + i % 2, 0:15 * GC], ACT.Copy).then_inc(kt_ev, 1)

            act.wait_ge(vec_t, 1)
            sa(vcol[:, :], ps[:, 0, 0:116], ACT.Copy).then_inc(vec_ok, 1)
            act.wait_ge(vec_ok, 1)
            sa(scol[:, :, :].rearrange("p a k -> p (a k)"), vcol[:, 0:16], ACT.Silu).then_inc(sil_ok, 1)
            for i in range(2):
                act.wait_ge(ct_t, i + 1)
                sa(cn[:, i].rearrange("p g c -> p (g c)"), ps[:, 1 + i, :], ACT.Copy, scale=1.0 - 2.0 * i).then_inc(ct_ev, 1)
            modulation(0)
            modulation(1)
            act.wait_ge(ang_ok, 1)
            sa(sm[:, 4, :], sm[:, 3, :], ACT.Sin).then_inc(sin_ok, 1)
            sa(sm[:, 5, :], sm[:, 3, :], ACT.Sin, scale=0.5).then_inc(sin_ok, 1)
            modulation(2)
            modulation(3)
            act.wait_ge(q4_t, 1)
            sa(q4t[:, :, :], ps[:, 3, 0:4 * G].rearrange("p (a g) -> p a g", a=4), ACT.Copy).then_inc(q4_ev, 1)
            for q in range(4, 6):
                modulation(q)
            v_evict(0)
            k_evict(0)
            v_evict(1)
            k_evict(1)

            def conv_up(n):
                act.wait_ge(up_ld[n % 4], 16 * (n // 4 + 1))
                if n >= 2:
                    act.wait_ge(up_used, n - 1)
                sa(up_hi[:, n % 2], up_raw[:, n % 4], ACT.Copy).then_inc(up_hi_ok, 1)

            def conv_dn(n):
                act.wait_ge(dn_ld[n % 4], 16 * (n // 4 + 1))
                if n >= 2:
                    act.wait_ge(dn_used, n - 1)
                sa(dn_hi[:, n % 2], dn_raw[:, n % 4], ACT.Copy).then_inc(dn_hi_ok, 1)

            def squares(p):
                if p["ev"]:
                    act.wait_ge(added, p["ev"])
                if p["n"] == 1:
                    act.wait_ge(xl_ld, 16)
                if p["ads"]:
                    act.wait_ge(ad_acc, p["ads"])
                for t in range(p["nt"]):
                    q = p["q0"] + t
                    if p["n"] >= 1:
                        act.wait_ge(ht_ok, 8 * p["n"])
                        act.wait_ge(rstd_ok, p["n"])
                    sa(xn[:, t, :], xt(p, t), ACT.Square, accum_out=ssq[:, t:t + 1]).then_inc(sq_ok, 1)

            def hi_of_h(p, k0, k1):
                nk = p["nt"] * P
                for k in range(k0, k1):
                    act.wait_ge(h32_ok, 8 * p["n"] + k + 1)
                    sa(h_hi[:, k, 0:nk], h32[:, k % 2, 0:nk], ACT.Copy).then_inc(hhi_ok, 1)

            def ffn(b, prep, look):
                nt = 2 if b["ctx"] else 4
                nk = nt * P
                u, dd, F = b["up0"], b["dn0"], b["F0"]
                for r in range(NR):
                    for f in range(FR):
                        nxt = [("u", u + 2 * f + 2), ("u", u + 2 * f + 3)] if f < FR - 1 else [("d", dd), ("d", dd + 1)]
                        fn = {"u": conv_up, "d": conv_dn}
                        fn[nxt[0][0]](nxt[0][1])
                        act.wait_ge(up_used, u + 2 * f + 1)
                        if F + f >= 2:
                            act.wait_ge(prod_ok, F + f - 1)
                        sa(sg[:, (F + f) % 2, 0:nk], ps[:, 4 * r + 2 * (f % 2), 0:nk], ACT.Silu).then_inc(silu_ok, 1)
                        fn[nxt[1][0]](nxt[1][1])
                        act.wait_ge(prod_ok, F + f + 1)
                        sa(a_hi[:, f, 0:nk], a32[:, (F + f) % 2, 0:nk], ACT.Copy).then_inc(ahi_ok, 1)
                        if r == 1 and prep is not None and f == 4:
                            squares(prep)
                        if r == 1 and prep is None and b is BLOCKS[4] and f == 4:
                            final_squares(0)
                        if r == 0 and 2 <= f < len(b["ad"]) + 2:
                            ad_evict(b["ad"][f - 2])
                    if r == 0 and len(b["ad"]) > FR - 2:
                        ad_evict(b["ad"][FR - 2])
                    for i in range(2 * FR):
                        if i + 2 < 2 * FR:
                            conv_dn(dd + i + 2)
                        elif r == 0:
                            conv_up(u + 2 * FR + i + 2 - 2 * FR)
                        elif look is not None:
                            conv_up(look + i + 2 - 2 * FR)
                        if r == 1 and prep is not None and i in (FR + 3, FR + 7):
                            hi_of_h(prep, *((0, 4) if i == FR + 3 else (4, 8)))
                    u += 2 * FR
                    dd += 2 * FR
                    F += FR

            def final_squares(g4):
                for t in range(4):
                    if g4 == 0:
                        act.wait_ge(added, BLOCKS[4]["ev0"])
                        act.wait_ge(ht_ok, 64)
                        act.wait_ge(rstd_ok, len(PREPS))
                    else:
                        act.wait_ge(added, EV_END - 3 + t)
                        act.wait_ge(rstd_ok, len(PREPS) + 1)
                    sa(xn[:, t, :], xl[:, 4 * g4 + t, :], ACT.Square, accum_out=ssq[:, t:t + 1]).then_inc(sq_ok, 1)

            act.wait_ge(setup_ok, 1)
            act.wait_ge(xc_ld, 16)
            squares(PREPS[0])
            hi_of_h(PREPS[0], 0, 8)
            conv_up(0)
            conv_up(1)
            ffn(BLOCKS[0], PREPS[1], BLOCKS[1]["up0"])
            ffn(BLOCKS[1], PREPS[2], BLOCKS[2]["up0"])
            ffn(BLOCKS[2], PREPS[3], PROJ[0]["up0"])
            for pi, pr in enumerate(PROJ):
                if pi:
                    hi_of_h(PREPS[3 + pi], 0, 8)
                for j in range(len(pr["tiles"])):
                    n = pr["up0"] + j + 2
                    if n < UP_F2:
                        conv_up(n)
                    if j == 1 and pi < 2:
                        squares(PREPS[4 + pi])
            for i in range(4):
                act.wait_ge(sc_t, i + 1)
                cc, gh = i // 2, i % 2
                src = ps[:, i, :].rearrange("p (g k) -> p k g", k=KC)
                sa(Sc[0:ST, :, gh, cc, :], src[0:ST], ACT.Copy)
                sa(Sc[ST:P, ::-1, gh, cc, :], src[ST:P], ACT.Copy).then_inc(sc_ev, 1)
            for i in range(16):
                act.wait_ge(sl_t, i + 1)
                cc, g4 = i % 2, i // 2
                src = ps[:, 4 + i % 4, :].rearrange("p (g k) -> p k g", k=KL)
                gq = 4 * (g4 % 4)
                sa(S[0:ST, :, g4 // 4, cc, gq:gq + 4], src[0:ST], ACT.Copy)
                sa(S[ST:P, ::-1, g4 // 4, cc, gq:gq + 4], src[ST:P], ACT.Copy).then_inc(sl_ev, 1)
            act.wait_ge(scan_step, SCAN_END)
            for gh in range(2):
                hs_ = slice(16 * gh, 16 * gh + 16)
                sa(Hk[0:ST, :, hs_, 0], Sc[0:ST, KC - 1, gh], ACT.Copy)
                for a in range(2):
                    ins = sa(Hk[0:ST, a, hs_, 1:], S[0:ST, 0:KL - 1, gh, a, :].rearrange("p k g -> p g k"), ACT.Copy)
                ins.then_inc(hk_a, 1)
            for i in range(8):
                act.wait_ge(y_t, i + 1)
                if i == 0:
                    act.wait_ge(hk_a, 2)
                    act.wait_ge(hk_d, 2)
                sa(y[:, :, 64 * i:64 * i + 64].rearrange("p t (g c) -> p g t c", c=GC),
                   ps[:, i % 4, :].rearrange("p (g t c) -> p g t c", g=4, c=GC), ACT.Copy).then_inc(y_ev, 1)
            for i in range(8):
                act.wait_ge(yt_t, i + 1)
                cc, tb = i % 4, i // 4
                sa(yg[:, cc, tb * TB:(tb + 1) * TB], ps[:, 4 + i % 4, :], ACT.Gelu_apprx_tanh).then_inc(yg_ok, 1)
            for tb in range(2):
                for j in range(8):
                    n = tb * 8 + j
                    if j >= 4:
                        act.wait_ge(z_t, tb * 4 + j - 3)
                        if n >= 6:
                            act.wait_ge(m32_ok, (n - 2) + 1)
                        sa(gs[:, n % 2, :], ps[:, 4 + j % 4, :], ACT.Sigmoid).then_inc(gs_ok, 1)
                    act.wait_ge(m32_ok, n + 1)
                    sa(mix_tile(tb, j, 0), m32[:, n % 2, :], ACT.Copy).then_inc(mhi_ok, 1)
            d0 = MIX[0]["dn0"]
            conv_dn(d0)
            conv_dn(d0 + 1)
            for i in range(32):
                if i + 2 < 32:
                    conv_dn(d0 + i + 2)
                elif i == 30:
                    conv_up(UP_F2)
                    conv_up(UP_F2 + 1)
                if i == 18:
                    squares(PREPS[6])
                if i == 28:
                    hi_of_h(PREPS[6], 0, 4)
            hi_of_h(PREPS[6], 4, 8)
            ffn(BLOCKS[3], PREPS[7], BLOCKS[4]["up0"])
            ffn(BLOCKS[4], None, None)
            final_squares(1)

        @block.vector
        def _(dve):
            ve = nc.vector
            tt, ts, stt = ve.tensor_tensor, ve.tensor_scalar, ve.scalar_tensor_tensor
            count = [0]

            def step(ins):
                count[0] += 1
                ins.then_inc(dve_step, 1)
                dve.wait_ge(dve_step, count[0])

            def exp(dst, src, k, f, ki):
                step(ts(f, src, -88.0, 89.0, ALU.max, ALU.min))
                step(ts(k, f, LOG2E, MAGIC, ALU.mult, ALU.add))
                step(ts(k, k, -MAGIC, None, ALU.add))
                step(stt(out=f, in0=k, scalar=-LN2[0], in1=f, op0=ALU.mult, op1=ALU.add))
                step(stt(out=f, in0=k, scalar=-LN2[1], in1=f, op0=ALU.mult, op1=ALU.add))
                step(ts(k, k, 127.0, None, ALU.add))
                step(ve.tensor_copy(ki, k))
                step(ts(ki, ki, 23, None, ALU.logical_shift_left))
                step(ts(k, f, 1.0 / 5040, None, ALU.mult))
                for n in (720, 120, 24, 6, 2, 1):
                    step(stt(out=k, in0=k, scalar=1.0 / n, in1=f, op0=ALU.add, op1=ALU.mult))
                step(ts(k, k, 1.0, None, ALU.add))
                step(tt(dst, k, ki.bitcast(F32), ALU.mult))

            dve.wait_ge(vec_ok, 1)
            for n in range(3):
                ins = stt(out=gb[:, n, :], in0=vcol[:, 44 + 8 * (3 * n + 1):44 + 8 * (3 * n + 2)], scalar=1.0,
                          in1=vcol[:, 16 + 8 * n:24 + 8 * n], op0=ALU.add, op1=ALU.mult)
            ins.then_inc(gb_ok, 1)
            dve.wait_ge(s5_ld, 16 * S5_LOADS)
            are, aim = sm[:, 0, :], sm[:, 1, :]
            exp(dt2[:, 1, :], dt2[:, 0, :], dt2[:, 2, :], dt2[:, 3, :], dt2i[:, :])
            for d in range(2):
                half = slice(d * ST, (d + 1) * ST)
                step(ts(sm[:, 2, half], sm[:, 0, half], dt2[:, 1, d:d + 1], None, ALU.mult))
                step(ts(sm[:, 3, half], sm[:, 1, half], dt2[:, 1, d:d + 1], None, ALU.mult))
            th, k_ = sm[:, 3, :], sm[:, 6, :]
            step(ts(k_, th, INV2PI, MAGIC, ALU.mult, ALU.add))
            step(ts(k_, k_, -MAGIC, None, ALU.add))
            for part in TWO_PI:
                step(stt(out=th, in0=k_, scalar=-part, in1=th, op0=ALU.mult, op1=ALU.add))
            step(ts(th, th, -PI_IN, PI_IN, ALU.max, ALU.min))
            ts(th, th, 1.0, None, ALU.mult).then_inc(ang_ok, 1)
            exp(sm[:, 7, :], sm[:, 2, :], sm[:, 6, :], sm[:, 8, :], smi[:, :])
            dve.wait_ge(sin_ok, 2)
            mag, s1, s2 = sm[:, 7, :], sm[:, 4, :], sm[:, 5, :]
            ar, ai, cr, ci = (sm[:, 9 + i, :] for i in range(4))
            step(tt(s2, s2, s2, ALU.mult))
            step(ts(s2, s2, -2.0, 1.0, ALU.mult, ALU.add))
            step(tt(ar, mag, s2, ALU.mult))
            step(tt(ai, mag, s1, ALU.mult))
            nr, den, ta, tb = sm[:, 13, :], sm[:, 14, :], sm[:, 15, :], sm[:, 6, :]
            step(ts(nr, ar, -1.0, None, ALU.add))
            step(tt(den, are, are, ALU.mult))
            step(tt(ta, aim, aim, ALU.mult))
            step(tt(den, den, ta, ALU.add))
            step(ve.reciprocal(den, den))
            step(tt(ta, nr, are, ALU.mult))
            step(tt(tb, ai, aim, ALU.mult))
            step(tt(ta, ta, tb, ALU.add))
            step(tt(cr, ta, den, ALU.mult))
            step(tt(ta, ai, are, ALU.mult))
            step(tt(tb, nr, aim, ALU.mult))
            step(tt(ta, ta, tb, ALU.subtract))
            tt(ci, ta, den, ALU.mult).then_inc(q4_ok, 1)

            def cmul(outr, outi, ar, ai, br, bi, ta, tb, neg=False):
                step(tt(ta, ar, br, ALU.mult))
                step(tt(tb, ai, bi, ALU.mult))
                step(tt(outr, ta, tb, ALU.add if neg else ALU.subtract))
                step(tt(ta, ar, bi, ALU.mult))
                step(tt(tb, ai, br, ALU.mult))
                step(tt(outi, ta, tb, ALU.subtract if neg else ALU.add))

            def over_c(a):
                return a.unsqueeze(2).broadcast_to([P, G, GC])
            dve.wait_ge(pw_ok, 1)
            dve.wait_ge(ct_ev, 2)
            ta, tb = t3[:, 0], t3[:, 1]
            for s in range(V_POOL, T):
                cmul(vn[:, 0, :, s, :], vn[:, 1, :, s, :], over_c(pwv[:, s, 0, :]), over_c(pwv[:, s, 1, :]),
                     bb[:, 0], bb[:, 1], ta, tb)
            ve.tensor_copy(dt2[:, 4, :], dt2[:, 1, :]).then_inc(vd_ok, 1)
            for t in range(T):
                cmul(wn[:, 0, :, t, :], wn[:, 1, :, t, :], over_c(pww[:, t, 0, :]), over_c(pww[:, t, 1, :]),
                     cn[:, 0], cn[:, 1], ta, tb, neg=True)
            ve.tensor_copy(dt2[:, 5, :], dt2[:, 1, :]).then_inc(w_ok, 1)

            def ad_sum(n, part, parts=4):
                both = 3 + n // 4 < 5
                ops = [(k, cond, cond, k == 0) for k in range(DK) for cond in range(2)] if both else \
                    [(k, 0, k % 2, k < 2) for k in range(DK)]
                if part == 0:
                    dve.wait_ge(ad_ld[n % 2], 16 * (n // 2 + 1))
                    if n >= 2:
                        dve.wait_ge(ad_t, n - 1)
                each = len(ops) // parts
                for i in range(part * each, (part + 1) * each):
                    k, cond, chain, first = ops[i]
                    a, sc = acc[:, n % 2, chain, :], scol[:, cond, k:k + 1]
                    if first:
                        ins = ts(a, adx[:, n % 2, k, :], sc, None, ALU.mult)
                    else:
                        dve.wait_ge(dve_step, count[0] - 1)
                        ins = stt(out=a, in0=adx[:, n % 2, k, :], scalar=sc, in1=a, op0=ALU.mult, op1=ALU.add)
                    ins.then_inc(dve_step, 1)
                    count[0] += 1
                if part == parts - 1:
                    dve.wait_ge(dve_step, count[0])
                    ve.tensor_copy(rs[:, 3, 0:1], ssq[:, 0:1]).then_inc(ad_acc, 1)

            def rstd(n, nt, last):
                v, r, a, b_ = (rs[:, i, 0:nt] for i in range(4))
                ri = rs[:, 4, 0:nt].bitcast(I32)
                dve.wait_ge(sq_ok, last)
                step(ts(v, ssq[:, 0:nt], 1.0 / D, EPS, ALU.mult, ALU.add))
                step(ts(ri, v.bitcast(I32), 1, None, ALU.logical_shift_right))
                step(ve.tensor_copy(a, ri))
                step(ts(a, a, -1.0, float(0x5f3759df), ALU.mult, ALU.add))
                step(ve.tensor_copy(ri, a))
                step(ve.tensor_copy(r, ri.bitcast(F32)))
                for it in range(4):
                    step(tt(a, r, r, ALU.mult))
                    step(tt(a, a, v, ALU.mult))
                    step(ts(a, a, -0.5, 1.5, ALU.mult, ALU.add))
                    if it < 3:
                        step(tt(r, r, a, ALU.mult))
                    else:
                        tt(rs[:, 5, 0:nt], r, a, ALU.mult).then_inc(rstd_ok, 1)
                        dve.wait_ge(rstd_ok, n + 1)

            def normalise(p):
                rstd(p["n"], p["nt"], p["q0"] + p["nt"])
                for t in range(p["nt"]):
                    ts(xn[:, t, :], xt(p, t), rs[:, 5, t:t + 1], None, ALU.mult).then_inc(xn_ok, 1)

            def split_h(p, k0, k1):
                nk = p["nt"] * P
                if k0 == 0 and p["n"] >= 2:
                    dve.wait_ge(ad_t, p["ads"])
                if k0 == 0 and p["n"] >= 3:
                    dve.wait_ge(ad_ev, AD_COLS if p["n"] < 6 else AD_COLS2)

                def low(k):
                    dve.wait_ge(hhi_ok, 8 * p["n"] + k + 1)
                    tt(h_lo[:, k, 0:nk], h32[:, k % 2, 0:nk], h_hi[:, k, 0:nk].bitcast(F32), ALU.subtract).then_inc(hlo_ok, 1)
                for k in range(k0, k1):
                    dve.wait_ge(ht_ok, 8 * p["n"] + k + 1)
                    if 8 * p["n"] + k >= 2:
                        dve.wait_ge(hlo_ok, 8 * p["n"] + k - 1)
                    ts(h32[:, k % 2, 0:nk], ps[:, k % 4, 0:nk], gcol[:, p["col"], k:k + 1], bcol[:, p["col"], k:k + 1],
                       ALU.mult, ALU.add).then_inc(h32_ok, 1)
                    if k > k0:
                        low(k - 1)
                low(k1 - 1)

            def lo_up(n):
                dve.wait_ge(up_hi_ok, n + 1)
                tt(up_lo[:, n % 2], up_raw[:, n % 4], up_hi[:, n % 2].bitcast(F32), ALU.subtract).then_inc(up_lo_ok, 1)

            def lo_dn(n):
                dve.wait_ge(dn_hi_ok, n + 1)
                tt(dn_lo[:, n % 2], dn_raw[:, n % 4], dn_hi[:, n % 2].bitcast(F32), ALU.subtract).then_inc(dn_lo_ok, 1)

            def gated_tile(e, t, g_row, hh, bank):
                if e >= 2:
                    dve.wait_ge(added, e - 1)
                tt(evt[:, e % 2, :], ps[:, bank + t, :], gate[:, g_row, hh * HALF:(hh + 1) * HALF], ALU.mult).then_inc(gated, 1)

            def ffn(b, prep, look):
                nt = 2 if b["ctx"] else 4
                nk = nt * P
                u, dd, F = b["up0"], b["dn0"], b["F0"]
                fn = {"u": lo_up, "d": lo_dn}
                for r in range(NR):
                    for f in range(FR):
                        nxt = [("u", u + 2 * f + 2), ("u", u + 2 * f + 3)] if f < FR - 1 else [("d", dd), ("d", dd + 1)]
                        fn[nxt[0][0]](nxt[0][1])
                        n = F + f
                        ad = b["ad"][f] if r == 0 and f < len(b["ad"]) else None
                        if ad is not None:
                            ad_sum(ad, 0)
                        dve.wait_ge(silu_ok, n + 1)
                        dve.wait_ge(up_used, u + 2 * f + 2)
                        if n >= 2:
                            dve.wait_ge(ahi_ok, n - 1)
                            dve.wait_ge(alo_ok, n - 1)
                        tt(a32[:, n % 2, 0:nk], sg[:, n % 2, 0:nk], ps[:, 4 * r + 2 * (f % 2) + 1, 0:nk], ALU.mult).then_inc(prod_ok, 1)
                        if ad is not None:
                            ad_sum(ad, 1)
                        fn[nxt[1][0]](nxt[1][1])
                        if ad is not None:
                            ad_sum(ad, 2)
                        dve.wait_ge(ahi_ok, n + 1)
                        tt(a_lo[:, f, 0:nk], a32[:, n % 2, 0:nk], a_hi[:, f, 0:nk].bitcast(F32), ALU.subtract).then_inc(alo_ok, 1)
                        if ad is not None:
                            ad_sum(ad, 3)
                        if r == 1 and prep is not None and f == 6:
                            normalise(prep)
                        if r == 1 and prep is None and f == 6:
                            final_scale(0)
                    for i in range(2 * FR):
                        if i in (FR - 1, 2 * FR - 1):
                            hh = i // FR
                            e0 = b["ev0"] + (2 * r + hh) * nt
                            dve.wait_ge(dn_used, dd + i + 1)
                            if b is BLOCKS[3] and r == 0 and hh == 0:
                                dve.wait_ge(ad_ev, AD_ALL)
                            for t in range(nt):
                                gated_tile(e0 + t, t, b["gate"], hh, 4 * bank_set(r, hh))
                                if t == nt // 2 - 1:
                                    if i == FR - 1:
                                        lo_dn(dd + i + 2)
                                    elif r == 0:
                                        lo_up(u + 2 * FR + 1)
                                    elif look is not None:
                                        lo_up(look + 1)
                        elif i + 2 < 2 * FR:
                            lo_dn(dd + i + 2)
                        elif r == 0:
                            lo_up(u + 2 * FR)
                        elif look is not None:
                            lo_up(look)
                        if r == 1 and prep is not None and i in (FR + 3, FR + 7):
                            split_h(prep, *((0, 4) if i == FR + 3 else (4, 8)))
                    u += 2 * FR
                    dd += 2 * FR
                    F += FR

            def final_scale(g4):
                rstd(len(PREPS) + g4, 4, Q_FINAL + 4 * (g4 + 1))
                dve.wait_ge(fg_ld, 16)
                for t in range(4):
                    tl = xl[:, 4 * g4 + t, :]
                    stt(out=tl, in0=tl, scalar=rs[:, 5, t:t + 1], in1=gate[:, 0, :], op0=ALU.mult, op1=ALU.mult).then_inc(fin_ok, 1)

            dve.wait_ge(mod_ev, 4)
            normalise(PREPS[0])
            split_h(PREPS[0], 0, 8)
            lo_up(0)
            lo_up(1)
            ffn(BLOCKS[0], PREPS[1], BLOCKS[1]["up0"])
            ffn(BLOCKS[1], PREPS[2], BLOCKS[2]["up0"])
            ffn(BLOCKS[2], PREPS[3], PROJ[0]["up0"])
            for pi, pr in enumerate(PROJ):
                if pi:
                    split_h(PREPS[3 + pi], 0, 8)
                for j, mt in enumerate(pr["tiles"]):
                    n = pr["up0"] + j
                    if n + 2 < UP_F2:
                        lo_up(n + 2)
                    dve.wait_ge(up_used, n + 1)
                    src = ps[:, 4 + j % 4, :]
                    if pr["ctx"]:
                        ve.tensor_copy(hs[:, mt - 4, 0:CTX].rearrange("p (s i k) -> p s i k", s=4, i=2),
                                       src[:, 0:CTX].rearrange("p (i k s) -> p s i k", s=4, i=2)).then_inc(pj_ev, 1)
                    elif mt >= 4:
                        n0 = CTX + pr["t0"] * P
                        ve.tensor_copy(hs[:, mt - 4, n0:n0 + TB], src).then_inc(pj_ev, 1)
                    else:
                        ve.tensor_copy(vp[:, mt + 1, :].rearrange("p (k s) -> p s k", s=T)[:, pr["t0"]:pr["t0"] + 4, :],
                                       src.rearrange("p (s k) -> p s k", s=4)).then_inc(pj_ev, 1)
                    if j == 2 and pi < 2:
                        normalise(PREPS[4 + pi])

            def scan_chunk(dst, prev, at0):
                n = [at0]

                def go(ins):
                    n[0] += 1
                    ins.then_inc(scan_step, 1)

                def wait():
                    if not (isinstance(n[0], int) and n[0] < 2):
                        dve.wait_ge(scan_step, n[0] - 1)
                for h in range(2):
                    wait()
                    go(tt(scn[:, h, 0:2], abar[:, h], prev[:, h].unsqueeze(1).broadcast_to([P, 2, 2, 16]), ALU.mult))
                for h in range(2):
                    wait()
                    go(tt(scn[:, h, 2], scn[:, h, 0], scn[:, h, 1, ::-1, :], ALU.add))
                for h in range(2):
                    wait()
                    go(tt(dst[:, h], scn[:, h, 2], dst[:, h], ALU.add))

            dve.wait_ge(sc_ev, 4)
            for k in range(1, KC):
                scan_chunk(Sc[:, k], Sc[:, k - 1], 6 * (k - 1))
            dve.wait_ge(sl_ev, 16)
            at0 = 6 * (KC - 1)
            for k in range(SCAN_STEPS):
                scan_chunk(S[:, k], Sc[:, KC - 1] if k == 0 else S[:, k - 1], at0 + 6 * k)
            with dve.Fori(1, KL // SCAN_STEPS) as i:
                for j in range(SCAN_STEPS):
                    k = i * SCAN_STEPS + j
                    scan_chunk(S[:, bass.ds(k, 1)].squeeze(1), S[:, bass.ds(k - 1, 1)].squeeze(1), k * 6 + at0)
            dve.wait_ge(scan_step, SCAN_END)
            for gh in range(2):
                hs_ = slice(16 * gh, 16 * gh + 16)
                ve.tensor_copy(Hk[ST:P, :, hs_, KL - 1], Sc[ST:P, KC - 1, gh])
                for a in range(2):
                    ins = ve.tensor_copy(Hk[ST:P, a, hs_, 0:KL - 1][:, :, ::-1], S[ST:P, 0:KL - 1, gh, a, :].rearrange("p k g -> p g k"))
                ins.then_inc(hk_d, 1)
            dve.wait_ge(y_t, 8)
            dve.wait_ge(ad_ev, AD_GATE_MIX)
            for tb in range(2):
                for j in range(8):
                    n = tb * 8 + j
                    if n >= 2:
                        dve.wait_ge(mhi_ok, n - 1)
                        dve.wait_ge(mlo_ok, n - 1)
                    if j < 4:
                        dve.wait_ge(pm_t, tb * 4 + j + 1)
                        ts(m32[:, n % 2, :], ps[:, j, :], vcol[:, 40 + j:41 + j], None, ALU.mult).then_inc(m32_ok, 1)
                    else:
                        dve.wait_ge(gs_ok, tb * 4 + j - 3)
                        tt(m32[:, n % 2, :], gs[:, n % 2, :], yg[:, j - 4, tb * TB:(tb + 1) * TB], ALU.mult).then_inc(m32_ok, 1)
                    dve.wait_ge(mhi_ok, n + 1)
                    tt(mix_tile(tb, j, 1), m32[:, n % 2, :], mix_tile(tb, j, 0).bitcast(F32), ALU.subtract).then_inc(mlo_ok, 1)
            d0 = MIX[0]["dn0"]
            lo_dn(d0)
            lo_dn(d0 + 1)
            for i in range(32):
                if i % 8 == 7:
                    mx, hh = MIX[i // 16], (i // 8) % 2
                    dve.wait_ge(dn_used, d0 + i + 1)
                    for t in range(4):
                        gated_tile(mx["ev0"] + hh * 4 + t, t, 0, hh, 4 * hh)
                        if t == 1 and i + 2 < 32:
                            lo_dn(d0 + i + 2)
                elif i + 2 < 32:
                    lo_dn(d0 + i + 2)
                elif i == 30:
                    lo_up(UP_F2)
                    lo_up(UP_F2 + 1)
                if i == 20:
                    normalise(PREPS[6])
                if i == 28:
                    split_h(PREPS[6], 0, 4)
            split_h(PREPS[6], 4, 8)
            ffn(BLOCKS[3], PREPS[7], BLOCKS[4]["up0"])
            ffn(BLOCKS[4], None, None)
            final_scale(1)

        @block.tensor
        def _(pe):
            mm = nc.tensor.matmul
            tr = nc.tensor.transpose
            pe.wait_ge(const_ok, 1)
            pe.wait_ge(pool_step, 2)
            pe.wait_ge(vec_ld, 16 * 5)
            tr(ps[:, 0, 0:116], vecrow[:, :], ident[0:116, 0:116]).then_inc(vec_t, 1)
            pe.wait_ge(s5_ld, 16 * S5_LOADS)
            for i in range(2):
                for j in range(4):
                    ins = tr(ps[:, 1 + i, j * P:(j + 1) * P], craw[:, i, j, :], ident[:, :])
                ins.then_inc(ct_t, 1)

            def modulation(q):
                m = q // 2
                pe.wait_ge(ada_ld[q % 2], 16 * (q // 2 + 1))
                if q >= 2:
                    pe.wait_ge(mod_ev, q - 1)
                if m == 2:
                    for cond in range(2):
                        o = ps[:, 4 + 2 * (q % 2) + cond, :]
                        for k in range(DK):
                            mm(o, scol[:, cond, k:k + 1].broadcast_to([P, P]), ada[:, q % 2, k, :], start=k == 0, stop=False)
                        for j in range(4):
                            bc = 44 + 4 * q + j
                            ins = mm(o[:, j * P:(j + 1) * P], vcol[:, bc:bc + 1].broadcast_to([P, P]), ident[:, :], start=False, stop=j == 3)
                else:
                    for j in range(4):
                        for k in range(DK):
                            ins = mm(ps[:, 4 + 2 * (q % 2), 2 * j:2 * j + 2], ada[:, q % 2, k, j * P:(j + 1) * P], scol[:, :, k],
                                     start=k == 0, stop=k == DK - 1)
                ins.then_inc(mod_t, 1)

            def ad_columns(n):
                m = 3 + n // 4
                pe.wait_ge(ad_acc, n + 1)
                if n >= 2:
                    pe.wait_ge(ad_ev, n - 1)
                for cond in range(2 if m < 5 else 1):
                    o = ps[:, 4 + 2 * (n % 2) + cond, :]
                    sums = [acc[:, n % 2, cond, :]] if m < 5 else [acc[:, n % 2, i, :] for i in range(2)]
                    if m % 3 == 2:
                        for i, a in enumerate(sums):
                            mm(o[:, 0:256], ones[:, :], a, start=i == 0, stop=False)
                        for j in range(2):
                            bc = 44 + 24 + 2 * n + j
                            ins = mm(o[:, j * P:(j + 1) * P], vcol[:, bc:bc + 1].broadcast_to([P, P]), ident[:, :], start=False, stop=j == 1)
                    else:
                        for j in range(2):
                            for i, a in enumerate(sums):
                                ins = mm(o[:, j:j + 1], a[:, j * P:(j + 1) * P], ones[:, 0:1], start=i == 0, stop=i == len(sums) - 1)
                ins.then_inc(ad_t, 1)

            pe.wait_ge(sil_ok, 1)
            for q in range(3):
                modulation(q)
            pe.wait_ge(q4_ok, 1)
            for i in range(4):
                ins = tr(ps[:, 3, i * G:(i + 1) * G], sm[:, 9 + i, :], ident[0:G, 0:G])
            ins.then_inc(q4_t, 1)
            for q in range(3, 6):
                modulation(q)

            def v_transposes(gh):
                pe.wait_ge(vp_v_ok, 1)
                pe.wait_ge(vd_ok, 1)
                for i in range(8):
                    n = gh * 8 + i
                    if n >= 2:
                        pe.wait_ge(vt_ev, n - 1)
                    elif n == 0:
                        pe.wait_ge(vec_ok, 1)
                        pe.wait_ge(ct_ev, 2)
                    for g2 in range(2):
                        for a in range(2):
                            ins = tr(ps[:, i % 2, (2 * g2 + a) * P:(2 * g2 + a + 1) * P],
                                     vn[:, a, 16 * gh + 2 * i + g2].rearrange("p s c -> p (s c)"), ident[:, :])
                    ins.then_inc(vt_t, 1)

            def responses(gh):
                pe.wait_ge(w_ok, 1)
                pe.wait_ge(bf_ok, 1)
                for i in range(16):
                    n, g = gh * 16 + i, gh * 16 + i
                    if n >= 2:
                        pe.wait_ge(kt_ev, n - 1)
                    elif n == 0:
                        pe.wait_ge(q4_ev, 1)
                    o = ps[0:GC, 2 + i % 2, :]
                    w = [wn[:, a, g].rearrange("p t c -> p (t c)") for a in range(2)]
                    for a in range(2):
                        mm(o[:, 0:7 * GC], bk[:, a, g, :], w[a][:, GC:], start=a == 0, stop=a == 1)
                    for a in range(2):
                        mm(o[:, 7 * GC:8 * GC], bb[:, a, g, :], cn[:, a, g, :], start=a == 0, stop=a == 1)
                    for a in range(2):
                        ins = mm(o[:, 8 * GC:15 * GC], bf[:, a, g, :], w[a][:, 0:7 * GC], start=a == 0, stop=a == 1)
                    ins.then_inc(kt_t, 1)

            for gh in range(2):
                v_transposes(gh)
                responses(gh)

            def transposes(p, k0):
                if k0 == 0:
                    pe.wait_ge(xn_ok, p["q0"] + p["nt"])
                for k in range(k0, k0 + 4):
                    n = 8 * p["n"] + k
                    if n >= 4:
                        pe.wait_ge(h32_ok, n - 3)
                    for t in range(p["nt"]):
                        ins = tr(ps[:, k % 4, t * P:(t + 1) * P], xn[:, t, k * P:(k + 1) * P], ident[:, :])
                    ins.then_inc(ht_ok, 1)

            def three(o, l_hi, l_lo, r_hi, r_lo, start, stop):
                mm(o, l_hi, r_hi, start=start, stop=False)
                mm(o, l_hi, r_lo, start=False, stop=False)
                return mm(o, l_lo, r_hi, start=False, stop=stop)

            def up_unit(n, o, nk, prep=None):
                pe.wait_ge(up_lo_ok, n + 1)
                if prep is not None:
                    pe.wait_ge(h32_ok, 8 * prep["n"] + 5)
                for k in range(DK):
                    if prep is not None:
                        pe.wait_ge(hlo_ok, 8 * prep["n"] + k + 1)
                    ins = three(o, up_hi[:, n % 2, k], up_lo[:, n % 2, k], h_hi[:, k, 0:nk], h_lo[:, k, 0:nk], k == 0, k == DK - 1)
                ins.then_inc(up_used, 1)

            def ffn(b, prep, own):
                nt = 2 if b["ctx"] else 4
                nk = nt * P
                u, dd, F = b["up0"], b["dn0"], b["F0"]
                for r in range(NR):
                    if r == 0 and b["ev0"]:
                        pe.wait_ge(gated, b["ev0"] - b["prev_nt"])
                    if r == 1:
                        pe.wait_ge(gated, b["ev0"] + nt)
                    for f in range(FR):
                        n = F + f
                        bank = 4 * r + 2 * (f % 2)
                        if n >= 2:
                            pe.wait_ge(silu_ok, n - 1)
                        up_unit(u + 2 * f, ps[:, bank, 0:nk], nk, own if r == 0 and f == 0 else None)
                        if n >= 2:
                            pe.wait_ge(prod_ok, n - 1)
                        up_unit(u + 2 * f + 1, ps[:, bank + 1, 0:nk], nk)
                        if r == 0 and 1 <= f < len(b["ad"]) + 1:
                            if f == 1:
                                pe.wait_ge(gated, b["ev0"])
                            ad_columns(b["ad"][f - 1])
                    for hh in range(2):
                        bank = 4 * bank_set(r, hh)
                        e0 = b["ev0"] + (2 * r + hh) * nt
                        if hh == 0:
                            if e0 > 0:
                                pe.wait_ge(gated, e0)
                            if r == 0 and b["ad"]:
                                pe.wait_ge(ad_ev, b["ad"][-1] + 1)
                        else:
                            pe.wait_ge(prod_ok, F + FR)
                        for k in range(FR):
                            n = dd + hh * FR + k
                            pe.wait_ge(dn_lo_ok, n + 1)
                            pe.wait_ge(alo_ok, F + k + 1)
                            for t in range(nt):
                                ts_ = slice(t * P, (t + 1) * P)
                                ins = three(ps[:, bank + t, :], a_hi[:, k, ts_], a_lo[:, k, ts_],
                                            dn_hi[:, n % 2, :], dn_lo[:, n % 2, :], k == 0, k == FR - 1)
                            ins.then_inc(dn_used, 1)
                            if r == 1 and hh == 1 and prep is not None and k in (2, 6):
                                if k == 2:
                                    pe.wait_ge(gated, e0)
                                transposes(prep, 0 if k == 2 else 4)
                    u += 2 * FR
                    dd += 2 * FR
                    F += FR

            pe.wait_ge(kt_ev, 32)
            transposes(PREPS[0], 0)
            transposes(PREPS[0], 4)
            ffn(BLOCKS[0], PREPS[1], PREPS[0])
            ffn(BLOCKS[1], PREPS[2], PREPS[1])
            ffn(BLOCKS[2], PREPS[3], PREPS[2])
            pe.wait_ge(gated, MIX[0]["ev0"])
            done = 0
            for pi, pr in enumerate(PROJ):
                prep = PREPS[3 + pi]
                nk = prep["nt"] * P
                if pi:
                    transposes(prep, 0)
                    transposes(prep, 4)
                for j in range(len(pr["tiles"])):
                    if done >= 4:
                        pe.wait_ge(pj_ev, done - 3)
                    up_unit(pr["up0"] + j, ps[:, 4 + j % 4, 0:nk], nk, prep if j == 0 else None)
                    done += 1
            pe.wait_ge(vt_ld, 16)
            pe.wait_ge(uc_ld, 16 * T)
            for i in range(4):
                cc, gh = i // 2, i % 2
                for g in range(16):
                    ins = mm(ps[:, i, g * KC:(g + 1) * KC], vt[:, cc, 16 * gh + g, :], Uc[:, 16 * gh + g, :], start=True, stop=True)
                ins.then_inc(sc_t, 1)
            pe.wait_ge(pj_ev, 20)
            pe.wait_ge(u_ld, 16 * T)
            for i in range(16):
                if i >= 4:
                    pe.wait_ge(sl_ev, i - 3)
                cc, gq = i % 2, (i // 2) * 4
                for g in range(4):
                    ins = mm(ps[:, 4 + i % 4, g * KL:(g + 1) * KL], vt[:, cc, gq + g, :], U[:, gq + g, :], start=True, stop=True)
                ins.then_inc(sl_t, 1)
            pe.wait_ge(w_ld, 32)
            pe.wait_ge(m_ld, 16 * T)
            pe.wait_ge(sc_ev, 4)
            for i in range(8):
                if i % 4 == 0:
                    pe.wait_ge(hk_a, i // 4 + 1)
                    pe.wait_ge(hk_d, i // 4 + 1)
                if i >= 4:
                    pe.wait_ge(y_ev, i - 3)
                for g4 in range(4):
                    g = 4 * i + g4
                    o = ps[:, i % 4, g4 * P:(g4 + 1) * P]
                    mm(o, U[:, g, :], M[:, g, :], start=True, stop=False)
                    mm(o, Hk[:, 0, g, :], wy[0][:, g, :], start=False, stop=False)
                    ins = mm(o, Hk[:, 1, g, :], wy[1][:, g, :], start=False, stop=True)
                ins.then_inc(y_t, 1)
            pe.wait_ge(y_ev, 8)
            for i in range(8):
                cc, tb = i % 4, i // 4
                if i >= 4:
                    pe.wait_ge(yg_ok, i - 3)
                for t in range(4):
                    ins = tr(ps[:, 4 + i % 4, t * P:(t + 1) * P], y[:, tb * 4 + t, cc * P:(cc + 1) * P], ident[:, :])
                ins.then_inc(yt_t, 1)
            pe.wait_ge(pws_ld, 16)
            pe.wait_ge(pool_ok, 4)
            for tb in range(2):
                for j in range(4):
                    if tb:
                        pe.wait_ge(m32_ok, j + 1)
                    mm(ps[:, j, :], pws[:, j, :], vp[:, j, tb * TB:(tb + 1) * TB], start=True, stop=True).then_inc(pm_t, 1)
                if tb == 0:
                    pe.wait_ge(yg_ok, 8)
                    pe.wait_ge(glu_ld, 16)
                for j in range(4):
                    if tb:
                        pe.wait_ge(gs_ok, j + 1)
                    for k in range(4):
                        ins = mm(ps[:, 4 + j, :], wglu[:, k, j * P:(j + 1) * P], yg[:, k, tb * TB:(tb + 1) * TB],
                                 start=k == 0, stop=k == 3)
                    ins.then_inc(z_t, 1)
            for tb, mx in enumerate(MIX):
                for hh in range(2):
                    if tb == 0:
                        pe.wait_ge(m32_ok, 12) if hh == 0 else pe.wait_ge(gs_ok, 8)
                    else:
                        pe.wait_ge(gated, MIX[0]["ev0"] + 4 * (hh + 1))
                    for k in range(DK):
                        n = mx["dn0"] + hh * DK + k
                        pe.wait_ge(dn_lo_ok, n + 1)
                        pe.wait_ge(mlo_ok, tb * 8 + k + 1)
                        for t in range(4):
                            ts_ = slice(t * P, (t + 1) * P)
                            ins = three(ps[:, 4 * hh + t, :], mix_tile(tb, k, 0)[:, ts_], mix_tile(tb, k, 1)[:, ts_],
                                        dn_hi[:, n % 2, :], dn_lo[:, n % 2, :], k == 0, k == DK - 1)
                        ins.then_inc(dn_used, 1)
                        if tb == 1 and hh == 1 and k in (3, 6):
                            if k == 3:
                                pe.wait_ge(gated, mx["ev0"] + 4)
                            transposes(PREPS[6], 0 if k == 3 else 4)
            ffn(BLOCKS[3], PREPS[7], PREPS[6])
            ffn(BLOCKS[4], None, PREPS[7])


_INS = ['x', 'c', 'ctx', 'c_ctx', 'norm_g', 'w_ada', 'b_ada', 'ffn_w1', 'ffn_w3', 'ffn_w2', 'w_in', 'pool_w',
        'pool_scale', 's5_a_re', 's5_a_im', 's5_log_dt', 's5_b_re', 's5_b_im', 's5_c_re', 's5_c_im', 's5_d',
        's5_w_glu', 'w_out', 'final_g']


def kernel(**inputs):
    import numpy as _np
    import concourse.bacc as _bacc
    from concourse import mybir as _mybir
    from concourse.bass_utils import run_bass_kernel_spmd as _run

    nc = _bacc.Bacc("TRN2", target_bir_lowering=False, num_devices=1)
    arrays, args = {}, []
    for name in _INS:
        a = _np.ascontiguousarray(inputs[name])
        arrays[f"in_{name}_dram"] = a
        args.append(nc.dram_tensor(f"in_{name}_dram", a.shape, _mybir.dt.from_np(a.dtype), kind="ExternalInput").ap())
    args.append(nc.dram_tensor("out_0_dram", (1, SEQ, D), _mybir.dt.float32, kind="ExternalOutput").ap())
    hybrid_layer(nc, *args)
    r = _run(nc, [arrays], core_ids=[0])
    return r.results[0]["out_0_dram"]
```

```python
from contextlib import ExitStack

import numpy as np
import concourse.bass as bass
from concourse import mybir

P = 128
F32 = mybir.dt.float32
F32R = mybir.dt.float32r
I32 = mybir.dt.int32
ALU = mybir.AluOpType
ACT = mybir.ActivationFunctionType
KB = 1024

D = 1024
DK = D // P
SEQ, CTX = 1024, 256
FF = 2816
NF = FF // P
NR = 2
FR = NF // NR
TB = 512
HALF = 512
GW = 64
GR = SEQ // GW
WINDOWS = (2, 4, 8, 16)
G, ST, GC = 32, 64, 16
T = 8
SCAN_STEPS = 8
NS = 4
V_POOL = 5
KL, KC = SEQ // T, CTX // T
EPS = 1e-6
SL, SC = KL // NS, KC // NS
FIX = 16
S5_LOADS = 13

MAGIC = 12582912.0
LOG2E = 1.4426950408889634
LN2 = (0.693359375, -2.12194440e-4)
INV2PI = 0.15915494309189535
TWO_PI = (6.28125, 0.0019350051879882812, 3.0199159819e-7)
PI_IN = 3.1415925


def hybrid_layer(nc, x, c, ctx_tok, c_ctx, norm_g, w_ada, b_ada, ffn_w1, ffn_w3, ffn_w2, w_in,
                 pool_w, pool_scale, s5_a_re, s5_a_im, s5_log_dt, s5_b_re, s5_b_im,
                 s5_c_re, s5_c_im, s5_d, s5_w_glu, w_out, final_g, out):
    base = (nc._sbuf_addr_for_side("left") + 31) // 32 * 32

    def at(name, shape, kb, dt=F32):
        return nc.alloc_sbuf_tensor_at(name, shape, dt, offset=base + int(kb * KB))

    xl = at("xl", [P, T, D], 0)
    gate = at("gate", [P, 2, D], 32)
    ident = at("ident", [P, P], 40)
    ones = at("ones", [P, P], 40.5)
    vcol = at("vcol", [P, 116], 41)
    scol = at("scol", [P, 2, DK], 41.46875)
    gcol = at("gcol", [P, 5, DK], 41.53125)
    bcol = at("bcol", [P, 5, DK], 41.6875)
    ssq = at("ssq", [P, 4], 41.84375)
    rs = at("rs", [P, 6, 4], 41.875)
    gb = at("gb", [P, 3, DK], 207.75)
    xc = at("xc", [P, 2, D], 42)
    h_hi = at("h_hi", [P, DK, TB], 50, F32R)
    h_lo = at("h_lo", [P, DK, TB], 66, F32R)
    a_hi = at("a_hi", [P, FR, TB], 82, F32R)
    a_lo = at("a_lo", [P, FR, TB], 104, F32R)
    up_raw = at("up_raw", [P, 4, DK, P], 126)
    up_hi = at("up_hi", [P, 2, DK, P], 142, F32R)
    up_lo = at("up_lo", [P, 2, DK, P], 150, F32R)
    dn_raw = at("dn_raw", [P, 4, HALF], 158)
    dn_hi = at("dn_hi", [P, 2, HALF], 166, F32R)
    dn_lo = at("dn_lo", [P, 2, HALF], 170, F32R)
    xn = at("xn", [P, 4, D], 174)
    h32 = at("h32", [P, 2, TB], 190)
    sg = at("sg", [P, 2, TB], 194)
    a32 = at("a32", [P, 2, TB], 198)
    evt = at("evt", [P, 2, HALF], 202)
    h32f = at("fgrow", [P, D], 50)[:, :]
    xn4 = at("xn4", [P, 2, D], 194)
    hc_hi = at("hc_hi", [P, DK, CTX], 158, F32R)
    hc_lo = at("hc_lo", [P, DK, CTX], 166, F32R)
    adx = at("adx", [P, 2, DK, 256], 174)
    acc = at("acc", [P, 2, 2, 256], 190)
    ada = at("ada", [P, 2, DK, 512], 158)
    xn0 = at("xn0", [P, 2, D], 86)
    inv_r = at("inv_r", [P, 4, GR], 206)
    inv_c = at("inv_c", [P, 4, GW], 206.25)
    abar = at("abar", [P, 2, 2, 2, 16], 207.25)
    bn = at("bn", [P, 2, G, GC], 102)
    cn = at("cn", [P, 2, G, GC], 106)
    bb = at("bb", [P, 2, G, GC], 110)
    craw = at("craw", [P, 2, 4, P], 114)
    bf = at("bf", [P, 2, G, GC], 102)
    bk = at("bk", [P, 2, G, GC], 114)
    t1 = at("t1", [P, 2, G, GC], 118)
    t3 = at("t3", [P, 2, G, GC], 82)
    vn = at("vn", [P, 2, G, T, GC], 126)
    vts = at("vts", [P, 16, 2, P], 158)
    wn = at("wn", [P, 2, G, T, GC], 0)
    pwx = at("pwx", [P, 2, SL, G], 0)
    ptx = at("ptx", [P, 2, SL // 2, G], 8)
    kp = at("kp", [GC, 16, 15, GC], 174)
    dm = at("dm", [GC, G, GC], 122)
    sm = at("sm", [G, 16, P], 190)
    pw = at("pw", [P, 9, 2, G], 198)
    pwv = at("pwv", [P, T, 2, G], 96)
    pww = at("pww", [P, T, 2, G], 94)
    q4t = at("q4t", [P, 4, G], 203)
    smi = at("smi", [G, P], 203.5, I32)
    vecrow = at("vecrow", [116, P], 204)
    dt2 = at("dt2", [G, 8, 2], 204.5)
    dt2i = at("dt2i", [G, 2], 204.75, I32)
    pt = at("pt", [P, 2, 4, G], 205)
    vp = at("vp", [P, 5, SEQ], 82)
    hs = at("hs", [P, 4, CTX + SEQ], 102)
    Uc = at("Uc", [P, G, KC], 122)
    U = at("U", [P, G, KL], 158)
    vt = at("vt", [P, 2, G, P], 174)
    S = at("S", [P, KL, 2, 2, 16], 126)
    Sc = at("Sc", [P, KC, 2, 2, 16], 42)
    scn = at("scn", [P, 2, 2, NS, 2, 16], 118)
    a8re = at("a8re", [P, SL, G], 36)
    a8im = at("a8im", [P, SL, G], 122)
    fm = at("fm", [P, 2, 2, FIX, 2, 16], 42)
    fc = at("fc", [P, NS - 1, 2, 2, 16], 118)
    fe = at("fe", [P, 2, 2, 2, 16], 119)
    pws = at("pws", [P, 4, P], 120)
    M = at("M", [P, G, P], 50)
    wy = [at("wy_re", [P, G, P], 102), at("wy_im", [P, G, P], 66)]
    Hk = at("Hk", [P, 2, G, KL], 174)
    bxa = at("bxa", [P, 23 * GW], 102)
    bxb = at("bxb", [P, 23 * GW], 108)
    bxd = at("bxd", [P, SEQ], 114)
    y = at("y", [P, T, G * GC], 126)
    yg = at("yg", [P, 4, SEQ], 142)
    wglu = at("wglu", [P, 4, 512], 42)
    mp_hi = at("mp_hi", [P, 4, TB], 102, F32R)
    mp_lo = at("mp_lo", [P, 4, TB], 110, F32R)
    ms_hi = at("ms_hi", [P, 4, TB], 82, F32R)
    ms_lo = at("ms_lo", [P, 4, TB], 90, F32R)

    v_dram = nc.dram_tensor("v_dram", [P, 2, G, P], F32, kind="Internal").ap()
    w_dram = nc.dram_tensor("w_dram", [2, P, G, P], F32, kind="Internal").ap()
    k_dram = nc.dram_tensor("k_dram", [GC, G, 15 * GC], F32, kind="Internal").ap()
    a_dram = nc.dram_tensor("a_dram", [2, P, SL, G], F32, kind="Internal").ap()
    u_dram = nc.dram_tensor("u_dram", [4, P, CTX + SEQ], F32, kind="Internal").ap()

    xl_d = x.rearrange("o (k t) c -> k (o t) c", t=T)
    xc_d = ctx_tok.rearrange("o (q i) c -> q (o i) c", i=2)
    out_d = out.rearrange("o (k t) c -> k (o t) c", t=T)
    ada_d = w_ada[0].rearrange("(k p) n -> p k n", p=P)
    w1_d = ffn_w1[0].rearrange("l (k p) f -> l p k f", p=P)
    w3_d = ffn_w3[0].rearrange("l (k p) f -> l p k f", p=P)
    win_d = w_in[0].rearrange("(k p) f -> p k f", p=P)

    up_src, dn_src = [], []
    BLOCKS = [dict(ffn=0, ctx=True, t0=0, gate=0), dict(ffn=0, ctx=False, t0=0, gate=1),
              dict(ffn=0, ctx=False, t0=4, gate=1), dict(ffn=1, ctx=False, t0=0, gate=1),
              dict(ffn=1, ctx=False, t0=4, gate=1)]

    def add_ffn(b):
        b["up0"], b["dn0"] = len(up_src), len(dn_src)
        l = b["ffn"]
        for r in range(NR):
            for f in range(FR):
                fs = slice((r * FR + f) * P, (r * FR + f + 1) * P)
                up_src.append(w1_d[l][:, :, fs])
                up_src.append(w3_d[l][:, :, fs])
            for h in range(2):
                for k in range(FR):
                    row = (r * FR + k) * P
                    dn_src.append(ffn_w2[0, l, row:row + P, h * HALF:(h + 1) * HALF])

    for b in BLOCKS[:3]:
        add_ffn(b)
    PROJ = [dict(ctx=False, t0=0, tiles=range(8)), dict(ctx=True, t0=0, tiles=range(4, 8)),
            dict(ctx=False, t0=4, tiles=range(8))]
    for pr in PROJ:
        pr["up0"] = len(up_src)
        for m in pr["tiles"]:
            up_src.append(win_d[:, :, m * P:(m + 1) * P])
    MIX = [dict(ctx=False, t0=0), dict(ctx=False, t0=4)]
    for mx in MIX:
        mx["dn0"] = len(dn_src)
        for h in range(2):
            for k in range(DK):
                dn_src.append(w_out[0, k * P:(k + 1) * P, h * HALF:(h + 1) * HALF])
    for b in BLOCKS[3:]:
        add_ffn(b)
    UP_MIX = PROJ[0]["up0"]
    UP_F2 = BLOCKS[3]["up0"]
    DN_MIX = MIX[0]["dn0"]

    for n, b in enumerate(BLOCKS):
        b["F0"] = n * NF
    ev = 0
    for b in BLOCKS[:3]:
        b["ev0"] = ev
        ev += 2 * NR * (2 if b["ctx"] else 4)
    for mx in MIX:
        mx["ev0"] = ev
        ev += 2 * 4
    for b in BLOCKS[3:]:
        b["ev0"] = ev
        ev += 2 * NR * 4
    EV_END = ev

    PREPS = [dict(ctx=True, t0=0, col=0, ev=0), dict(ctx=False, t0=0, col=2, ev=0),
             dict(ctx=False, t0=4, col=2, ev=0),
             dict(ctx=False, t0=0, col=3, ev=BLOCKS[2]["ev0"]),
             dict(ctx=True, t0=0, col=1, ev=BLOCKS[1]["ev0"]),
             dict(ctx=False, t0=4, col=3, ev=MIX[0]["ev0"]),
             dict(ctx=False, t0=0, col=4, ev=MIX[1]["ev0"]),
             dict(ctx=False, t0=4, col=4, ev=BLOCKS[3]["ev0"])]
    tiles0 = 0
    for n, p in enumerate(PREPS):
        p["n"] = n
        p["ads"] = [0, 0, 10, 20, 20, 20, 20, 24][n]
        p["nt"] = 2 if p["ctx"] else 4
        p["q0"] = tiles0
        tiles0 += p["nt"]
    Q_FINAL = tiles0

    AD = {0: [], 1: list(range(0, 10)), 2: list(range(10, 20)), 3: list(range(20, 24)), 4: []}
    AD_COLS, AD_GATE_MIX, AD_COLS2, AD_ALL = 8, 12, 20, 24
    for n, b in enumerate(BLOCKS):
        b["ad"] = AD[n]
        b["prev_nt"] = [0, 2, 4, 4, 4][n]

    def bank_set(r, hh):
        return 1 - r if hh == 0 else r

    SPLITS = {3: (0, 1), 4: (1, 2), 5: (2, 3), 6: (3, 4), 8: (4, 6), 9: (6, 8)}
    PROJ_SPLITS = {(0, 5): (PREPS[4], 0, 4), (0, 7): (PREPS[4], 4, 8), (1, 1): (PREPS[5], 0, 4), (1, 3): (PREPS[5], 4, 8)}
    gs, m32 = sg, a32

    def proj_bank(pi, j):
        return j if pi == 0 else 4 + j % 4
    SCAN_END = 6 * (SC - 1 + SL)
    FIXES = [(h, sg_, j, min(j + FIX, SL - 1)) for h in range(2) for sg_ in range(1, NS) for j in range(0, SL, FIX)]

    def fix_done(u):
        return 4 * u + 6 if u + 1 < len(FIXES) else 4 * u + 4

    def mix_tile(tb, j, lo):
        if tb == 0:
            return (h_lo if lo else h_hi)[:, j, :]
        if j < 4:
            return (mp_lo if lo else mp_hi)[:, j, :]
        return (ms_lo if lo else ms_hi)[:, j - 4, :]

    def xnt(prep, t):
        return {0: xn0, 4: xn4}.get(prep["n"], xn)[:, t, :]

    def h_part(prep, lo):
        if prep["n"] == 4:
            return hc_lo if lo else hc_hi
        return h_lo if lo else h_hi

    def xt(st, t):
        return xc[:, t, :] if st["ctx"] else xl[:, st["t0"] + t, :]

    with ExitStack() as ctx:
        def sem(name):
            return ctx.enter_context(nc.semaphore(name))

        ps = ctx.enter_context(nc.psum_tensor("ps", [P, 8, 512], F32))

        vec_ld, xc_ld, s5_ld, fg_ld = (sem(n) for n in ("vec_ld", "xc_ld", "s5_ld", "fg_ld"))
        xl_ld = [sem(f"xl_ld{i}") for i in range(2)]
        ada_ld = [sem(f"ada_ld{i}") for i in range(2)]
        ad_ld = [sem(f"ad_ld{i}") for i in range(2)]
        up_ld = [sem(f"up_ld{i}") for i in range(4)]
        dn_ld = [sem(f"dn_ld{i}") for i in range(4)]
        const_ok, vec_t, vec_ok, sil_ok = (sem(n) for n in ("const_ok", "vec_t", "vec_ok", "sil_ok"))
        dve_step, pool_step = sem("dve_step"), sem("pool_step")
        ang_ok, sin_ok, q4_ok, q4_t, q4_ev, ct_t, ct_ev = (
            sem(n) for n in ("ang_ok", "sin_ok", "q4_ok", "q4_t", "q4_ev", "ct_t", "ct_ev"))
        gb_ok, mod_t, mod_ev = sem("gb_ok"), sem("mod_t"), sem("mod_ev")
        ad_acc, ad_t, ad_ev = sem("ad_acc"), sem("ad_t"), sem("ad_ev")
        pw_ok, vp_v_ok, vd_ok, w_ok, bf_ok, vt_t, vt_ev, kt_t, kt_ev = (
            sem(n) for n in ("pw_ok", "vp_v_ok", "vd_ok", "w_ok", "bf_ok", "vt_t", "vt_ev", "kt_t", "kt_ev"))
        v_st, w_st, k_st, a_st, setup_ok = sem("v_st"), sem("w_st"), sem("k_st"), sem("a_st"), sem("setup_ok")
        sq_ok, rstd_ok, xn_ok, ht_ok, hhi_ok, h32_ok, hlo_ok = (
            sem(n) for n in ("sq_ok", "rstd_ok", "xn_ok", "ht_ok", "hhi_ok", "h32_ok", "hlo_ok"))
        up_hi_ok, up_lo_ok, up_used = sem("up_hi_ok"), sem("up_lo_ok"), sem("up_used")
        dn_hi_ok, dn_lo_ok, dn_used = sem("dn_hi_ok"), sem("dn_lo_ok"), sem("dn_used")
        silu_ok, prod_ok, ahi_ok, alo_ok = sem("silu_ok"), sem("prod_ok"), sem("ahi_ok"), sem("alo_ok")
        gated, added = sem("gated"), sem("added")
        pj_ev = sem("pj_ev")
        u_st = [sem(f"u_st{i}") for i in range(3)]
        u_ld, uc_ld, vt_ld, m_ld, w_ld, glu_ld, pws_ld = (
            sem(n) for n in ("u_ld", "uc_ld", "vt_ld", "m_ld", "w_ld", "glu_ld", "pws_ld"))
        sc_t, sc_ev, sl_t, sl_ev = (sem(n) for n in ("sc_t", "sc_ev", "sl_t", "sl_ev"))
        scan_step, fix_step, a8_ld, hk_a = sem("scan_step"), sem("fix_step"), sem("a8_ld"), sem("hk_a")
        box0_ok = sem("box0_ok")
        y_t, y_ev, yt_t, yg_ok = (sem(n) for n in ("y_t", "y_ev", "yt_t", "yg_ok"))
        pool_ok, pm_t, z_t, gs_ok, m32_ok, mhi_ok, mlo_ok = (
            sem(n) for n in ("pool_ok", "pm_t", "z_t", "gs_ok", "m32_ok", "mhi_ok", "mlo_ok"))
        fin_ok, out_st = sem("fin_ok"), sem("out_st")

        block = ctx.enter_context(nc.Block())

        @block.sync
        def _(sp):
            ld = sp.dma_start
            ld(vecrow[0:8, :], c.rearrange("o (k p) -> (o k) p", p=P)).then_inc(vec_ld, 16)
            ld(vecrow[8:16, :], c_ctx.rearrange("(k p) -> k p", p=P)).then_inc(vec_ld, 16)
            ld(vecrow[16:40, :], norm_g[0].rearrange("l (k p) -> (l k) p", p=P)).then_inc(vec_ld, 16)
            ld(vecrow[40:44, :], pool_scale[0].rearrange("(k p) -> k p", p=P)).then_inc(vec_ld, 16)
            ld(vecrow[44:116, :], b_ada[0].rearrange("(k p) -> k p", p=P)).then_inc(vec_ld, 16)
            ld(sm[:, 0, :].rearrange("g (d p) -> g d p", d=2), s5_a_re[0].rearrange("d g p -> g d p")).then_inc(s5_ld, 16)
            ld(sm[:, 1, :].rearrange("g (d p) -> g d p", d=2), s5_a_im[0].rearrange("d g p -> g d p")).then_inc(s5_ld, 16)
            for d in range(2):
                ld(dt2[:, 0, d:d + 1], s5_log_dt[0, d].rearrange("(g o) -> g o", o=1)).then_inc(s5_ld, 16)
                for i, src in enumerate((s5_b_re, s5_b_im)):
                    ld(bn[d * ST:(d + 1) * ST, i, :, :], src[0].rearrange("g p c -> p g c")).then_inc(s5_ld, 16)
                for i, src in enumerate((s5_c_re, s5_c_im)):
                    ld(craw[:, i, :, d * ST:(d + 1) * ST],
                       src[0, d].rearrange("(i g) c p -> (g c) i p", g=8)).then_inc(s5_ld, 16)
            ld(dm[:, :, :].rearrange("p g c -> p (g c)"), s5_d[0:1, :].broadcast_to([GC, G * GC])).then_inc(s5_ld, 16)
            ld(xc[:, :, :], xc_d).then_inc(xc_ld, 16)
            for q in range(6):
                if q >= 2:
                    sp.wait_ge(mod_t, q - 1)
                ld(ada[:, q % 2, :, :], ada_d[:, :, q * 512:(q + 1) * 512]).then_inc(ada_ld[q % 2], 16)

            def load_up(n):
                if n >= 4:
                    sp.wait_ge(up_lo_ok, n - 3)
                ld(up_raw[:, n % 4, :, :], up_src[n]).then_inc(up_ld[n % 4], 16)

            def load_dn(n):
                if n >= 4:
                    sp.wait_ge(dn_lo_ok, n - 3)
                ld(dn_raw[:, n % 4, :], dn_src[n]).then_inc(dn_ld[n % 4], 16)

            def load_latent(t):
                ld(xl[:, t, :], xl_d[:, t, :]).then_inc(xl_ld[t // 4], 16)

            def load_ffn(b, transposed):
                for r in range(NR):
                    for u in range(2 * FR):
                        load_up(b["up0"] + r * 2 * FR + u)
                        if b is BLOCKS[0] and r == 1 and u % 5 == 4:
                            load_latent(4 + u // 5)
                        if r == 0 and u % 2 == 1 and u // 2 < len(b["ad"]):
                            n = b["ad"][u // 2]
                            if u == 1:
                                sp.wait_ge(ht_ok, transposed)
                                sp.wait_ge(hlo_ok, transposed)
                            if n >= 2:
                                sp.wait_ge(ad_acc, n - 1)
                            ld(adx[:, n % 2, :, :], ada_d[:, :, 3 * D + n * 256:3 * D + (n + 1) * 256]).then_inc(ad_ld[n % 2], 16)
                    if b is BLOCKS[0] and r == 0:
                        sp.wait_ge(setup_ok, 1)
                    for u in range(2 * FR):
                        load_dn(b["dn0"] + r * 2 * FR + u)
                        if b is BLOCKS[0] and r == 0 and u % 5 == 4:
                            if u == 4:
                                sp.wait_ge(a_st, 32)
                            load_latent(u // 5)

            sp.wait_ge(vt_t, 16)
            load_ffn(BLOCKS[0], 8)
            load_ffn(BLOCKS[1], 16)
            load_ffn(BLOCKS[2], 24)
            for n in range(UP_MIX, UP_F2 - 4):
                load_up(n)
            uc = u_dram[:, :, 0:CTX].rearrange("c (g i) (s k) -> s i (c g) k", i=GC, s=T)
            ul = u_dram[:, :, CTX:].rearrange("c (g i) (s k) -> s i (c g) k", i=GC, s=T)

            def store_u(i, n0, n1):
                ld(u_dram[:, :, n0:n1].rearrange("c p n -> p c n"), hs[:, :, n0:n1]).then_inc(u_st[i], 16)
            sp.wait_ge(pj_ev, 8)
            store_u(0, CTX, CTX + TB)
            sp.wait_ge(pj_ev, 12)
            store_u(1, 0, CTX)
            sp.wait_ge(u_st[0], 16)
            sp.wait_ge(up_used, PROJ[2]["up0"])
            for s in range(4):
                ld(U[s * GC:(s + 1) * GC, :, :], ul[s]).then_inc(u_ld, 16)
            sp.wait_ge(u_st[1], 16)
            for s in range(T):
                ld(Uc[s * GC:(s + 1) * GC, :, :], uc[s]).then_inc(uc_ld, 16)
            for n in range(UP_F2 - 4, UP_F2):
                load_up(n)
            sp.wait_ge(hlo_ok, 8 * 6)
            sp.wait_ge(added, MIX[0]["ev0"])
            ld(vt[:, :, :, :], v_dram).then_inc(vt_ld, 16)
            sp.wait_ge(pj_ev, 20)
            store_u(2, CTX + TB, CTX + 2 * TB)
            sp.wait_ge(u_st[2], 16)
            for s in range(4, T):
                ld(U[s * GC:(s + 1) * GC, :, :], ul[s]).then_inc(u_ld, 16)
            ld(pws[:, :, :], pool_w[0].rearrange("k c d -> c k d")).then_inc(pws_ld, 16)
            sp.wait_ge(gated, MIX[0]["ev0"])
            ld(a8re[:, :, :], a_dram[0]).then_inc(a8_ld, 16)
            sp.wait_ge(sc_t, 4)
            ld(a8im[:, :, :], a_dram[1]).then_inc(a8_ld, 16)
            sp.wait_ge(up_used, UP_F2)
            for s in range(T):
                ld(M[s * GC:(s + 1) * GC, :, :], k_dram[:, :, (7 - s) * GC:(15 - s) * GC]).then_inc(m_ld, 16)
            ld(wy[1][:, :, :], w_dram[1]).then_inc(w_ld, 16)
            sp.wait_ge(box0_ok, 1)
            sp.wait_ge(pool_ok, 3)
            ld(wy[0][:, :, :], w_dram[0]).then_inc(w_ld, 16)
            sp.wait_ge(fix_step, fix_done(len(FIXES) - 1))
            ld(wglu[:, :, :], s5_w_glu[0].rearrange("(k p) n -> p k n", p=P)).then_inc(glu_ld, 16)
            sp.wait_ge(y_t, 8)
            for mx in MIX:
                for u in range(16):
                    load_dn(mx["dn0"] + u)
            sp.wait_ge(m32_ok, 16)
            load_ffn(BLOCKS[3], 56)
            sp.wait_ge(gated, BLOCKS[3]["ev0"])
            ld(gate[:, 0, :], final_g.rearrange("(o n) -> o n", o=1).broadcast_to([P, D])).then_inc(fg_ld, 16)
            load_ffn(BLOCKS[4], 0)
            for t in range(T):
                sp.wait_ge(fin_ok, t + 1)
                ld(out_d[:, t, :], xl[:, t, :]).then_inc(out_st, 16)
            sp.wait_ge(out_st, 16 * T)

        @block.gpsimd
        def _(pool):
            gp = nc.gpsimd
            count = [0]

            def step(ins):
                count[0] += 1
                ins.then_inc(pool_step, 1)
                pool.wait_ge(pool_step, count[0])

            step(gp.memset(ident[:, :], 0.0))
            step(gp.affine_select(out=ident[:, :], in_=ident[:, :], compare_op=ALU.not_equal, fill=1.0,
                                  base=0, pattern=[[-1, P]], channel_multiplier=1))
            gp.memset(ones[:, :], 1.0).then_inc(const_ok, 1)
            for i, w in enumerate(WINDOWS):
                lo, hi = w // 2, w - 1 - w // 2
                for tab, n in ((inv_r, GR), (inv_c, GW)):
                    if n > lo + hi:
                        gp.memset(tab[:, i, lo:n - hi], 1.0 / w)
                    for t in list(range(min(lo, n))) + list(range(max(lo, n - hi), n)):
                        gp.memset(tab[:, i, t:t + 1], 1.0 / (min(t + hi + 1, n) - max(t - lo, 0)))
            pool.wait_ge(s5_ld, 16 * S5_LOADS)
            step(gp.affine_select(out=dm[:, :, :], in_=dm[:, :, :], compare_op=ALU.is_equal, fill=0.0,
                                  base=0, pattern=[[0, G], [-1, GC]], channel_multiplier=1))
            pool.wait_ge(q4_ev, 1)

            def cmul(outr, outi, ar, ai, br, bi, ta, tb, neg=False):
                step(gp.tensor_tensor(ta, ar, br, ALU.mult))
                step(gp.tensor_tensor(tb, ai, bi, ALU.mult))
                step(gp.tensor_tensor(outr, ta, tb, ALU.add if neg else ALU.subtract))
                step(gp.tensor_tensor(ta, ar, bi, ALU.mult))
                step(gp.tensor_tensor(tb, ai, br, ALU.mult))
                step(gp.tensor_tensor(outi, ta, tb, ALU.subtract if neg else ALU.add))

            step(gp.memset(pw[:, 0, 0, :], 1.0))
            step(gp.memset(pw[:, 0, 1, :], 0.0))
            step(gp.tensor_copy(pw[:, 1, :, :], q4t[:, 0:2, :]))
            for n in (1, 2, 4):
                def b(i):
                    return pw[:, n, i, :].unsqueeze(1).broadcast_to([P, n, G])
                cmul(pw[:, n + 1:2 * n + 1, 0, :], pw[:, n + 1:2 * n + 1, 1, :],
                     pw[:, 1:n + 1, 0, :], pw[:, 1:n + 1, 1, :], b(0), b(1), pt[:, 0, 0:n, :], pt[:, 1, 0:n, :])
            step(gp.tensor_copy(pww[0:ST, :, :, :], pw[0:ST, 1:9, :, :]))
            step(gp.tensor_copy(pww[ST:P, ::-1, :, :], pw[ST:P, 1:9, :, :]))
            step(gp.tensor_copy(pwv[0:ST, ::-1, :, :], pw[0:ST, 0:8, :, :]))
            step(gp.tensor_copy(pwv[ST:P, :, :, :], pw[ST:P, 0:8, :, :]))

            def over_c(a):
                return a.unsqueeze(2).broadcast_to([P, G, GC])
            ta, tb = t1[:, 0], t1[:, 1]
            cmul(bb[:, 0], bb[:, 1], over_c(q4t[:, 2, :]), over_c(q4t[:, 3, :]), bn[:, 0], bn[:, 1], ta, tb)
            gp.tensor_copy(pt[:, 0, 0, 0:1], pw[:, 0, 0, 0:1]).then_inc(pw_ok, 1)
            for s in range(V_POOL):
                cmul(vn[:, 0, :, s, :], vn[:, 1, :, s, :], over_c(pwv[:, s, 0, :]), over_c(pwv[:, s, 1, :]),
                     bb[:, 0], bb[:, 1], ta, tb)
            gp.tensor_copy(pt[:, 0, 1, 0:1], pw[:, 0, 0, 0:1]).then_inc(vp_v_ok, 1)
            pool.wait_ge(ct_ev, 2)
            step(gp.tensor_copy(bf[0:ST], bb[0:ST]))
            step(gp.memset(bf[ST:P], 0.0))
            step(gp.tensor_copy(bk[ST:P], bb[ST:P]))
            step(gp.memset(bk[0:ST], 0.0))
            a8 = pw[:, 8, :, :].rearrange("p a (h g) -> p a h g", h=2)
            for i in range(2):
                step(gp.tensor_copy(abar[:, :, 0, i, :], a8[:, 0]))
            step(gp.tensor_copy(abar[:, :, 1, 0, :], a8[:, 1]))
            gp.tensor_scalar(abar[:, :, 1, 1, :], a8[:, 1], -1.0, None, ALU.mult).then_inc(bf_ok, 1)
            pool.wait_ge(w_ok, 1)
            for i in range(2):
                pool.dma_start(w_dram[i], wn[:, i].rearrange("p g t c -> p g (t c)")).then_inc(w_st, 16)
            for gh in range(2):
                gs_ = slice(gh * 16, gh * 16 + 16)
                pool.wait_ge(vt_ev, 8 * (gh + 1))
                for i in range(2):
                    pool.dma_start(v_dram[:, i, gs_, :], vts[:, :, i, :]).then_inc(v_st, 16)
                pool.wait_ge(kt_ev, 16 * (gh + 1))
                step(gp.tensor_tensor(kp[:, :, 7, :], kp[:, :, 7, :], dm[:, gs_, :], ALU.add))
                pool.dma_start(k_dram[:, gs_, :], kp[:, :, :, :].rearrange("p g n c -> p g (n c)")).then_inc(k_st, 16)
            pool.wait_ge(v_st, 64)
            pool.wait_ge(w_st, 32)
            pool.wait_ge(k_st, 32)
            gp.memset(pt[:, 0, 0, 1:2], 0.0).then_inc(setup_ok, 1)
            for i in range(2):
                step(gp.tensor_copy(pwx[:, i, 0, :].rearrange("p (h g) -> p h g", h=2), abar[:, :, i, 0, :]))
            n = 1
            while n < SL:
                def last(i):
                    return pwx[:, i, n - 1, :].unsqueeze(1).broadcast_to([P, n, G])
                cmul(pwx[:, 0, n:2 * n, :], pwx[:, 1, n:2 * n, :], pwx[:, 0, 0:n, :], pwx[:, 1, 0:n, :],
                     last(0), last(1), ptx[:, 0, 0:n, :], ptx[:, 1, 0:n, :])
                n *= 2
            for i in range(2):
                pool.dma_start(a_dram[i], pwx[:, i]).then_inc(a_st, 16)
            pool.wait_ge(a_st, 32)

            def add_tiles(st, nt, halves):
                for hh in range(halves):
                    for t in range(nt):
                        e = st["ev0"] + hh * nt + t
                        pool.wait_ge(gated, e + 1)
                        dst = xt(st, t)[:, (hh % 2) * HALF:(hh % 2 + 1) * HALF]
                        gp.tensor_tensor(dst, dst, evt[:, e % 2, :], ALU.add).then_inc(added, 1)

            for b in BLOCKS[:3]:
                add_tiles(b, 2 if b["ctx"] else 4, 2 * NR)
            pool.wait_ge(pj_ev, 20)
            for i in range(3):
                pool.wait_ge(u_st[i], 16)
            for i, w in enumerate(WINDOWS):
                if i == 0:
                    continue
                if i == 1:
                    pool.wait_ge(box0_ok, 1)
                hi = w // 2 - 1
                v = vp[:, i + 1, :].rearrange("p (r c) -> p r c", c=GW)
                cur, nxt = bxa, bxb

                def rows(buf):
                    return buf[:, 0:(GR + hi) * GW].rearrange("p (r c) -> p r c", c=GW)

                def cols(buf):
                    return buf[:, 0:GR * (GW + hi)].rearrange("p (r c) -> p r c", c=GW + hi)
                o = rows(cur)
                step(gp.tensor_tensor(o[:, 1:GR, :], v[:, 1:, :], v[:, 0:GR - 1, :], ALU.add))
                step(gp.tensor_copy(o[:, 0:1, :], v[:, 0:1, :]))
                if hi:
                    step(gp.tensor_copy(o[:, GR:GR + 1, :], v[:, GR - 1:GR, :]))
                if hi > 1:
                    step(gp.memset(o[:, GR + 1:, :], 0.0))
                m = 2
                while m < w:
                    a, o = rows(cur), rows(nxt)
                    step(gp.tensor_tensor(o[:, m:, :], a[:, m:, :], a[:, 0:GR + hi - m, :], ALU.add))
                    step(gp.tensor_copy(o[:, 0:m, :], a[:, 0:m, :]))
                    cur, nxt = nxt, cur
                    m *= 2
                step(gp.tensor_tensor(cols(nxt)[:, :, 0:GW], rows(cur)[:, hi:, :],
                                      inv_r[:, i, :].unsqueeze(2).broadcast_to([P, GR, GW]), ALU.mult))
                cur, nxt = nxt, cur
                if hi:
                    step(gp.memset(cols(cur)[:, :, GW:], 0.0))
                m = 1
                while m < w:
                    a, o = cols(cur), cols(nxt)
                    step(gp.tensor_tensor(o[:, :, m:], a[:, :, m:], a[:, :, 0:GW + hi - m], ALU.add))
                    step(gp.tensor_copy(o[:, :, 0:m], a[:, :, 0:m]))
                    cur, nxt = nxt, cur
                    m *= 2
                pooled = nxt[:, 0:SEQ].rearrange("p (r c) -> p r c", c=GW)
                step(gp.tensor_tensor(pooled, cols(cur)[:, :, hi:],
                                      inv_c[:, i, :].unsqueeze(1).broadcast_to([P, GR, GW]), ALU.mult))
                gp.tensor_tensor(vp[:, i, :].rearrange("p (s k) -> p k s", s=T), nxt[:, 0:SEQ].rearrange("p (k s) -> p k s", s=T),
                                 vp[:, i + 1, :].rearrange("p (k s) -> p k s", s=T), ALU.subtract).then_inc(pool_ok, 1)
                pool.wait_ge(pool_ok, i)
            for mx in MIX:
                add_tiles(mx, 4, 2)
            for b in BLOCKS[3:]:
                add_tiles(b, 4, 2 * NR)

        @block.scalar
        def _(act):
            sa = nc.scalar.activation
            def modulation(q):
                m, h = q // 2, q % 2
                act.wait_ge(mod_t, q + 1)
                if m == 1:
                    act.wait_ge(gb_ok, 1)
                for cond in range(2):
                    if m == 2:
                        ins = sa(gate[:, 1 - cond, h * 512:(h + 1) * 512], ps[:, 4 + 2 * (q % 2) + cond, :], ACT.Copy, scale=0.5)
                    else:
                        for j in range(4):
                            k = 4 * h + j
                            src = ps[:, 4 + 2 * (q % 2), 2 * j + cond:2 * j + cond + 1]
                            ins = mod_column(src, m, 2 * (1 - cond), k)
                ins.then_inc(mod_ev, 1)

            def mod_column(src, m, col, k):
                if m % 3 == 0:
                    return sa(bcol[:, col, k:k + 1], src, ACT.Identity, bias=vcol[:, 44 + 8 * m + k:45 + 8 * m + k])
                n = m // 3
                return sa(gcol[:, col, k:k + 1], src, ACT.Identity, scale=vcol[:, 16 + 8 * n + k:17 + 8 * n + k],
                          bias=gb[:, n, k:k + 1])

            def ad_evict(n):
                m, part = 3 + n // 4, n % 4
                act.wait_ge(ad_t, n + 1)
                if m == 5 and part == 0:
                    act.wait_ge(gated, BLOCKS[1]["ev0"])
                if m == 8 and part == 0:
                    act.wait_ge(gated, MIX[0]["ev0"])
                for cond in range(2 if m < 5 else 1):
                    src = ps[:, 4 + 2 * (n % 2) + cond, :]
                    if m % 3 == 2:
                        ins = sa(gate[:, m // 8, part * 256:(part + 1) * 256], src[:, 0:256], ACT.Copy, scale=0.5 if m == 8 else 1.0)
                    else:
                        for j in range(2):
                            ins = mod_column(src[:, j:j + 1], m, m // 3 + (2 if cond == 0 else 0), 2 * part + j)
                ins.then_inc(ad_ev, 1)

            def v_evict(gh):
                for i in range(8):
                    act.wait_ge(vt_t, gh * 8 + i + 1)
                    if gh and i == 0:
                        act.wait_ge(v_st, 32)
                    sa(vts[:, 2 * i:2 * i + 2, :, :].rearrange("p g a n -> p (g a n)"), ps[:, i % 2, :], ACT.Copy).then_inc(vt_ev, 1)

            def k_evict(gh):
                for i in range(16):
                    act.wait_ge(kt_t, gh * 16 + i + 1)
                    if gh and i == 0:
                        act.wait_ge(k_st, 16)
                    sa(kp[:, i, :, :].rearrange("p n c -> p (n c)"), ps[0:GC, 2 + i % 2, 0:15 * GC], ACT.Copy).then_inc(kt_ev, 1)

            def squares(p, tiles=None):
                if p["ev"]:
                    act.wait_ge(added, p["ev"])
                if p["n"] in (1, 2):
                    act.wait_ge(xl_ld[p["n"] - 1], 64)
                if p["ads"]:
                    act.wait_ge(ad_acc, p["ads"])
                for t in range(p["nt"]) if tiles is None else tiles:
                    if p["n"] >= 1:
                        act.wait_ge(ht_ok, 8 * (p["n"] if p["n"] != 5 else 4))
                        act.wait_ge(rstd_ok, p["n"])
                    sa(xnt(p, t), xt(p, t), ACT.Square, accum_out=ssq[:, t:t + 1]).then_inc(sq_ok, 1)

            def hi_of_h(p, k0, k1):
                nk = p["nt"] * P
                if p["n"] == 5:
                    act.wait_ge(up_used, PROJ[1]["up0"])
                for k in range(k0, k1):
                    act.wait_ge(h32_ok, 8 * p["n"] + k + 1)
                    sa(h_part(p, 0)[:, k, 0:nk], h32[:, k % 2, 0:nk], ACT.Copy).then_inc(hhi_ok, 1)

            act.wait_ge(vec_t, 1)
            sa(vcol[:, :], ps[:, 0, 0:116], ACT.Copy).then_inc(vec_ok, 1)
            act.wait_ge(vec_ok, 1)
            sa(scol[:, :, :].rearrange("p a k -> p (a k)"), vcol[:, 0:16], ACT.Silu).then_inc(sil_ok, 1)
            for i in range(2):
                act.wait_ge(ct_t, i + 1)
                sa(cn[:, i].rearrange("p g c -> p (g c)"), ps[:, 1 + i, :], ACT.Copy, scale=1.0 - 2.0 * i).then_inc(ct_ev, 1)
            act.wait_ge(ang_ok, 1)
            sa(sm[:, 4, :], sm[:, 3, :], ACT.Sin).then_inc(sin_ok, 1)
            sa(sm[:, 5, :], sm[:, 3, :], ACT.Sin, scale=0.5).then_inc(sin_ok, 1)
            act.wait_ge(xc_ld, 16)
            squares(PREPS[0])
            modulation(0)
            modulation(1)
            act.wait_ge(q4_t, 1)
            sa(q4t[:, :, :], ps[:, 3, 0:4 * G].rearrange("p (a g) -> p a g", a=4), ACT.Copy).then_inc(q4_ev, 1)
            modulation(2)
            modulation(3)
            hi_of_h(PREPS[0], 0, 8)
            for q in range(4, 6):
                modulation(q)
            v_evict(0)
            k_evict(0)
            v_evict(1)
            k_evict(1)

            def conv_up(n):
                act.wait_ge(up_ld[n % 4], 16 * (n // 4 + 1))
                if n >= 2:
                    act.wait_ge(up_used, n - 1)
                sa(up_hi[:, n % 2], up_raw[:, n % 4], ACT.Copy).then_inc(up_hi_ok, 1)

            def conv_dn(n):
                act.wait_ge(dn_ld[n % 4], 16 * (n // 4 + 1))
                if n >= 2:
                    act.wait_ge(dn_used, n - 1)
                sa(dn_hi[:, n % 2], dn_raw[:, n % 4], ACT.Copy).then_inc(dn_hi_ok, 1)

            def ffn(b, prep, look):
                nt = 2 if b["ctx"] else 4
                nk = nt * P
                u, dd, F = b["up0"], b["dn0"], b["F0"]
                for r in range(NR):
                    for f in range(FR):
                        nxt = [("u", u + 2 * f + 2), ("u", u + 2 * f + 3)] if f < FR - 1 else [("d", dd), ("d", dd + 1)]
                        fn = {"u": conv_up, "d": conv_dn}
                        fn[nxt[0][0]](nxt[0][1])
                        act.wait_ge(up_used, u + 2 * f + 1)
                        if F + f >= 2:
                            act.wait_ge(prod_ok, F + f - 1)
                        sa(sg[:, (F + f) % 2, 0:nk], ps[:, 4 * r + 2 * (f % 2), 0:nk], ACT.Silu).then_inc(silu_ok, 1)
                        fn[nxt[1][0]](nxt[1][1])
                        act.wait_ge(prod_ok, F + f + 1)
                        sa(a_hi[:, f, 0:nk], a32[:, (F + f) % 2, 0:nk], ACT.Copy).then_inc(ahi_ok, 1)
                        if r == 1 and prep is not None and 3 <= f < 3 + prep["nt"]:
                            squares(prep, [f - 3])
                        if r == 1 and prep is None and b is BLOCKS[4] and f == 4:
                            final_squares(0)
                        if r == 0 and 2 <= f < len(b["ad"]) + 2:
                            ad_evict(b["ad"][f - 2])
                    if r == 0 and len(b["ad"]) > FR - 2:
                        ad_evict(b["ad"][FR - 2])
                    for i in range(2 * FR):
                        if i + 2 < 2 * FR:
                            conv_dn(dd + i + 2)
                        elif r == 0:
                            conv_up(u + 2 * FR + i + 2 - 2 * FR)
                        elif look is not None:
                            conv_up(look + i + 2 - 2 * FR)
                        if r == 1 and prep is not None and i - FR in SPLITS:
                            hi_of_h(prep, *SPLITS[i - FR])
                    u += 2 * FR
                    dd += 2 * FR
                    F += FR

            def final_squares(g4):
                for t in range(4):
                    if g4 == 0:
                        act.wait_ge(added, BLOCKS[4]["ev0"])
                        act.wait_ge(ht_ok, 64)
                        act.wait_ge(rstd_ok, len(PREPS))
                    else:
                        act.wait_ge(added, EV_END - 3 + t)
                        act.wait_ge(rstd_ok, len(PREPS) + 1)
                    sa(xn[:, t, :], xl[:, 4 * g4 + t, :], ACT.Square, accum_out=ssq[:, t:t + 1]).then_inc(sq_ok, 1)

            act.wait_ge(bf_ok, 1)
            act.wait_ge(w_ok, 1)
            conv_up(0)
            conv_up(1)
            ffn(BLOCKS[0], PREPS[1], BLOCKS[1]["up0"])
            ffn(BLOCKS[1], PREPS[2], BLOCKS[2]["up0"])
            ffn(BLOCKS[2], PREPS[3], PROJ[0]["up0"])
            for pi, pr in enumerate(PROJ):
                for j in range(len(pr["tiles"])):
                    n = pr["up0"] + j + 2
                    if n < UP_F2:
                        conv_up(n)
                    if pi == 0 and j in (0, 3):
                        squares(PREPS[4 if j == 0 else 5])
                    if (pi, j) in PROJ_SPLITS:
                        hi_of_h(*PROJ_SPLITS[pi, j])
            for i in range(4):
                act.wait_ge(sc_t, i + 1)
                cc, gh = i // 2, i % 2
                src = ps[:, i, :].rearrange("p (g k) -> p k g", k=KC)
                sa(Sc[0:ST, :, gh, cc, :], src[0:ST], ACT.Copy)
                sa(Sc[ST:P, ::-1, gh, cc, :], src[ST:P], ACT.Copy).then_inc(sc_ev, 1)
            for i in range(16):
                act.wait_ge(sl_t, i + 1)
                cc, g4 = i % 2, i // 2
                src = ps[:, 4 + i % 4, :].rearrange("p (g k) -> p k g", k=KL)
                gq = 4 * (g4 % 4)
                sa(S[0:ST, :, g4 // 4, cc, gq:gq + 4], src[0:ST], ACT.Copy)
                sa(S[ST:P, ::-1, g4 // 4, cc, gq:gq + 4], src[ST:P], ACT.Copy).then_inc(sl_ev, 1)
            act.wait_ge(sl_t, 16)
            act.wait_ge(scan_step, SCAN_END)

            def enter(gh, k0, k1):
                hs_ = slice(16 * gh, 16 * gh + 16)
                for a in range(2):
                    src = S[:, k0:k1, gh, a, :].rearrange("p k g -> p g k")
                    sa(Hk[0:ST, a, hs_, k0 + 1:k1 + 1], src[0:ST], ACT.Copy)
                    ins = sa(Hk[ST:P, a, hs_, KL - 1 - k1:KL - 1 - k0][:, :, ::-1], src[ST:P], ACT.Copy)
                return ins
            for gh in range(2):
                hs_ = slice(16 * gh, 16 * gh + 16)
                sa(Hk[0:ST, :, hs_, 0], Sc[0:ST, KC - 1, gh], ACT.Copy)
                sa(Hk[ST:P, :, hs_, KL - 1], Sc[ST:P, KC - 1, gh], ACT.Copy).then_inc(hk_a, 1)
            for gh in range(2):
                enter(gh, 0, SL)
            for gh in range(2):
                for n in range(1, NS):
                    act.wait_ge(fix_step, fix_done((gh * (NS - 1) + n) * SL // FIX - 1))
                    ins = enter(gh, n * SL, min((n + 1) * SL, KL - 1))
                ins.then_inc(hk_a, 1)
            for i in range(8):
                act.wait_ge(y_t, i + 1)
                if i == 0:
                    act.wait_ge(hk_a, 4)
                sa(y[:, :, 64 * i:64 * i + 64].rearrange("p t (g c) -> p g t c", c=GC),
                   ps[:, i % 4, :].rearrange("p (g t c) -> p g t c", g=4, c=GC), ACT.Copy).then_inc(y_ev, 1)
            for i in range(8):
                act.wait_ge(yt_t, i + 1)
                cc, tb = i % 4, i // 4
                sa(yg[:, cc, tb * TB:(tb + 1) * TB], ps[:, 4 + i % 4, :], ACT.Gelu_apprx_tanh).then_inc(yg_ok, 1)
            for tb in range(2):
                for j in range(8):
                    n = tb * 8 + j
                    if j >= 4:
                        act.wait_ge(z_t, tb * 4 + j - 3)
                        if n >= 6:
                            act.wait_ge(m32_ok, (n - 2) + 1)
                        sa(gs[:, n % 2, :], ps[:, 4 + j % 4, :], ACT.Sigmoid).then_inc(gs_ok, 1)
                    act.wait_ge(m32_ok, n + 1)
                    sa(mix_tile(tb, j, 0), m32[:, n % 2, :], ACT.Copy).then_inc(mhi_ok, 1)
            d0 = MIX[0]["dn0"]
            conv_dn(d0)
            conv_dn(d0 + 1)
            for i in range(32):
                if i + 2 < 32:
                    conv_dn(d0 + i + 2)
                elif i == 30:
                    conv_up(UP_F2)
                    conv_up(UP_F2 + 1)
                if i == 18:
                    squares(PREPS[6])
                if i in (28, 29):
                    hi_of_h(PREPS[6], 2 * (i - 28), 2 * (i - 27))
            hi_of_h(PREPS[6], 4, 8)
            ffn(BLOCKS[3], PREPS[7], BLOCKS[4]["up0"])
            ffn(BLOCKS[4], None, None)
            final_squares(1)

        @block.vector
        def _(dve):
            ve = nc.vector
            tt, ts, stt = ve.tensor_tensor, ve.tensor_scalar, ve.scalar_tensor_tensor
            count = [0]

            def step(ins):
                count[0] += 1
                ins.then_inc(dve_step, 1)
                dve.wait_ge(dve_step, count[0])

            def exp(dst, src, k, f, ki):
                step(ts(f, src, -88.0, 89.0, ALU.max, ALU.min))
                step(ts(k, f, LOG2E, MAGIC, ALU.mult, ALU.add))
                step(ts(k, k, -MAGIC, None, ALU.add))
                step(stt(out=f, in0=k, scalar=-LN2[0], in1=f, op0=ALU.mult, op1=ALU.add))
                step(stt(out=f, in0=k, scalar=-LN2[1], in1=f, op0=ALU.mult, op1=ALU.add))
                step(ts(k, k, 127.0, None, ALU.add))
                step(ve.tensor_copy(ki, k))
                step(ts(ki, ki, 23, None, ALU.logical_shift_left))
                step(ts(k, f, 1.0 / 5040, None, ALU.mult))
                for n in (720, 120, 24, 6, 2, 1):
                    step(stt(out=k, in0=k, scalar=1.0 / n, in1=f, op0=ALU.add, op1=ALU.mult))
                step(ts(k, k, 1.0, None, ALU.add))
                step(tt(dst, k, ki.bitcast(F32), ALU.mult))

            def rstd(n, nt, last):
                v, r, a, b_ = (rs[:, i, 0:nt] for i in range(4))
                ri = rs[:, 4, 0:nt].bitcast(I32)
                dve.wait_ge(sq_ok, last)
                step(ts(v, ssq[:, 0:nt], 1.0 / D, EPS, ALU.mult, ALU.add))
                step(ts(ri, v.bitcast(I32), 1, None, ALU.logical_shift_right))
                step(ve.tensor_copy(a, ri))
                step(ts(a, a, -1.0, float(0x5f3759df), ALU.mult, ALU.add))
                step(ve.tensor_copy(ri, a))
                step(ve.tensor_copy(r, ri.bitcast(F32)))
                for it in range(4):
                    step(tt(a, r, r, ALU.mult))
                    step(tt(a, a, v, ALU.mult))
                    step(ts(a, a, -0.5, 1.5, ALU.mult, ALU.add))
                    if it < 3:
                        step(tt(r, r, a, ALU.mult))
                    else:
                        tt(rs[:, 5, 0:nt], r, a, ALU.mult).then_inc(rstd_ok, 1)
                        dve.wait_ge(rstd_ok, n + 1)

            def normalise(p, tiles=None):
                if tiles is None or tiles[0] == 0:
                    rstd(p["n"], p["nt"], p["q0"] + p["nt"])
                for t in range(p["nt"]) if tiles is None else tiles:
                    ts(xnt(p, t), xt(p, t), rs[:, 5, t:t + 1], None, ALU.mult).then_inc(xn_ok, 1)

            def split_h(p, k0, k1):
                nk = p["nt"] * P
                if k0 == 0 and p["n"] >= 2:
                    dve.wait_ge(ad_t, p["ads"])
                if k0 == 0 and p["n"] >= 3:
                    dve.wait_ge(ad_ev, AD_COLS if p["n"] < 6 else AD_COLS2)

                def low(k):
                    dve.wait_ge(hhi_ok, 8 * p["n"] + k + 1)
                    tt(h_part(p, 1)[:, k, 0:nk], h32[:, k % 2, 0:nk], h_part(p, 0)[:, k, 0:nk].bitcast(F32), ALU.subtract).then_inc(hlo_ok, 1)
                for k in range(k0, k1):
                    dve.wait_ge(ht_ok, 8 * p["n"] + k + 1)
                    if 8 * p["n"] + k >= 2:
                        dve.wait_ge(hlo_ok, 8 * p["n"] + k - 1)
                    src = ps[:, k // 2, (k % 2) * nk:(k % 2 + 1) * nk] if p["n"] == 0 else ps[:, k % 4, 0:nk]
                    ts(h32[:, k % 2, 0:nk], src, gcol[:, p["col"], k:k + 1], bcol[:, p["col"], k:k + 1],
                       ALU.mult, ALU.add).then_inc(h32_ok, 1)
                    if k > k0:
                        low(k - 1)
                low(k1 - 1)

            dve.wait_ge(vec_ok, 1)
            for n in range(3):
                ins = stt(out=gb[:, n, :], in0=vcol[:, 44 + 8 * (3 * n + 1):44 + 8 * (3 * n + 2)], scalar=1.0,
                          in1=vcol[:, 16 + 8 * n:24 + 8 * n], op0=ALU.add, op1=ALU.mult)
            ins.then_inc(gb_ok, 1)
            dve.wait_ge(s5_ld, 16 * S5_LOADS)
            are, aim = sm[:, 0, :], sm[:, 1, :]
            exp(dt2[:, 1, :], dt2[:, 0, :], dt2[:, 2, :], dt2[:, 3, :], dt2i[:, :])
            for d in range(2):
                half = slice(d * ST, (d + 1) * ST)
                step(ts(sm[:, 2, half], sm[:, 0, half], dt2[:, 1, d:d + 1], None, ALU.mult))
                step(ts(sm[:, 3, half], sm[:, 1, half], dt2[:, 1, d:d + 1], None, ALU.mult))
            th, k_ = sm[:, 3, :], sm[:, 6, :]
            step(ts(k_, th, INV2PI, MAGIC, ALU.mult, ALU.add))
            step(ts(k_, k_, -MAGIC, None, ALU.add))
            for part in TWO_PI:
                step(stt(out=th, in0=k_, scalar=-part, in1=th, op0=ALU.mult, op1=ALU.add))
            step(ts(th, th, -PI_IN, PI_IN, ALU.max, ALU.min))
            ts(th, th, 1.0, None, ALU.mult).then_inc(ang_ok, 1)
            exp(sm[:, 7, :], sm[:, 2, :], sm[:, 6, :], sm[:, 8, :], smi[:, :])
            dve.wait_ge(sin_ok, 2)
            mag, s1, s2 = sm[:, 7, :], sm[:, 4, :], sm[:, 5, :]
            ar, ai, cr, ci = (sm[:, 9 + i, :] for i in range(4))
            step(tt(s2, s2, s2, ALU.mult))
            step(ts(s2, s2, -2.0, 1.0, ALU.mult, ALU.add))
            step(tt(ar, mag, s2, ALU.mult))
            step(tt(ai, mag, s1, ALU.mult))
            nr, den, ta, tb = sm[:, 13, :], sm[:, 14, :], sm[:, 15, :], sm[:, 6, :]
            step(ts(nr, ar, -1.0, None, ALU.add))
            step(tt(den, are, are, ALU.mult))
            step(tt(ta, aim, aim, ALU.mult))
            step(tt(den, den, ta, ALU.add))
            step(ve.reciprocal(den, den))
            step(tt(ta, nr, are, ALU.mult))
            step(tt(tb, ai, aim, ALU.mult))
            step(tt(ta, ta, tb, ALU.add))
            step(tt(cr, ta, den, ALU.mult))
            step(tt(ta, ai, are, ALU.mult))
            step(tt(tb, nr, aim, ALU.mult))
            step(tt(ta, ta, tb, ALU.subtract))
            tt(ci, ta, den, ALU.mult).then_inc(q4_ok, 1)
            normalise(PREPS[0])

            def cmul(outr, outi, ar, ai, br, bi, ta, tb, neg=False):
                step(tt(ta, ar, br, ALU.mult))
                step(tt(tb, ai, bi, ALU.mult))
                step(tt(outr, ta, tb, ALU.add if neg else ALU.subtract))
                step(tt(ta, ar, bi, ALU.mult))
                step(tt(tb, ai, br, ALU.mult))
                step(tt(outi, ta, tb, ALU.subtract if neg else ALU.add))

            def over_c(a):
                return a.unsqueeze(2).broadcast_to([P, G, GC])
            dve.wait_ge(pw_ok, 1)
            dve.wait_ge(ct_ev, 2)
            ta, tb = t3[:, 0], t3[:, 1]
            for s in range(V_POOL, T):
                cmul(vn[:, 0, :, s, :], vn[:, 1, :, s, :], over_c(pwv[:, s, 0, :]), over_c(pwv[:, s, 1, :]),
                     bb[:, 0], bb[:, 1], ta, tb)
            ve.tensor_copy(dt2[:, 4, :], dt2[:, 1, :]).then_inc(vd_ok, 1)
            dve.wait_ge(mod_ev, 4)
            dve.wait_ge(q4_t, 1)
            dve.wait_ge(ht_ok, 8)
            split_h(PREPS[0], 0, 8)
            for t in range(T):
                cmul(wn[:, 0, :, t, :], wn[:, 1, :, t, :], over_c(pww[:, t, 0, :]), over_c(pww[:, t, 1, :]),
                     cn[:, 0], cn[:, 1], ta, tb, neg=True)
            ve.tensor_copy(dt2[:, 5, :], dt2[:, 1, :]).then_inc(w_ok, 1)

            def ad_sum(n, part, parts=4):
                both = 3 + n // 4 < 5
                ops = [(k, cond, cond, k == 0) for k in range(DK) for cond in range(2)] if both else \
                    [(k, 0, k % 2, k < 2) for k in range(DK)]
                if part == 0:
                    dve.wait_ge(ad_ld[n % 2], 16 * (n // 2 + 1))
                    if n >= 2:
                        dve.wait_ge(ad_t, n - 1)
                each = len(ops) // parts
                for i in range(part * each, (part + 1) * each):
                    k, cond, chain, first = ops[i]
                    a, sc = acc[:, n % 2, chain, :], scol[:, cond, k:k + 1]
                    if first:
                        ins = ts(a, adx[:, n % 2, k, :], sc, None, ALU.mult)
                    else:
                        dve.wait_ge(dve_step, count[0] - 1)
                        ins = stt(out=a, in0=adx[:, n % 2, k, :], scalar=sc, in1=a, op0=ALU.mult, op1=ALU.add)
                    ins.then_inc(dve_step, 1)
                    count[0] += 1
                if part == parts - 1:
                    dve.wait_ge(dve_step, count[0])
                    ve.tensor_copy(rs[:, 3, 0:1], ssq[:, 0:1]).then_inc(ad_acc, 1)

            def lo_up(n):
                dve.wait_ge(up_hi_ok, n + 1)
                tt(up_lo[:, n % 2], up_raw[:, n % 4], up_hi[:, n % 2].bitcast(F32), ALU.subtract).then_inc(up_lo_ok, 1)

            def lo_dn(n):
                dve.wait_ge(dn_hi_ok, n + 1)
                tt(dn_lo[:, n % 2], dn_raw[:, n % 4], dn_hi[:, n % 2].bitcast(F32), ALU.subtract).then_inc(dn_lo_ok, 1)

            def gated_tile(e, t, g_row, hh, bank):
                if e >= 2:
                    dve.wait_ge(added, e - 1)
                tt(evt[:, e % 2, :], ps[:, bank + t, :], gate[:, g_row, hh * HALF:(hh + 1) * HALF], ALU.mult).then_inc(gated, 1)

            def ffn(b, prep, look):
                nt = 2 if b["ctx"] else 4
                nk = nt * P
                u, dd, F = b["up0"], b["dn0"], b["F0"]
                fn = {"u": lo_up, "d": lo_dn}
                for r in range(NR):
                    for f in range(FR):
                        nxt = [("u", u + 2 * f + 2), ("u", u + 2 * f + 3)] if f < FR - 1 else [("d", dd), ("d", dd + 1)]
                        fn[nxt[0][0]](nxt[0][1])
                        n = F + f
                        ad = b["ad"][f] if r == 0 and f < len(b["ad"]) else None
                        if ad is not None:
                            ad_sum(ad, 0)
                        if n == FR - 2:
                            dve.wait_ge(setup_ok, 1)
                        dve.wait_ge(silu_ok, n + 1)
                        dve.wait_ge(up_used, u + 2 * f + 2)
                        if n >= 2:
                            dve.wait_ge(ahi_ok, n - 1)
                            dve.wait_ge(alo_ok, n - 1)
                        tt(a32[:, n % 2, 0:nk], sg[:, n % 2, 0:nk], ps[:, 4 * r + 2 * (f % 2) + 1, 0:nk], ALU.mult).then_inc(prod_ok, 1)
                        if ad is not None:
                            ad_sum(ad, 1)
                        fn[nxt[1][0]](nxt[1][1])
                        if ad is not None:
                            ad_sum(ad, 2)
                        dve.wait_ge(ahi_ok, n + 1)
                        tt(a_lo[:, f, 0:nk], a32[:, n % 2, 0:nk], a_hi[:, f, 0:nk].bitcast(F32), ALU.subtract).then_inc(alo_ok, 1)
                        if ad is not None:
                            ad_sum(ad, 3)
                        if r == 1 and prep is not None and f >= 7:
                            normalise(prep, [f - 7])
                        if r == 1 and prep is None and f == 6:
                            final_scale(0)
                    for i in range(2 * FR):
                        if i in (FR - 1, 2 * FR - 1):
                            hh = i // FR
                            e0 = b["ev0"] + (2 * r + hh) * nt
                            dve.wait_ge(dn_used, dd + i + 1)
                            if b is BLOCKS[0] and r == 0 and hh == 0:
                                dve.wait_ge(setup_ok, 1)
                            if b is BLOCKS[3] and r == 0 and hh == 0:
                                dve.wait_ge(ad_ev, AD_ALL)
                            for t in range(nt):
                                gated_tile(e0 + t, t, b["gate"], hh, 4 * bank_set(r, hh))
                                if t == nt // 2 - 1:
                                    if i == FR - 1:
                                        lo_dn(dd + i + 2)
                                    elif r == 0:
                                        lo_up(u + 2 * FR + 1)
                                    elif look is not None:
                                        lo_up(look + 1)
                        elif i + 2 < 2 * FR:
                            lo_dn(dd + i + 2)
                        elif r == 0:
                            lo_up(u + 2 * FR)
                        elif look is not None:
                            lo_up(look)
                        if r == 1 and prep is not None and i - FR in SPLITS:
                            split_h(prep, *SPLITS[i - FR])
                    u += 2 * FR
                    dd += 2 * FR
                    F += FR

            def final_scale(g4):
                rstd(len(PREPS) + g4, 4, Q_FINAL + 4 * (g4 + 1))
                dve.wait_ge(fg_ld, 16)
                for t in range(4):
                    tl = xl[:, 4 * g4 + t, :]
                    stt(out=tl, in0=tl, scalar=rs[:, 5, t:t + 1], in1=gate[:, 0, :], op0=ALU.mult, op1=ALU.mult).then_inc(fin_ok, 1)

            dve.wait_ge(bf_ok, 1)
            lo_up(0)
            lo_up(1)
            ffn(BLOCKS[0], PREPS[1], BLOCKS[1]["up0"])
            ffn(BLOCKS[1], PREPS[2], BLOCKS[2]["up0"])
            ffn(BLOCKS[2], PREPS[3], PROJ[0]["up0"])
            for pi, pr in enumerate(PROJ):
                for j, mt in enumerate(pr["tiles"]):
                    n = pr["up0"] + j
                    if n + 2 < UP_F2:
                        lo_up(n + 2)
                    dve.wait_ge(up_used, n + 1)
                    src = ps[:, proj_bank(pi, j), :]
                    if pr["ctx"]:
                        ve.tensor_copy(hs[:, mt - 4, 0:CTX].rearrange("p (s i k) -> p s i k", s=4, i=2),
                                       src[:, 0:CTX].rearrange("p (i k s) -> p s i k", s=4, i=2)).then_inc(pj_ev, 1)
                    elif mt >= 4:
                        n0 = CTX + pr["t0"] * P
                        ve.tensor_copy(hs[:, mt - 4, n0:n0 + TB], src).then_inc(pj_ev, 1)
                    else:
                        ve.tensor_copy(vp[:, mt + 1, :].rearrange("p (k s) -> p s k", s=T)[:, pr["t0"]:pr["t0"] + 4, :],
                                       src.rearrange("p (s k) -> p s k", s=4)).then_inc(pj_ev, 1)
                    if pi == 0 and j in (1, 4):
                        normalise(PREPS[4 if j == 1 else 5])
                    if (pi, j) in PROJ_SPLITS:
                        split_h(*PROJ_SPLITS[pi, j])

            def scan_chunk(dst, prev, ns, at0):
                n = [at0]

                def go(ins):
                    n[0] += 1
                    ins.then_inc(scan_step, 1)

                def wait():
                    if not (isinstance(n[0], int) and n[0] < 2):
                        dve.wait_ge(scan_step, n[0] - 1)
                for h in range(2):
                    wait()
                    go(tt(scn[:, h, :, 0:ns], abar[:, h].unsqueeze(2).broadcast_to([P, 2, ns, 2, 16]),
                          prev[:, :, h].unsqueeze(1).broadcast_to([P, 2, ns, 2, 16]), ALU.mult))
                for h in range(2):
                    wait()
                    go(tt(scn[:, h, 0, 0:ns], scn[:, h, 0, 0:ns], scn[:, h, 1, 0:ns, ::-1, :], ALU.add))
                for h in range(2):
                    wait()
                    go(tt(dst[:, :, h], scn[:, h, 0, 0:ns], dst[:, :, h], ALU.add))

            def carry_on(n, j, carry, end):
                ts(fc[:, n, :, 0, :], carry[:, :, 1, :], -1.0, None, ALU.mult)
                step(ve.tensor_copy(fc[:, n, :, 1, :], carry[:, :, 0, :]))
                if end is not None:
                    for i, (tab, src) in enumerate(((a8re, carry), (a8im, fc[:, n]))):
                        pow_ = tab[:, j, :].rearrange("p (h g) -> p h g", h=2).unsqueeze(2).broadcast_to([P, 2, 2, 16])
                        step(tt(fe[:, i], pow_, src, ALU.mult))
                    step(tt(fe[:, 0], fe[:, 0], fe[:, 1], ALU.add))
                    step(tt(end, end, fe[:, 0], ALU.add))

            for i in range(3):
                dve.wait_ge(u_st[i], 16)
            dve.wait_ge(pj_ev, 20)
            v = vp[:, 1, :].rearrange("p (r c) -> p r c", c=GW)
            sums, scaled = bxd.rearrange("p (r c) -> p r c", c=GW), vp[:, 0, :].rearrange("p (r c) -> p r c", c=GW)
            ve.tensor_copy(sums[:, 0:1, :], v[:, 0:1, :])
            step(tt(sums[:, 1:, :], v[:, 1:, :], v[:, 0:GR - 1, :], ALU.add))
            step(tt(scaled, sums, inv_r[:, 0, :].unsqueeze(2).broadcast_to([P, GR, GW]), ALU.mult))
            ve.tensor_copy(sums[:, :, 0:1], scaled[:, :, 0:1])
            step(tt(sums[:, :, 1:], scaled[:, :, 1:], scaled[:, :, 0:GW - 1], ALU.add))
            step(tt(sums, sums, inv_c[:, 0, :].unsqueeze(1).broadcast_to([P, GR, GW]), ALU.mult))
            tt(vp[:, 0, :].rearrange("p (s k) -> p k s", s=T), bxd.rearrange("p (k s) -> p k s", s=T),
               vp[:, 1, :].rearrange("p (k s) -> p k s", s=T), ALU.subtract).then_inc(box0_ok, 1)
            dve.wait_ge(sc_ev, 4)
            cseg = Sc.rearrange("p (s j) h a g -> p s j h a g", s=NS)
            for j in range(1, SC):
                scan_chunk(cseg[:, :, j], cseg[:, :, j - 1], NS, 6 * (j - 1))
            at0 = 6 * (SC - 1)
            dve.wait_ge(scan_step, at0)
            dve.wait_ge(a8_ld, 32)
            for n in range(1, NS):
                carry_on(n - 1, SC - 1, cseg[:, n - 1, SC - 1], cseg[:, n, SC - 1])
            dve.wait_ge(sl_ev, 16)
            seg = S.rearrange("p (s j) h a g -> p s j h a g", s=NS)
            scan_chunk(S[:, 0:1], Sc[:, KC - 1:KC], 1, at0)
            for j in range(1, SCAN_STEPS):
                scan_chunk(seg[:, :, j], seg[:, :, j - 1], NS, at0 + 6 * j)
            with dve.Fori(1, SL // SCAN_STEPS) as i:
                for n in range(SCAN_STEPS):
                    j = i * SCAN_STEPS + n
                    scan_chunk(seg[:, :, bass.ds(j, 1)].squeeze(2), seg[:, :, bass.ds(j - 1, 1)].squeeze(2), NS, j * 6 + at0)
            dve.wait_ge(scan_step, SCAN_END)
            dve.wait_ge(hk_a, 2)
            for n in range(1, NS):
                carry_on(n - 1, SL - 1, seg[:, n - 1, SL - 1], seg[:, n, SL - 1] if n < NS - 1 else None)
            fixed = [0]

            def fix(ins):
                fixed[0] += 1
                ins.then_inc(fix_step, 1)

            def fix_wait(back=1):
                if fixed[0] > back:
                    dve.wait_ge(fix_step, fixed[0] - back)

            def fix_state(u):
                h, n, j0, j1 = FIXES[u]
                st = seg[:, n, j0:j1, h]
                return tt(st, st, fm[:, u % 2, 0, 0:j1 - j0], ALU.add)
            for u, (h, n, j0, j1) in enumerate(FIXES):
                nj = j1 - j0
                for i, (tab, src) in enumerate(((a8re, seg[:, n - 1, SL - 1, h]), (a8im, fc[:, n - 1, h]))):
                    fix_wait()
                    fix(tt(fm[:, u % 2, i, 0:nj], tab[:, j0:j1, 16 * h:16 * h + 16].unsqueeze(2).broadcast_to([P, nj, 2, 16]),
                           src.unsqueeze(1).broadcast_to([P, nj, 2, 16]), ALU.mult))
                if u:
                    fix_wait()
                    fix(fix_state(u - 1))
                    fix_wait()
                else:
                    fix_wait(0)
                fix(tt(fm[:, u % 2, 0, 0:nj], fm[:, u % 2, 0, 0:nj], fm[:, u % 2, 1, 0:nj], ALU.add))
            fix_wait(0)
            fix(fix_state(len(FIXES) - 1))
            dve.wait_ge(y_t, 8)
            dve.wait_ge(ad_ev, AD_GATE_MIX)
            for tb in range(2):
                for j in range(8):
                    n = tb * 8 + j
                    if n >= 2:
                        dve.wait_ge(mhi_ok, n - 1)
                        dve.wait_ge(mlo_ok, n - 1)
                    if j < 4:
                        dve.wait_ge(pm_t, tb * 4 + j + 1)
                        ts(m32[:, n % 2, :], ps[:, j, :], vcol[:, 40 + j:41 + j], None, ALU.mult).then_inc(m32_ok, 1)
                    else:
                        dve.wait_ge(gs_ok, tb * 4 + j - 3)
                        tt(m32[:, n % 2, :], gs[:, n % 2, :], yg[:, j - 4, tb * TB:(tb + 1) * TB], ALU.mult).then_inc(m32_ok, 1)
                    dve.wait_ge(mhi_ok, n + 1)
                    tt(mix_tile(tb, j, 1), m32[:, n % 2, :], mix_tile(tb, j, 0).bitcast(F32), ALU.subtract).then_inc(mlo_ok, 1)
            d0 = MIX[0]["dn0"]
            lo_dn(d0)
            lo_dn(d0 + 1)
            for i in range(32):
                if i % 8 == 7:
                    mx, hh = MIX[i // 16], (i // 8) % 2
                    dve.wait_ge(dn_used, d0 + i + 1)
                    for t in range(4):
                        gated_tile(mx["ev0"] + hh * 4 + t, t, 0, hh, 4 * hh)
                        if t == 1 and i + 2 < 32:
                            lo_dn(d0 + i + 2)
                elif i + 2 < 32:
                    lo_dn(d0 + i + 2)
                elif i == 30:
                    lo_up(UP_F2)
                    lo_up(UP_F2 + 1)
                if i == 20:
                    normalise(PREPS[6])
                if i in (28, 29):
                    split_h(PREPS[6], 2 * (i - 28), 2 * (i - 27))
            split_h(PREPS[6], 4, 8)
            ffn(BLOCKS[3], PREPS[7], BLOCKS[4]["up0"])
            ffn(BLOCKS[4], None, None)
            final_scale(1)

        @block.tensor
        def _(pe):
            mm = nc.tensor.matmul
            tr = nc.tensor.transpose
            pe.wait_ge(const_ok, 1)
            pe.wait_ge(pool_step, 2)
            pe.wait_ge(vec_ld, 16 * 5)
            tr(ps[:, 0, 0:116], vecrow[:, :], ident[0:116, 0:116]).then_inc(vec_t, 1)
            pe.wait_ge(s5_ld, 16 * S5_LOADS)
            for i in range(2):
                for j in range(4):
                    ins = tr(ps[:, 1 + i, j * P:(j + 1) * P], craw[:, i, j, :], ident[:, :])
                ins.then_inc(ct_t, 1)

            def modulation(q):
                m = q // 2
                pe.wait_ge(ada_ld[q % 2], 16 * (q // 2 + 1))
                if q >= 2:
                    pe.wait_ge(mod_ev, q - 1)
                if m == 2:
                    for cond in range(2):
                        o = ps[:, 4 + 2 * (q % 2) + cond, :]
                        for k in range(DK):
                            mm(o, scol[:, cond, k:k + 1].broadcast_to([P, P]), ada[:, q % 2, k, :], start=k == 0, stop=False)
                        for j in range(4):
                            bc = 44 + 4 * q + j
                            ins = mm(o[:, j * P:(j + 1) * P], vcol[:, bc:bc + 1].broadcast_to([P, P]), ident[:, :], start=False, stop=j == 3)
                else:
                    for j in range(4):
                        for k in range(DK):
                            ins = mm(ps[:, 4 + 2 * (q % 2), 2 * j:2 * j + 2], ada[:, q % 2, k, j * P:(j + 1) * P], scol[:, :, k],
                                     start=k == 0, stop=k == DK - 1)
                ins.then_inc(mod_t, 1)

            def ad_columns(n):
                m = 3 + n // 4
                pe.wait_ge(ad_acc, n + 1)
                if n >= 2:
                    pe.wait_ge(ad_ev, n - 1)
                for cond in range(2 if m < 5 else 1):
                    o = ps[:, 4 + 2 * (n % 2) + cond, :]
                    sums = [acc[:, n % 2, cond, :]] if m < 5 else [acc[:, n % 2, i, :] for i in range(2)]
                    if m % 3 == 2:
                        for i, a in enumerate(sums):
                            mm(o[:, 0:256], ones[:, :], a, start=i == 0, stop=False)
                        for j in range(2):
                            bc = 44 + 24 + 2 * n + j
                            ins = mm(o[:, j * P:(j + 1) * P], vcol[:, bc:bc + 1].broadcast_to([P, P]), ident[:, :], start=False, stop=j == 1)
                    else:
                        for j in range(2):
                            for i, a in enumerate(sums):
                                ins = mm(o[:, j:j + 1], a[:, j * P:(j + 1) * P], ones[:, 0:1], start=i == 0, stop=i == len(sums) - 1)
                ins.then_inc(ad_t, 1)

            pe.wait_ge(sil_ok, 1)
            modulation(0)
            modulation(1)
            pe.wait_ge(q4_ok, 1)
            for i in range(4):
                ins = tr(ps[:, 3, i * G:(i + 1) * G], sm[:, 9 + i, :], ident[0:G, 0:G])
            ins.then_inc(q4_t, 1)
            modulation(2)
            modulation(3)
            pe.wait_ge(xn_ok, 2)
            pe.wait_ge(ct_ev, 2)
            pe.wait_ge(q4_ev, 1)
            for k in range(DK):
                for t in range(2):
                    ins = tr(ps[:, k // 2, (2 * (k % 2) + t) * P:(2 * (k % 2) + t + 1) * P], xn0[:, t, k * P:(k + 1) * P], ident[:, :])
                ins.then_inc(ht_ok, 1)
            modulation(4)
            modulation(5)

            def v_transposes(gh):
                pe.wait_ge(vp_v_ok, 1)
                pe.wait_ge(vd_ok, 1)
                for i in range(8):
                    n = gh * 8 + i
                    if n >= 2:
                        pe.wait_ge(vt_ev, n - 1)
                    elif n == 0:
                        pe.wait_ge(h32_ok, 8)
                    for g2 in range(2):
                        for a in range(2):
                            ins = tr(ps[:, i % 2, (2 * g2 + a) * P:(2 * g2 + a + 1) * P],
                                     vn[:, a, 16 * gh + 2 * i + g2].rearrange("p s c -> p (s c)"), ident[:, :])
                    ins.then_inc(vt_t, 1)

            def responses(gh):
                pe.wait_ge(w_ok, 1)
                pe.wait_ge(bf_ok, 1)
                for i in range(16):
                    n, g = gh * 16 + i, gh * 16 + i
                    if n >= 2:
                        pe.wait_ge(kt_ev, n - 1)
                    o = ps[0:GC, 2 + i % 2, :]
                    w = [wn[:, a, g].rearrange("p t c -> p (t c)") for a in range(2)]
                    for a in range(2):
                        mm(o[:, 0:7 * GC], bk[:, a, g, :], w[a][:, GC:], start=a == 0, stop=a == 1)
                    for a in range(2):
                        mm(o[:, 7 * GC:8 * GC], bb[:, a, g, :], cn[:, a, g, :], start=a == 0, stop=a == 1)
                    for a in range(2):
                        ins = mm(o[:, 8 * GC:15 * GC], bf[:, a, g, :], w[a][:, 0:7 * GC], start=a == 0, stop=a == 1)
                    ins.then_inc(kt_t, 1)

            for gh in range(2):
                v_transposes(gh)
                responses(gh)

            def transposes(p, k0):
                if k0 == 0:
                    pe.wait_ge(xn_ok, p["q0"] + p["nt"])
                for k in range(k0, k0 + 4):
                    n = 8 * p["n"] + k
                    if n >= 4:
                        pe.wait_ge(h32_ok, n - 3)
                    for t in range(p["nt"]):
                        ins = tr(ps[:, k % 4, t * P:(t + 1) * P], xnt(p, t)[:, k * P:(k + 1) * P], ident[:, :])
                    ins.then_inc(ht_ok, 1)

            def three(o, l_hi, l_lo, r_hi, r_lo, start, stop):
                mm(o, l_hi, r_hi, start=start, stop=False)
                mm(o, l_hi, r_lo, start=False, stop=False)
                return mm(o, l_lo, r_hi, start=False, stop=stop)

            def up_unit(n, o, nk, prep=None, parts=(h_hi, h_lo)):
                hh_, hl_ = parts
                pe.wait_ge(up_lo_ok, n + 1)
                if prep is not None:
                    pe.wait_ge(h32_ok, 8 * prep["n"] + 5)
                for k in range(DK):
                    if prep is not None:
                        pe.wait_ge(hlo_ok, 8 * prep["n"] + k + 1)
                    ins = three(o, up_hi[:, n % 2, k], up_lo[:, n % 2, k], hh_[:, k, 0:nk], hl_[:, k, 0:nk], k == 0, k == DK - 1)
                ins.then_inc(up_used, 1)

            def ffn(b, prep, own):
                nt = 2 if b["ctx"] else 4
                nk = nt * P
                u, dd, F = b["up0"], b["dn0"], b["F0"]
                for r in range(NR):
                    if r == 0 and b["ev0"]:
                        pe.wait_ge(gated, b["ev0"] - b["prev_nt"])
                    if r == 1:
                        pe.wait_ge(gated, b["ev0"] + nt)
                    for f in range(FR):
                        n = F + f
                        bank = 4 * r + 2 * (f % 2)
                        if n >= 2:
                            pe.wait_ge(silu_ok, n - 1)
                        up_unit(u + 2 * f, ps[:, bank, 0:nk], nk, own if r == 0 and f == 0 else None)
                        if n >= 2:
                            pe.wait_ge(prod_ok, n - 1)
                        up_unit(u + 2 * f + 1, ps[:, bank + 1, 0:nk], nk)
                        if r == 0 and 1 <= f < len(b["ad"]) + 1:
                            if f == 1:
                                pe.wait_ge(gated, b["ev0"])
                            ad_columns(b["ad"][f - 1])
                    for hh in range(2):
                        bank = 4 * bank_set(r, hh)
                        e0 = b["ev0"] + (2 * r + hh) * nt
                        if hh == 0:
                            if e0 > 0:
                                pe.wait_ge(gated, e0)
                            if r == 0 and b["ad"]:
                                pe.wait_ge(ad_ev, b["ad"][-1] + 1)
                        else:
                            pe.wait_ge(prod_ok, F + FR)
                        for k in range(FR):
                            n = dd + hh * FR + k
                            pe.wait_ge(dn_lo_ok, n + 1)
                            pe.wait_ge(alo_ok, F + k + 1)
                            for t in range(nt):
                                ts_ = slice(t * P, (t + 1) * P)
                                ins = three(ps[:, bank + t, :], a_hi[:, k, ts_], a_lo[:, k, ts_],
                                            dn_hi[:, n % 2, :], dn_lo[:, n % 2, :], k == 0, k == FR - 1)
                            ins.then_inc(dn_used, 1)
                            if r == 1 and hh == 1 and prep is not None and k in (2, 7):
                                if k == 2:
                                    pe.wait_ge(gated, e0)
                                transposes(prep, 0 if k == 2 else 4)
                    u += 2 * FR
                    dd += 2 * FR
                    F += FR

            pe.wait_ge(kt_ev, 32)
            ffn(BLOCKS[0], PREPS[1], PREPS[0])
            ffn(BLOCKS[1], PREPS[2], PREPS[1])
            ffn(BLOCKS[2], PREPS[3], PREPS[2])
            done = 0
            for pi, pr in enumerate(PROJ):
                prep = PREPS[3 + pi]
                nk = prep["nt"] * P
                for j in range(len(pr["tiles"])):
                    if pi == 0 and j == 4:
                        pe.wait_ge(gated, MIX[0]["ev0"])
                    if pi:
                        pe.wait_ge(pj_ev, done - 3)
                    up_unit(pr["up0"] + j, ps[:, proj_bank(pi, j), 0:nk], nk, prep if j == 0 else None,
                            (h_part(prep, 0), h_part(prep, 1)))
                    done += 1
                    if (pi, j) == (0, 4):
                        pe.wait_ge(pj_ev, 4)
                        transposes(PREPS[4], 0)
                    if (pi, j) == (0, 6):
                        transposes(PREPS[4], 4)
                    if (pi, j) == (1, 0):
                        transposes(PREPS[5], 0)
                    if (pi, j) == (1, 2):
                        transposes(PREPS[5], 4)
            pe.wait_ge(vt_ld, 16)
            pe.wait_ge(uc_ld, 16 * T)
            for i in range(4):
                cc, gh = i // 2, i % 2
                for g in range(16):
                    ins = mm(ps[:, i, g * KC:(g + 1) * KC], vt[:, cc, 16 * gh + g, :], Uc[:, 16 * gh + g, :], start=True, stop=True)
                ins.then_inc(sc_t, 1)
            pe.wait_ge(pj_ev, 20)
            pe.wait_ge(u_ld, 16 * T)
            for i in range(16):
                if i >= 4:
                    pe.wait_ge(sl_ev, i - 3)
                cc, gq = i % 2, (i // 2) * 4
                for g in range(4):
                    ins = mm(ps[:, 4 + i % 4, g * KL:(g + 1) * KL], vt[:, cc, gq + g, :], U[:, gq + g, :], start=True, stop=True)
                ins.then_inc(sl_t, 1)
            pe.wait_ge(w_ld, 32)
            pe.wait_ge(m_ld, 16 * T)
            pe.wait_ge(sc_ev, 4)
            for i in range(8):
                if i % 4 == 0:
                    pe.wait_ge(hk_a, i // 4 + 3)
                if i >= 4:
                    pe.wait_ge(y_ev, i - 3)
                for g4 in range(4):
                    g = 4 * i + g4
                    o = ps[:, i % 4, g4 * P:(g4 + 1) * P]
                    mm(o, U[:, g, :], M[:, g, :], start=True, stop=False)
                    mm(o, Hk[:, 0, g, :], wy[0][:, g, :], start=False, stop=False)
                    ins = mm(o, Hk[:, 1, g, :], wy[1][:, g, :], start=False, stop=True)
                ins.then_inc(y_t, 1)
            pe.wait_ge(y_ev, 8)
            for i in range(8):
                cc, tb = i % 4, i // 4
                if i >= 4:
                    pe.wait_ge(yg_ok, i - 3)
                for t in range(4):
                    ins = tr(ps[:, 4 + i % 4, t * P:(t + 1) * P], y[:, tb * 4 + t, cc * P:(cc + 1) * P], ident[:, :])
                ins.then_inc(yt_t, 1)
            pe.wait_ge(pws_ld, 16)
            pe.wait_ge(box0_ok, 1)
            pe.wait_ge(pool_ok, 3)
            for tb in range(2):
                for j in range(4):
                    if tb:
                        pe.wait_ge(m32_ok, j + 1)
                    mm(ps[:, j, :], pws[:, j, :], vp[:, j, tb * TB:(tb + 1) * TB], start=True, stop=True).then_inc(pm_t, 1)
                if tb == 0:
                    pe.wait_ge(yg_ok, 8)
                    pe.wait_ge(glu_ld, 16)
                for j in range(4):
                    if tb:
                        pe.wait_ge(gs_ok, j + 1)
                    for k in range(4):
                        ins = mm(ps[:, 4 + j, :], wglu[:, k, j * P:(j + 1) * P], yg[:, k, tb * TB:(tb + 1) * TB],
                                 start=k == 0, stop=k == 3)
                    ins.then_inc(z_t, 1)
            for tb, mx in enumerate(MIX):
                for hh in range(2):
                    if tb == 0:
                        pe.wait_ge(m32_ok, 12) if hh == 0 else pe.wait_ge(gs_ok, 8)
                    else:
                        pe.wait_ge(gated, MIX[0]["ev0"] + 4 * (hh + 1))
                    for k in range(DK):
                        n = mx["dn0"] + hh * DK + k
                        pe.wait_ge(dn_lo_ok, n + 1)
                        pe.wait_ge(mlo_ok, tb * 8 + k + 1)
                        for t in range(4):
                            ts_ = slice(t * P, (t + 1) * P)
                            ins = three(ps[:, 4 * hh + t, :], mix_tile(tb, k, 0)[:, ts_], mix_tile(tb, k, 1)[:, ts_],
                                        dn_hi[:, n % 2, :], dn_lo[:, n % 2, :], k == 0, k == DK - 1)
                        ins.then_inc(dn_used, 1)
                        if tb == 1 and hh == 1 and k in (3, 6):
                            if k == 3:
                                pe.wait_ge(gated, mx["ev0"] + 4)
                            transposes(PREPS[6], 0 if k == 3 else 4)
            ffn(BLOCKS[3], PREPS[7], PREPS[6])
            ffn(BLOCKS[4], None, PREPS[7])


_INS = ['x', 'c', 'ctx', 'c_ctx', 'norm_g', 'w_ada', 'b_ada', 'ffn_w1', 'ffn_w3', 'ffn_w2', 'w_in', 'pool_w',
        'pool_scale', 's5_a_re', 's5_a_im', 's5_log_dt', 's5_b_re', 's5_b_im', 's5_c_re', 's5_c_im', 's5_d',
        's5_w_glu', 'w_out', 'final_g']


def kernel(**inputs):
    import numpy as _np
    import concourse.bacc as _bacc
    from concourse import mybir as _mybir
    from concourse.bass_utils import run_bass_kernel_spmd as _run

    nc = _bacc.Bacc("TRN2", target_bir_lowering=False, num_devices=1)
    arrays, args = {}, []
    for name in _INS:
        a = _np.ascontiguousarray(inputs[name])
        arrays[f"in_{name}_dram"] = a
        args.append(nc.dram_tensor(f"in_{name}_dram", a.shape, _mybir.dt.from_np(a.dtype), kind="ExternalInput").ap())
    args.append(nc.dram_tensor("out_0_dram", (1, SEQ, D), _mybir.dt.float32, kind="ExternalOutput").ap())
    hybrid_layer(nc, *args)
    r = _run(nc, [arrays], core_ids=[0])
    return r.results[0]["out_0_dram"]
```
